# Optimizing a Trainium2 kernel written in Bass

```python
import jax, jax.numpy as jnp
from jax import lax
import numpy as np

D_MODEL = 1024
BATCH = 1
SEQ = 1024
DEPTH = 1

GRID_W = 64
CTX_LEN = 256
N_MOD = 6
D_MIX = D_MODEL
D_REC = D_MIX // 2
REC_HEADS = 8
REC_HEAD_DIM = D_REC // REC_HEADS
CONV_W = 4
LRU_C = 8.0
D_POOL = D_MIX // 4
POOL_WINDOWS = (2, 4, 8, 16)
POOL_GROUP = D_POOL // len(POOL_WINDOWS)
D_FOUR = D_MIX - D_REC - D_POOL
FOUR_HEADS = 4
FOUR_HEAD_DIM = D_FOUR // FOUR_HEADS
D_IN = 2 * D_REC + D_POOL + D_FOUR
N_GROUPS = 4
EXPERTS_PER_GROUP = 4
N_EXPERTS = N_GROUPS * EXPERTS_PER_GROUP
TOP_K_EXPERT = 2
D_EXPERT = 512
EPS = 1e-6

kernel_name = 'hybrid_rglru_pool_fourier_hmoe_dit'

def rms_norm(x, g):
    x32 = x.astype(jnp.float32)
    y = x32 * lax.rsqrt(jnp.mean(x32 * x32, axis=-1, keepdims=True) + EPS)
    return (y * g.astype(jnp.float32)).astype(x.dtype)

def modulate(h, shift, scale):
    return h * (1.0 + scale) + shift

def _linear_combine(e1, e2):
    a1, b1 = e1
    a2, b2 = e2
    return a1 * a2, a2 * b1 + b2

def conv_centred(u, w, b):
    n = u.shape[1]
    left = CONV_W // 2
    right = CONV_W - 1 - left
    up = jnp.pad(u, ((0, 0), (left, right), (0, 0)))
    w32 = w.astype(jnp.float32)
    y = b.astype(jnp.float32)
    for k in range(CONV_W):
        y = y + w32[k] * up[:, k:k + n, :]
    return y

def rglru_direction(u, wa, ba, wx, bx, lam, h0, reverse):
    B, N, C = u.shape
    uh = u.reshape(B, N, REC_HEADS, REC_HEAD_DIM)
    r = jax.nn.sigmoid(jnp.einsum('bnhi,hij->bnhj', uh, wa.astype(jnp.float32)).reshape(B, N, C) + ba.astype(jnp.float32))
    ig = jax.nn.sigmoid(jnp.einsum('bnhi,hij->bnhj', uh, wx.astype(jnp.float32)).reshape(B, N, C) + bx.astype(jnp.float32))
    log_a = -LRU_C * r * jax.nn.softplus(-lam.astype(jnp.float32))
    a = jnp.exp(log_a)
    b = jnp.sqrt(-jnp.expm1(2.0 * log_a)) * (ig * u)
    a_cum, b_cum = lax.associative_scan(_linear_combine, (a, b), axis=1, reverse=reverse)
    return b_cum + a_cum * h0[:, None, :]

def recurrent_branch(z_x, conv_w, conv_b, wa, ba, wx, bx, lam, h0f, h0b):
    u = conv_centred(z_x.astype(jnp.float32), conv_w, conv_b)
    hf = rglru_direction(u, wa[0], ba[0], wx[0], bx[0], lam[0], h0f, False)
    hb = rglru_direction(u, wa[1], ba[1], wx[1], bx[1], lam[1], h0b, True)
    return hf, hb

def box_mean(x, w, axis):
    n = x.shape[axis]
    pads = [(0, 0)] * x.ndim
    pads[axis] = (1, 0)
    cs = jnp.cumsum(jnp.pad(x, pads), axis=axis)
    t = jnp.arange(n)
    lo = jnp.clip(t - w // 2, 0, n)
    hi = jnp.clip(t + (w - w // 2), 0, n)
    total = jnp.take(cs, hi, axis=axis) - jnp.take(cs, lo, axis=axis)
    cnt = (hi - lo).astype(x.dtype).reshape((n,) + (1,) * (x.ndim - axis - 1))
    return total / cnt

def pool_branch(z_p, pool_w, pool_scale, rows):
    B, N, _ = z_p.shape
    u = z_p.astype(jnp.float32).reshape(B, N, len(POOL_WINDOWS), POOL_GROUP)
    pooled = []
    for g, w in enumerate(POOL_WINDOWS):
        ug = u[:, :, g, :]
        if rows is None:
            pg = box_mean(ug, w, axis=1)
        else:
            grid = ug.reshape(B, rows, GRID_W, POOL_GROUP)
            pg = box_mean(box_mean(grid, w, axis=1), w, axis=2).reshape(B, N, POOL_GROUP)
        pooled.append(pg)
    d = jnp.stack(pooled, axis=2) - u
    y = jnp.einsum('bngi,gij->bngj', d, pool_w.astype(jnp.float32)).reshape(B, N, D_POOL)
    return (y * pool_scale.astype(jnp.float32)).astype(z_p.dtype)

def fourier_branch(z_f, fourier_w):
    B, N, _ = z_f.shape
    uh = z_f.astype(jnp.float32).reshape(B, N, FOUR_HEADS, FOUR_HEAD_DIM)
    f = jnp.fft.fft2(uh, axes=(1, 3), norm='ortho').real
    y = jnp.einsum('bnhi,hij->bnhj', f, fourier_w.astype(jnp.float32)).reshape(B, N, D_FOUR)
    return y.astype(z_f.dtype)

def token_mixer(h, w_in, w_out, conv_w, conv_b, wa, ba, wx, bx, lam, pool_w, pool_scale, fourier_w, h0f, h0b, rows):
    z = h @ w_in
    z_x = z[..., :D_REC]
    z_g = z[..., D_REC:2 * D_REC]
    z_p = z[..., 2 * D_REC:2 * D_REC + D_POOL]
    z_f = z[..., 2 * D_REC + D_POOL:]
    hf, hb = recurrent_branch(z_x, conv_w, conv_b, wa, ba, wx, bx, lam, h0f, h0b)
    y_a = ((hf + hb) * jax.nn.gelu(z_g.astype(jnp.float32))).astype(h.dtype)
    y_p = pool_branch(z_p, pool_w, pool_scale, rows)
    y_f = fourier_branch(z_f, fourier_w)
    y = jnp.concatenate([y_a, y_p, y_f], axis=-1) @ w_out
    return y, hf[:, -1, :], hb[:, 0, :]

def hier_moe(h, rg_w, rg_b, re_w, re_b, wg, wu, wd):
    lg = (h @ rg_w + rg_b).astype(jnp.float32)
    pg = jax.nn.softmax(lg, axis=-1)
    _, g_idx = lax.top_k(lg, 1)
    p_group = jnp.take_along_axis(pg, g_idx, axis=-1)
    le = (h @ re_w + re_b).astype(jnp.float32).reshape(h.shape[:-1] + (N_GROUPS, EXPERTS_PER_GROUP))
    g_mask = jax.nn.one_hot(g_idx[..., 0], N_GROUPS, dtype=jnp.float32)
    le_sel = jnp.sum(le * g_mask[..., None], axis=-2)
    e_top, e_idx = lax.top_k(le_sel, TOP_K_EXPERT)
    w_e = jax.nn.softmax(e_top, axis=-1) * p_group
    ids = g_idx * EXPERTS_PER_GROUP + e_idx
    gates = jnp.sum(jax.nn.one_hot(ids, N_EXPERTS, dtype=jnp.float32) * w_e[..., None], axis=-2).astype(h.dtype)
    y = jnp.zeros_like(h)
    for e in range(N_EXPERTS):
        hid = jax.nn.silu(h @ wg[e]) * (h @ wu[e])
        y = y + gates[..., e:e + 1] * (hid @ wd[e])
    return y

def setup_inputs(seed: int = 0) -> dict:
    key = jax.random.key(seed)
    ks = jax.random.split(key, 32)
    f32 = jnp.float32

    def nrm(k, shape, scale):
        return jax.random.normal(k, shape, f32) * scale

    a0 = jax.random.uniform(ks[13], (DEPTH, 2, D_REC), f32, 0.9, 0.999)
    sig_l = a0 ** (1.0 / LRU_C)
    rec_lambda = jnp.log(sig_l) - jnp.log1p(-sig_l)
    return {
        'x': nrm(ks[0], (BATCH, SEQ, D_MODEL), 1.0),
        'c': nrm(ks[1], (BATCH, D_MODEL), 1.0),
        'ctx': nrm(ks[2], (BATCH, CTX_LEN, D_MODEL), 1.0),
        'c_ctx': nrm(ks[3], (D_MODEL,), 1.0),
        'mod_w': nrm(ks[4], (DEPTH, D_MODEL, N_MOD * D_MODEL), 0.5 * D_MODEL ** -0.5),
        'mod_b': nrm(ks[5], (DEPTH, N_MOD * D_MODEL), 0.02),
        'norm_mix_g': 1.0 + nrm(ks[6], (DEPTH, D_MODEL), 0.02),
        'norm_ffn_g': 1.0 + nrm(ks[7], (DEPTH, D_MODEL), 0.02),
        'w_in': nrm(ks[8], (DEPTH, D_MODEL, D_IN), D_MODEL ** -0.5),
        'conv_w': nrm(ks[9], (DEPTH, CONV_W, D_REC), CONV_W ** -0.5),
        'conv_b': nrm(ks[10], (DEPTH, D_REC), 0.02),
        'rec_gate_a_w': nrm(ks[11], (DEPTH, 2, REC_HEADS, REC_HEAD_DIM, REC_HEAD_DIM), REC_HEAD_DIM ** -0.5),
        'rec_gate_a_b': nrm(ks[12], (DEPTH, 2, D_REC), 0.02),
        'rec_gate_x_w': nrm(ks[14], (DEPTH, 2, REC_HEADS, REC_HEAD_DIM, REC_HEAD_DIM), REC_HEAD_DIM ** -0.5),
        'rec_gate_x_b': nrm(ks[15], (DEPTH, 2, D_REC), 0.02),
        'rec_lambda': rec_lambda,
        'pool_w': nrm(ks[16], (DEPTH, len(POOL_WINDOWS), POOL_GROUP, POOL_GROUP), POOL_GROUP ** -0.5),
        'pool_scale': 1.0 + nrm(ks[17], (DEPTH, D_POOL), 0.1),
        'fourier_w': nrm(ks[18], (DEPTH, FOUR_HEADS, FOUR_HEAD_DIM, FOUR_HEAD_DIM), FOUR_HEAD_DIM ** -0.5),
        'w_out': nrm(ks[19], (DEPTH, D_MIX, D_MODEL), D_MIX ** -0.5),
        'router_group_w': nrm(ks[20], (DEPTH, D_MODEL, N_GROUPS), D_MODEL ** -0.5),
        'router_group_b': nrm(ks[21], (DEPTH, N_GROUPS), 0.01),
        'router_expert_w': nrm(ks[22], (DEPTH, D_MODEL, N_EXPERTS), D_MODEL ** -0.5),
        'router_expert_b': nrm(ks[23], (DEPTH, N_EXPERTS), 0.01),
        'expert_w_gate': nrm(ks[24], (DEPTH, N_EXPERTS, D_MODEL, D_EXPERT), D_MODEL ** -0.5),
        'expert_w_up': nrm(ks[25], (DEPTH, N_EXPERTS, D_MODEL, D_EXPERT), D_MODEL ** -0.5),
        'expert_w_down': nrm(ks[26], (DEPTH, N_EXPERTS, D_EXPERT, D_MODEL), D_EXPERT ** -0.5),
        'final_norm_g': 1.0 + nrm(ks[27], (D_MODEL,), 0.02),
    }

def reference(x, c, ctx, c_ctx, mod_w, mod_b, norm_mix_g, norm_ffn_g, w_in, conv_w, conv_b,
              rec_gate_a_w, rec_gate_a_b, rec_gate_x_w, rec_gate_x_b, rec_lambda, pool_w, pool_scale,
              fourier_w, w_out, router_group_w, router_group_b, router_expert_w, router_expert_b,
              expert_w_gate, expert_w_up, expert_w_down, final_norm_g):
    B = x.shape[0]
    rows = x.shape[1] // GRID_W
    zeros_state = jnp.zeros((B, D_REC), jnp.float32)
    for l in range(DEPTH):
        last = l == DEPTH - 1
        mod_lat = (jax.nn.silu(c) @ mod_w[l] + mod_b[l]).reshape(B, N_MOD, D_MODEL)[:, :, None, :]
        mod_ctx = (jax.nn.silu(c_ctx) @ mod_w[l] + mod_b[l]).reshape(N_MOD, D_MODEL)
        rec_p = (conv_w[l], conv_b[l], rec_gate_a_w[l], rec_gate_a_b[l], rec_gate_x_w[l], rec_gate_x_b[l], rec_lambda[l])
        moe_p = (router_group_w[l], router_group_b[l], router_expert_w[l], router_expert_b[l],
                 expert_w_gate[l], expert_w_up[l], expert_w_down[l])

        hc = modulate(rms_norm(ctx, norm_mix_g[l]), mod_ctx[0], mod_ctx[1])
        if not last:
            mix_c, sf, sb = token_mixer(hc, w_in[l], w_out[l], *rec_p, pool_w[l], pool_scale[l], fourier_w[l],
                                        zeros_state, zeros_state, None)
            ctx = ctx + mod_ctx[2] * mix_c
        else:
            hf_c, hb_c = recurrent_branch(hc @ w_in[l][:, :D_REC], *rec_p, zeros_state, zeros_state)
            sf, sb = hf_c[:, -1, :], hb_c[:, 0, :]

        hx = modulate(rms_norm(x, norm_mix_g[l]), mod_lat[:, 1], mod_lat[:, 0] * 0.0 + mod_lat[:, 1]) if False else \
            modulate(rms_norm(x, norm_mix_g[l]), mod_lat[:, 0], mod_lat[:, 1])
        mix_x, _, _ = token_mixer(hx, w_in[l], w_out[l], *rec_p, pool_w[l], pool_scale[l], fourier_w[l], sf, sb, rows)
        x = x + mod_lat[:, 2] * mix_x

        x = x + mod_lat[:, 5] * hier_moe(modulate(rms_norm(x, norm_ffn_g[l]), mod_lat[:, 3], mod_lat[:, 4]), *moe_p)
        if not last:
            ctx = ctx + mod_ctx[5] * hier_moe(modulate(rms_norm(ctx, norm_ffn_g[l]), mod_ctx[3], mod_ctx[4]), *moe_p)
    return rms_norm(x, final_norm_g)


_drawn_inputs = setup_inputs


def setup_inputs(seed=0):
    import zlib

    import numpy as np

    out = dict(_drawn_inputs(seed))
    spreads = {}
    factors = {'norm_mix_g': 4.574,
     'norm_ffn_g': 6.061,
     'rec_gate_a_b': 8.0,
     'rec_gate_x_b': 8.0,
     'pool_scale': 3.94,
     'router_group_b': 8.0,
     'router_expert_b': 45.82,
     'final_norm_g': 9.885}
    for name, (base, spread) in spreads.items():
        noise = np.random.default_rng([zlib.crc32(name.encode()), seed]).standard_normal(out[name].shape)
        drawn = base * np.exp(spread * noise) if base else spread * noise
        out[name] = __import__('jax').numpy.asarray(drawn.astype(out[name].dtype))
    for name, factor in factors.items():
        out[name] = (out[name] * factor).astype(out[name].dtype)
    return out
```

```python
from contextlib import ExitStack

import numpy as np
import concourse.bass as bass
from concourse import mybir

F32 = mybir.dt.float32
F32R = mybir.dt.float32r
BF16 = mybir.dt.bfloat16
I32 = mybir.dt.int32
ALU = mybir.AluOpType
ACT = mybir.ActivationFunctionType
AX = mybir.AxisListType

P = 128
D = 1024
KD = D // P
SEQ = 1024
NT = SEQ // P
CTX = 256
NC_ = CTX // P
ROWS, COLS = 16, 64
D_REC, D_POOL, D_FOUR = 512, 256, 256
D_IN = 2 * D_REC + D_POOL + D_FOUR
NI = D_REC // P
TOT = CTX + SEQ
HALF = 512
GRID_PAD = 8
NE, NG, EPG = 16, 4, 4
DE = 512
KE = DE // P
EPS = 1e-6
GELU_C = float(np.sqrt(2.0 / np.pi))
MAXT = SEQ * 2 // P + NE
TAB = MAXT + 2

CO = {}
_at = 0
for _n, _w in (("ident", P), ("ones", P), ("tri", P), ("iota", P), ("cos64", P), ("sin64", P), ("icr", 2 * ROWS),
               ("icc", 2 * COLS), ("alt", 1), ("pidx", 1), ("slot0", TAB), ("tok0", NT), ("first4", 4),
               ("tcount", 7), ("sidx", TAB), ("dump", 1)):
    CO[_n] = (_at, _at + _w)
    _at += _w
NCONST = _at

PV = {}
_at = 0
for _n, _w in (("c", KD), ("cc", KD), ("gmix", KD), ("gffn", KD), ("modb", 6 * KD), ("convw", 4 * NI), ("convb", NI),
               ("ba", 2 * NI), ("bx", 2 * NI), ("lam", 2 * NI), ("psc", 2)):
    PV[_n] = (_at, _at + _w)
    _at += _w
NPV = _at


def constants():
    c = np.zeros((P, NCONST), np.float32)

    def put(name, value):
        c[:, CO[name][0]:CO[name][1]] = value

    put("ident", np.eye(P))
    put("ones", 1.0)
    put("tri", np.triu(np.ones((P, P)), 1))
    put("iota", np.arange(P)[None])
    h = np.arange(64)
    ang = 2 * np.pi * np.outer(h, h) / 64
    scale = 1.0 / np.sqrt(SEQ * 64)
    put("cos64", np.kron(np.eye(2), np.cos(ang) * scale))
    put("sin64", np.kron(np.eye(2), -np.sin(ang) * scale))
    for m in range(2):
        for half in range(2):
            w = (2, 4, 8, 16)[2 * m + half]
            for name, n in (("icr", ROWS), ("icc", COLS)):
                t = np.arange(n)
                cnt = np.clip(t + w // 2, 0, n) - np.clip(t - w // 2, 0, n)
                c[64 * half:64 * half + 64, CO[name][0] + m * n:CO[name][0] + (m + 1) * n] = 1.0 / cnt
    p = np.arange(P)[:, None]
    put("alt", 1.0 - 2.0 * (p % 2))
    put("pidx", p)
    put("slot0", P * np.arange(TAB)[None])
    put("tok0", P * np.arange(NT)[None])
    put("first4", np.array([[4, 3, 2, 1]]))
    put("tcount", P * np.arange(1, 8)[None])
    put("sidx", np.arange(TAB)[None])
    put("dump", SEQ + p)
    n = np.arange(SEQ)
    ang = 2 * np.pi * (np.outer(n, np.arange(HALF)) % SEQ) / SEQ
    dft = np.concatenate([np.cos(ang), np.sin(ang)], axis=1).astype(np.float32)
    return c, dft


def build(nc, x, c, ctx, c_ctx, mod_w, mod_b, norm_mix_g, norm_ffn_g, w_in, conv_w, conv_b, gate_a_w, gate_a_b,
          gate_x_w, gate_x_b, lam, pool_w, pool_scale, fourier_w, w_out, rg_w, rg_b, re_w, re_b, wg, wu, wd,
          final_g, consts, dft, out):
    xn_d = nc.dram_tensor("normed_rows", [SEQ, D], F32).ap()
    x1_d = nc.dram_tensor("mixed_rows", [SEQ, D], F32).ap()
    acc_d = nc.dram_tensor("expert_sums", [SEQ + P, D], F32).ap()

    es = ExitStack()
    with es:
        free_at = [0]
        base = (nc.sbuf_usable_end - nc.sbuf_bytes_remaining + 63) // 64 * 64
        end = nc.sbuf_usable_end

        def at(name, shape, dt, off):
            size = int(np.prod(shape[1:])) * (2 if dt == BF16 else 4)
            assert base + off + size <= end, (name, base + off + size - end)
            free_at[0] = max(free_at[0], off + size)
            return nc.alloc_sbuf_tensor_at(name, list(shape), dt, offset=base + off)

        cursor = [0]

        def keep(name, shape, dt=F32):
            off = cursor[0]
            size = int(np.prod(shape[1:])) * (2 if dt == BF16 else 4)
            cursor[0] += (size + 31) // 32 * 32
            return at(name, shape, dt, off)

        def sem(name):
            return es.enter_context(nc.semaphore(name))

        bank = [es.enter_context(nc.psum_tensor(f"bank{i}", [P, HALF], F32)) for i in range(8)]

        cst = keep("cst", [P, NCONST])
        pv = keep("pv", [P, NPV])
        g2 = keep("g2", [P, D])
        g5 = keep("g5", [P, D])
        sc_mix = keep("sc_mix", [P, KD, 2])
        sh_mix = keep("sh_mix", [P, KD, 2])
        sc_ffn = keep("sc_ffn", [P, KD])
        sh_ffn = keep("sh_ffn", [P, KD])
        silu_c = keep("silu_c", [P, 2, KD])
        rw = keep("rw", [P, KD, NG + NE])
        rb = keep("rb", [P, NG + NE])
        stat = keep("stat", [P, 64])
        LG = keep("LG", [P, NT, NG + NE])
        tri_b = keep("tri_b", [P, P], BF16)
        ones_b = keep("ones_b", [P, P], BF16)
        held = keep("held", [P, 1])
        PHASE = cursor[0]

        def K(name):
            return cst[:, CO[name][0]:CO[name][1]]

        ident, ones = K("ident"), K("ones")

        def V(name, i=None):
            a, b = PV[name]
            return pv[:, a:b] if i is None else pv[:, a + i:a + i + 1]

        o = PHASE
        hT = at("hT", [P, KD, SEQ], F32, o)
        wout_sb = at("wout_sb", [P, KD, D], F32, o); o += 32768
        yT = at("yT", [P, KD, SEQ], F32, o)
        xt = at("xt", [P, NT, D], F32, o); o += 32768
        hTc = at("hTc", [P, KD, CTX], F32, o); o += 8192
        wring = at("wring", [P, 3, KD, P], F32, o); o += 12288
        dring = at("dring", [P, 3, SEQ], F32, o - 12288)
        mring = at("mring", [P, 2, KD, 256], F32, o); o += 16384
        macc = at("macc", [P, D], F32, o); o += 4096
        rec0 = o
        RH = [at(f"RH{d}", [P, TOT], F32, o + 5120 * d) for d in range(2)]
        IH = [at(f"IH{d}", [P, TOT], F32, o + 10240 + 5120 * d) for d in range(2)]
        AA = [at(f"AA{d}", [P, TOT], F32, o + 20480 + 5120 * d) for d in range(2)]
        Q = at("Q", [P, TOT], F32, o + 30720); o += 35840
        U = [at(f"U{d}", [P, TOT], F32, o + 5120 * d) for d in range(2)]; o += 10240
        ZPL = TOT + 6
        zpad = at("zpad", [P, ZPL], F32, o)
        zf1 = at("zf1", [P, SEQ], F32, o); o += 5152
        gz = [at(f"gz{d}", [P, SEQ], F32, o + 4096 * d) for d in range(2)]
        gt = at("gt", [P, SEQ], F32, o + 8192); o += 12288
        P0 = at("P0", [P, 2 * ROWS, COLS], F32, o)
        P1 = at("P1", [P, 2 * ROWS, COLS], F32, o + 8192)
        C0 = at("C0", [P, ROWS, COLS + 16], F32, o)
        C1 = at("C1", [P, ROWS, COLS + 16], F32, o + 8192)
        Vf = at("Vf", [P, NT, 2, 256], F32, o)
        ctxt = at("ctxt", [P, NC_, D], F32, o); o += 16384
        prow = at("prow", [P, P], F32, o - 4096)
        zf0 = at("zf0", [P, SEQ], F32, rec0 - 4096)
        bdg = at("bdg", [P, 4, NI, P], F32, o); o += 8192
        wfb = at("wfb", [P, 2, P], F32, o); o += 1024
        csw = at("csw", [P, 2, 256], F32, PHASE + 32768 + 6 * 4096)
        wpb = at("wpb", [P, 2, P], F32, o); o += 1024
        lamw = at("lamw", [P, 6, 2 * NI], F32, o); o += 192
        hb_ = at("hb_", [P, 4, NI], F32, o); o += 64
        NX = 3
        xr = [at(f"xr{n}", [P, D], F32, rec0 + 4096 * n) for n in range(NX)]
        xm = [at(f"xm{n}", [P, D], F32, rec0 + 12288 + 4096 * n) for n in range(2)]
        xs = [at(f"xs{n}", [P, D], F32, rec0 + 20480 + 4096 * n) for n in range(2)]
        h2 = at("h2", [P, KD, P], F32, rec0 + 28672)

        o = PHASE
        WP = at("WP", [P, KE, 2, 3 * D], F32R, o); o += KE * 2 * 3 * D * 4
        raw = at("raw", [P, KE, 3 * D], F32, o); o += KE * 3 * D * 4
        xg = at("xg", [P, D], F32, o); o += 4096
        xt_f = at("xt_f", [P, HALF], F32, o); o += 2048
        xp = at("xp", [P, 2, 2, KD, P], F32R, o); o += 16384
        sg = at("sg", [P, 2, P], F32, o); o += 1024
        hf = at("hf", [P, 2, P], F32, o); o += 1024
        hp = at("hp", [P, KE, 2, P], F32R, o); o += 4096
        ysc = at("ysc", [P, D], F32, o); o += 4096
        oh = at("oh", [P, NT, P], BF16, o); o += 2048
        RK = at("RK", [P, NE, NT], F32, o); o += 512
        rkt = at("rkt", [P, NT], F32, o); o += 32
        RV = at("RV", [P, NE, NT, 6], BF16, o); o += 1536
        idf = at("idf", [P, 8], F32, o); o += 32
        idg = at("idg", [P, 1], I32, o); o += 32
        ids = at("ids", [P, 2, 1], I32, o); o += 32
        gcol = at("gcol", [P, 2, 1], F32, o); o += 32
        tab = at("tab", [1, 4, TAB], I32, o); o += 640
        rs = at("rs", [P, 1800], F32, o)
        R_ = {}
        ra = 0
        for n_, sh_ in (("m", ()), ("goh", (4,)), ("key", (4,)), ("km", ()), ("d", (4,)), ("les", (4,)), ("m1", ()),
                        ("oh1", (4,)), ("m2", ()), ("oh2", (4,)), ("ex", ()), ("pg", ()), ("w1", ()), ("w2", ()),
                        ("big", (4, 4)), ("M1", (4, 4)), ("M2", (4, 4)), ("G", (4, 4)), ("rem", (NE, NT))):
            size = NT * int(np.prod(sh_)) if n_ != "rem" else NE * NT
            v_ = rs[:, ra:ra + size]
            if n_ == "rem":
                v_ = v_.rearrange("p (e t) -> p e t", t=NT)
            elif len(sh_) == 1:
                v_ = v_.rearrange("p (t a) -> p t a", a=4)
            elif len(sh_) == 2:
                v_ = v_.rearrange("p (t a b) -> p t a b", a=4, b=4)
            R_[n_] = v_
            ra += size
        NF = 2
        fa = [at(f"fa{n}", [P, D], F32, PHASE + 4096 * n) for n in range(NF)]
        fx = [at(f"fx{n}", [P, D], F32, PHASE + 8192 + 4096 * n) for n in range(NF)]
        fo = [at(f"fo{n}", [P, D], F32, PHASE + 16384 + 4096 * n) for n in range(NF)]
        gfin = at("gfin", [P, D], F32, PHASE + 24576)
        fj = at("fj", [P, D], F32, PHASE + 28672)

        s_cst, s_prow, s_x, s_rw = sem("consts_in"), sem("param_rows_in"), sem("x_in"), sem("router_in")
        s_bd, s_gb2, s_gb5, s_gf = sem("blockdiag_in"), sem("mix_gate_bias_in"), sem("ffn_gate_bias_in"), sem("final_gain_in")
        s_bd0 = sem("blockdiag_zeroed")
        s_mod = [sem(f"modw_in{n}") for n in range(2)]
        s_modu, s_modv = sem("modw_used_by_pe"), sem("modw_used_by_dve")
        s_win = [sem(f"win_in{n}") for n in range(3)]
        s_dft = [sem(f"dft_in{n}") for n in range(3)]
        s_dftu = sem("dft_used")
        s_wout = sem("wout_in")
        s_zero, s_zero_d = sem("zero_row"), sem("sums_zeroed")
        s_pvp, s_pv = sem("params_transposed"), sem("params_ready")
        s_sil, s_silu = sem("silu_tanh"), sem("silu_ready")
        s_ss, s_ms, s_sq, s_rstd, s_xs = (sem("x_square_sums"), sem("x_mean_squares"), sem("x_root"), sem("x_rstd"),
                                          sem("x_scaled"))
        s_m01, s_scsh = sem("mod01_summed"), sem("mix_scale_shift")
        s_tpe = sem("x_transposed")
        s_z, s_zu = sem("z_ready"), sem("z_taken")
        s_u, s_conv = sem("u_started"), sem("u_ready")
        s_g, s_gu = sem("gates_ready"), sem("gates_taken")
        s_ra, s_rm, s_rr, s_y = sem("decay_ready"), sem("input_scaled"), sem("root_ready"), sem("recurrent_done")
        s_gsq, s_gp, s_gth, s_gel = sem("gelu_square"), sem("gelu_poly"), sem("gelu_tanh"), sem("gelu_ready")
        s_pd, s_pm, s_py = (sem("pool_diff"), sem("pool_product"),
                                        sem("pool_ready"))
        s_fz, s_csw, s_cswc = sem("fourier_z"), sem("csw_product"), sem("csw_ready")
        s_v, s_vc = sem("v_product"), sem("v_ready")
        s_f, s_fc, s_fy = sem("dft_done"), sem("dft_copied"), sem("fourier_ready")
        s_lam, s_lame, s_lamc = sem("lam_abs"), sem("lam_exp"), sem("lam_ready")
        s_macc, s_m25, s_mrow, s_maccu = sem("mod_summed"), sem("mod_product"), sem("mod_ready"), sem("mod_acc_used")
        s_ydone = sem("mixed_inputs_done")
        s_mix, s_mixu = sem("mix_ready"), sem("mix_taken")
        s_xr = [sem(f"x_again{n}") for n in range(NX)]
        s_x1, s_x1d = sem("x1_ready"), [sem(f"x1_stored{n}") for n in range(NX)]
        s_ss2, s_ms2, s_rt2, s_xn = sem("x1_square_sum"), sem("x1_mean_square"), sem("x1_root"), sem("xn_ready")
        s_xnd = [sem(f"xn_stored{n}") for n in range(2)]
        s_t2, s_h2, s_lgp, s_lg = sem("xn_transposed"), sem("h2_ready"), sem("logits_summed"), sem("logits_ready")
        s_e1, s_e2 = sem("router_exponents"), sem("router_exps")
        s_mk, s_rk, s_tab = sem("masks_ready"), sem("ranks_summed"), sem("tables_ready")
        s_dv, s_ac, s_pc = sem("vector_chain"), sem("scalar_chain"), sem("pool_engine_chain")
        s_raw = [sem(f"raw_in{j}") for j in range(KE)]
        s_hi = sem("weight_hi")
        s_logu, s_lod = [sem(f"gate_up_split{j}") for j in range(KE)], [sem(f"down_split{j}") for j in range(KE)]
        s_gud, s_dd = sem("gate_up_done"), sem("down_done")
        s_sg, s_hid, s_hfr, s_hps = sem("silu_done"), sem("hidden_product"), sem("hidden_hi"), sem("hidden_ready")
        s_oh, s_idx, s_idf, s_ids = sem("onehot_ready"), sem("slots_summed"), sem("slot_fields"), sem("slot_ids_ready")
        s_xg, s_xgt, s_xgf, s_xgh, s_xgr = (sem("rows_gathered"), sem("rows_transposed"), sem("rows_modulated"),
                                            sem("rows_hi"), sem("rows_ready"))
        s_ye, s_ys = sem("y_scaled"), sem("y_scattered")
        s_held = sem("pool_held")
        s_end = sem("experts_finished")
        s_zp, s_tri = sem("conv_pads_zeroed"), sem("bf16_constants")
        s_tpa, s_tpv = sem("h_ready_scalar"), sem("h_ready_vector")
        s_hgu, s_hdn = sem("gate_up_hi"), sem("down_hi")
        s_pch = sem("prepare_chain")
        s_fl, s_fx1, s_fs, s_fm, s_fr, s_fo = ([sem(f"sums_in{n}") for n in range(NF)], sem("final_sum"),
                                               sem("final_square"), sem("final_mean"), sem("final_root"),
                                               sem("final_row"))
        s_out = [sem(f"out_stored{n}") for n in range(NF)]

        COLT = [("x", 0), ("g", 0), ("p", 0), ("x", 1), ("g", 1), ("p", 1), ("x", 2), ("g", 2), ("x", 3), ("g", 3),
                ("f", 0), ("f", 1)]
        OFF = {"x": 0, "g": D_REC, "p": 2 * D_REC, "f": 2 * D_REC + D_POOL}
        GATES_AFTER = {("p", 0): 0, ("p", 1): 1, ("g", 2): 2, ("g", 3): 3}
        UNITS = [(ct, part) for ct in COLT for part in ((("c",) if ct[0] == "x" else ()) + (0, 1))]
        UNIT = {u: n for n, u in enumerate(UNITS)}
        GPARTS = [(CTX, HALF), (CTX + HALF, HALF), (0, CTX)]
        GUNITS = [(i, d, g, q) for i in range(NI) for d in range(2) for g in range(2) for q in range(3)]
        NMC = 6 * D // 256
        MCH = D // 256

        block = es.enter_context(nc.Block())

        @block.sync
        def _(sp):
            sp.dma_start(cst[:], consts).then_inc(s_cst, 16)
            rows = lambda a: a.rearrange("(r q) -> r q", q=P)
            prows = [("c", rows(c[0])), ("cc", rows(c_ctx)), ("gmix", rows(norm_mix_g[0])),
                     ("gffn", rows(norm_ffn_g[0])), ("modb", rows(mod_b[0])),
                     ("convw", conv_w[0].rearrange("k (i q) -> (k i) q", q=P)), ("convb", rows(conv_b[0])),
                     ("ba", gate_a_b[0].rearrange("d (i q) -> (d i) q", q=P)),
                     ("bx", gate_x_b[0].rearrange("d (i q) -> (d i) q", q=P)),
                     ("lam", lam[0].rearrange("d (i q) -> (d i) q", q=P)), ("psc", rows(pool_scale[0]))]
            for name, src in prows:
                sp.dma_start(prow[PV[name][0]:PV[name][1], :], src).then_inc(s_prow, 16)
            xv = x[0].rearrange("(t p) d -> p t d", p=P)
            cv = ctx[0].rearrange("(t p) d -> p t d", p=P)
            mv = mod_w[0].rearrange("(k p) n -> p k n", p=P)

            def load_mod(n):
                if 2 <= n < 2 * MCH + 2:
                    sp.wait_ge(s_modu, n - 1)
                if n >= 2 * MCH + 2:
                    sp.wait_ge(s_modv, n - 1 - 2 * MCH)
                sp.dma_start(mring[:, n % 2], mv[:, :, n * 256:(n + 1) * 256]).then_inc(s_mod[n % 2], 16)

            load_mod(0)
            load_mod(1)
            sp.dma_start(ctxt[:], cv).then_inc(s_x, 16)
            sp.dma_start(xt[:, 0:4], xv[:, 0:4]).then_inc(s_x, 16)
            sp.dma_start(xt[:, 4:8], xv[:, 4:8]).then_inc(s_x, 16)
            for n in range(2, 2 * MCH):
                load_mod(n)
            wv = w_in[0].rearrange("(k p) n -> p k n", p=P)

            def load_win(n):
                if n >= 3:
                    sp.wait_ge(s_z, UNIT[(COLT[n - 3], 1)] + 1)
                a = OFF[COLT[n][0]] + COLT[n][1] * P
                sp.dma_start(wring[:, n % 3], wv[:, :, a:a + P]).then_inc(s_win[n % 3], 16)

            for n in range(3):
                load_win(n)
            sp.wait_ge(s_bd0, 3)
            for d in range(2):
                for g, w in enumerate((gate_a_w, gate_x_w)):
                    for h in range(2):
                        sp.dma_start(bdg[64 * h:64 * h + 64, 2 * d + g, :, 64 * h:64 * h + 64],
                                     w[0, d].rearrange("(i h) a b -> h a i b", h=2)[h]).then_inc(s_bd, 16)
            for h in range(2):
                sp.dma_start(wfb[64 * h:64 * h + 64, :, 64 * h:64 * h + 64],
                             fourier_w[0].rearrange("(m h) a b -> h a m b", h=2)[h]).then_inc(s_bd, 16)
                sp.dma_start(wpb[64 * h:64 * h + 64, :, 64 * h:64 * h + 64],
                             pool_w[0].rearrange("(m h) a b -> h a m b", h=2)[h]).then_inc(s_bd, 16)
            sp.dma_start(rw[:, :, 0:NG], rg_w[0].rearrange("(k p) n -> p k n", p=P)).then_inc(s_rw, 16)
            sp.dma_start(rw[:, :, NG:], re_w[0].rearrange("(k p) n -> p k n", p=P)).then_inc(s_rw, 16)
            sp.dma_start(rb[:, 0:NG], rg_b.partition_broadcast(P).rearrange("p a n -> p (a n)")).then_inc(s_rw, 16)
            sp.dma_start(rb[:, NG:], re_b.partition_broadcast(P).rearrange("p a n -> p (a n)")).then_inc(s_rw, 16)
            sp.dma_start(g2[:], mod_b[0:1, 2 * D:3 * D].partition_broadcast(P).rearrange("p a n -> p (a n)"))\
                .then_inc(s_gb2, 16)
            sp.wait_ge(s_zero, 1)
            for r in range(0, SEQ, P):
                sp.dma_start(acc_d[r:r + P, :], g5[:]).then_inc(s_zero_d, 16)
            mod_next = 2 * MCH
            for n in range(3, len(COLT)):
                load_win(n)
                for _ in range(2):
                    if mod_next < NMC:
                        load_mod(mod_next)
                        mod_next += 1
            sp.wait_ge(s_zero_d, 16 * (SEQ // P))
            sp.wait_ge(s_ys, 16)
            sp.dma_start(g5[:], mod_b[0:1, 5 * D:6 * D].partition_broadcast(P).rearrange("p a n -> p (a n)"))\
                .then_inc(s_gb5, 16)
            sp.wait_ge(s_z, len(UNITS))
            for k in range(NT):
                if k >= 3:
                    sp.wait_ge(s_dftu, k - 2)
                sp.dma_start(dring[:, k % 3], dft[k * P:(k + 1) * P, :]).then_inc(s_dft[k % 3], 16)
            for half in range(2):
                sp.dma_start(wout_sb[:, 4 * half:4 * half + 4],
                             w_out[0].rearrange("(k p) n -> p k n", p=P)[:, 4 * half:4 * half + 4]).then_inc(s_wout, 16)
            sp.wait_ge(s_y, NI)
            for t in range(NX):
                sp.dma_start(xr[t][:], xv[:, t]).then_inc(s_xr[t], 16)
            x1v = x1_d.rearrange("(t p) d -> p t d", p=P)
            xnv = xn_d.rearrange("(t p) d -> p t d", p=P)
            for t in range(NT):
                sp.wait_ge(s_x1, t + 1)
                sp.dma_start(x1v[:, t], xr[t % NX][:]).then_inc(s_x1d[t % NX], 16)
                sp.wait_ge(s_xn, t + 1)
                sp.dma_start(xnv[:, t], xs[t % 2][:]).then_inc(s_xnd[t % 2], 16)
                if t + NX < NT:
                    sp.wait_ge(s_x1d[t % NX], 16 * (t // NX + 1))
                    sp.dma_start(xr[t % NX][:], xv[:, t + NX]).then_inc(s_xr[t % NX], 16)

            def chunk(e, j):
                g = wg[0, e].rearrange("a (k p) n -> p (a k) n", p=P) if not isinstance(e, int) else \
                    wg[0, e].rearrange("(k p) n -> p k n", p=P)
                u = wu[0, e].rearrange("a (k p) n -> p (a k) n", p=P) if not isinstance(e, int) else \
                    wu[0, e].rearrange("(k p) n -> p k n", p=P)
                dn = wd[0, e].rearrange("a h n -> (a h) n") if not isinstance(e, int) else wd[0, e]
                sp.dma_start(raw[:, j, 0:D].rearrange("p (k n) -> p k n", n=P),
                             g[:, :, j * P:(j + 1) * P]).then_inc(s_raw[j], 16)
                sp.dma_start(raw[:, j, D:2 * D].rearrange("p (k n) -> p k n", n=P),
                             u[:, :, j * P:(j + 1) * P]).then_inc(s_raw[j], 16)
                sp.dma_start(raw[:, j, 2 * D:], dn[j * P:(j + 1) * P, :]).then_inc(s_raw[j], 16)

            sp.wait_ge(s_lg, NT)
            for n in range(NX):
                sp.wait_ge(s_x1d[n], 16 * len(range(n, NT, NX)))
            for n in range(2):
                sp.wait_ge(s_xnd[n], 16 * (NT // 2))
            sp.wait_ge(s_mrow, 6)
            for j in range(KE):
                chunk(0, j)
            with sp.Fori(1, NE) as e:
                for j in range(KE):
                    sp.wait_ge(s_logu[j], e)
                    sp.wait_ge(s_lod[j], e)
                    chunk(bass.ds(e, 1), j)
            sp.wait_ge(s_end, 1)
            sp.dma_start(gfin[:], final_g.partition_broadcast(P)).then_inc(s_gf, 16)
            accv = acc_d[0:SEQ, :].rearrange("(t p) d -> p t d", p=P)
            ov = out[0].rearrange("(t p) d -> p t d", p=P)
            for t in range(NT):
                if t >= NF:
                    sp.wait_ge(s_fo, t - NF + 1)
                sp.dma_start(fa[t % NF][:], accv[:, t]).then_inc(s_fl[t % NF], 16)
                sp.dma_start(fx[t % NF][:], x1v[:, t]).then_inc(s_fl[t % NF], 16)
                if t >= 1:
                    sp.wait_ge(s_fo, t)
                    sp.dma_start(ov[:, t - 1], fo[(t - 1) % NF][:]).then_inc(s_out[(t - 1) % NF], 16)
            sp.wait_ge(s_fo, NT)
            sp.dma_start(ov[:, NT - 1], fo[(NT - 1) % NF][:]).then_inc(s_out[(NT - 1) % NF], 16)
            for n in range(NF):
                sp.wait_ge(s_out[n], 16 * (NT // NF))

        @block.gpsimd
        def _(pool):
            pool.memset(g5[:], 0.0).then_inc(s_zero, 1)
            pool.memset(held[:], 0.0).then_inc(s_held, 1)
            pool.memset(zpad[:], 0.0).then_inc(s_zp, 1)
            pool.memset(bdg[:], 0.0).then_inc(s_bd0, 1)
            pool.memset(wfb[:], 0.0).then_inc(s_bd0, 1)
            pool.memset(wpb[:], 0.0).then_inc(s_bd0, 1)
            pool.wait_ge(s_cst, 16)
            pool.tensor_copy(tri_b[:], K("tri")).then_inc(s_tri, 1)
            pool.tensor_copy(ones_b[:], ones).then_inc(s_tri, 1)
            pool.wait_ge(s_zero, 1)
            pool.dma_start(acc_d[SEQ:SEQ + P, :], g5[:]).then_inc(s_ys, 16)

            chain = [0]

            def link(ins):
                chain[0] += 1
                ins.then_inc(s_pc, 1)
                pool.wait_ge(s_pc, chain[0])

            def add(o_, a_, b_):
                return pool.tensor_tensor(o_, a_, b_, ALU.add)

            for m in range(2):
                z = yT[:, 4 + m, :].rearrange("p (r c) -> p r c", c=COLS)
                pool.wait_ge(s_zu, UNIT[(("p", m), 1)] + 1)
                if m == 1:
                    pool.wait_ge(s_pd, 1)
                if m == 0:
                    pool.wait_ge(s_tpe, 3 * KD)
                link(pool.memset(P0[:, 0:GRID_PAD, :], 0.0))
                link(pool.memset(P0[:, GRID_PAD + ROWS:, :], 0.0))
                link(pool.tensor_copy(P0[:, GRID_PAD:GRID_PAD + ROWS, :], z))
                link(add(P1[:, 0:31, :], P0[:, 0:31, :], P0[:, 1:32, :]))
                if m == 1:
                    link(add(P0[:, 0:29, :], P1[:, 0:29, :], P1[:, 2:31, :]))
                    link(add(P1[:, 0:25, :], P0[:, 0:25, :], P0[:, 4:29, :]))
                a, b, c_ = ((7, 6, 8), (4, 0, 8))[m]
                link(pool.memset(C0[:, :, 0:8], 0.0))
                link(pool.memset(C0[:, :, 8 + COLS:], 0.0))
                link(pool.tensor_copy(C0[0:64, :, 8:8 + COLS], P1[0:64, a:a + ROWS, :]))
                link(add(C0[64:128, :, 8:8 + COLS], P1[64:128, b:b + ROWS, :], P1[64:128, c_:c_ + ROWS, :]))
                link(add(C1[:, :, 0:79], C0[:, :, 0:79], C0[:, :, 1:80]))
                if m == 1:
                    link(add(C0[:, :, 0:77], C1[:, :, 0:77], C1[:, :, 2:79]))
                    link(add(C1[:, :, 0:73], C0[:, :, 0:73], C0[:, :, 4:77]))
                icr = K("icr")[:, m * ROWS:(m + 1) * ROWS].unsqueeze(2)
                icc = K("icc")[:, m * COLS:(m + 1) * COLS].unsqueeze(1)
                link(add(C0[64:128, :, 0:COLS], C1[64:128, :, b:b + COLS], C1[64:128, :, c_:c_ + COLS]))
                link(pool.tensor_tensor(C0[64:128, :, 0:COLS], C0[64:128, :, 0:COLS],
                                        icr[64:128].to_broadcast([64, ROWS, COLS]), ALU.mult))
                link(pool.tensor_tensor(C0[0:64, :, 0:COLS], C1[0:64, :, a:a + COLS],
                                        icr[0:64].to_broadcast([64, ROWS, COLS]), ALU.mult))
                link(pool.tensor_tensor(C0[:, :, 0:COLS], C0[:, :, 0:COLS], icc.to_broadcast([P, ROWS, COLS]),
                                        ALU.mult))
                pool.tensor_tensor(z, C0[:, :, 0:COLS], z, ALU.subtract).then_inc(s_pd, 1)

            def hold(n):
                pool.wait_ge(s_held, n + 1)
                pool.tensor_tensor(held[:], held[:], held[:], ALU.mult).then_inc(s_held, 1)

            def split_down(e1, j):
                pool.wait_ge(s_hdn, 4 * e1 + j + 1)
                pool.tensor_tensor(WP[:, j, 1, 2 * D:], raw[:, j, 2 * D:], WP[:, j, 0, 2 * D:].bitcast(F32),
                                   ALU.subtract).then_inc(s_lod[j], 1)

            def gather(q):
                pool.wait_ge(s_ids, q + 1)
                hold(2 * q - 1 if not isinstance(q, int) else 0)
                pool.indirect_dma_start(out=xg[:], out_offset=None, in_=xn_d,
                                        in_offset=bass.IndirectOffsetOnAxis(ap=idg[:, 0:1], axis=0)).then_inc(s_xg, 16)

            for n in range(2):
                pool.wait_ge(s_xnd[n], 16 * (NT // 2))
            pool.wait_ge(s_zero_d, 16 * (SEQ // P))
            gather(0)
            for j in range(KE):
                split_down(0, j)
            W = pool.value_load(tab[0:1, 3, 0:1], min_val=NE, max_val=MAXT)
            with pool.Fori(0, MAXT // 2) as it:
                with pool.If(2 * it < W):
                    for par in range(2):
                        s = 2 * it + par
                        L = pool.value_load(tab[0:1, 2, bass.ds(s, 1)], min_val=0, max_val=1)
                        E1 = pool.value_load(tab[0:1, 0, bass.ds(s + 1, 1)], min_val=0, max_val=NE - 1)
                        pool.wait_ge(s_xgt, 2 * s + 2)
                        gather(s + 1)
                        with pool.If(L > 0):
                            for j in range(KE):
                                split_down(E1, j)
                        pool.wait_ge(s_ye, 2 * s + 4)
                        pool.wait_ge(s_ys, 16 * s + 16)
                        hold(2 * s + 2)
                        pool.indirect_dma_start(out=acc_d, out_offset=bass.IndirectOffsetOnAxis(ap=ids[:, par, 0:1],
                                                                                                axis=0),
                                                in_=ysc[:], in_offset=None, compute_op=ALU.add).then_inc(s_ys, 16)
                        pool.wait_ge(s_xg, 16 * s + 32)
            Wl = pool.value_load(tab[0:1, 3, 1:2], min_val=NE, max_val=MAXT)
            pool.wait_ge(s_ys, 16 * Wl + 16)
            hold(2 * Wl + 1)
            pool.memset(stat[:, 63:64], 0.0).then_inc(s_end, 1)

        @block.tensor
        def _(pe):
            pe.wait_ge(s_cst, 16)
            pe.wait_ge(s_prow, 16 * len(PV))
            pe.transpose(bank[7][:, 0:NPV], prow[0:NPV, :], ident[0:NPV, 0:NPV]).then_inc(s_pvp, 1)

            pe.wait_ge(s_silu, 1)
            for n in range(2 * MCH):
                pe.wait_ge(s_mod[n % 2], 16 * (n // 2 + 1))
                for h in range(2):
                    for k in range(KD):
                        mm = pe.matmul(bank[6][:, 2 * (2 * n + h):2 * (2 * n + h) + 2],
                                       mring[:, n % 2, k, h * P:(h + 1) * P], silu_c[:, :, k],
                                       start=k == 0, stop=k == KD - 1)
                mm.then_inc(s_modu, 1)

            n = 0
            for part in ("c", 0, 1):
                for k in range(KD):
                    cnt = NC_ if part == "c" else 4
                    if k == 0:
                        pe.wait_ge(s_xs, {"c": 2, 0: 6, 1: 10}[part])
                    if n >= 4:
                        m_ = n - 4
                        pe.wait_ge(s_tpa if m_ % 2 == 0 else s_tpv, m_ // 2 + 1)
                    for t in range(cnt):
                        src = ctxt[:, t] if part == "c" else xt[:, 4 * part + t]
                        mm = pe.transpose(bank[n % 4][:, t * P:(t + 1) * P], src[:, k * P:(k + 1) * P], ident)
                    n += 1
                    mm.then_inc(s_tpe, 1)

            pe.wait_ge(s_bd, 16 * 12)
            pe.wait_ge(s_pv, 1)
            for m in range(2):
                for q, name in enumerate(("cos64", "sin64")):
                    mm = pe.matmul(bank[7][:, (2 * m + q) * P:(2 * m + q + 1) * P], K(name), wfb[:, m, :],
                                   start=True, stop=True)
            mm.then_inc(s_csw, 1)

            pe.wait_ge(s_tpa, 12)
            pe.wait_ge(s_tpv, 12)

            def z_tile(n):
                ct = COLT[n]
                pe.wait_ge(s_win[n % 3], 16 * (n // 3 + 1))
                for part in ((("c",) if ct[0] == "x" else ()) + (0, 1)):
                    u = UNIT[(ct, part)]
                    if u >= 4:
                        pe.wait_ge(s_zu, u - 3)
                    o_ = bank[u % 4][:, 0:CTX] if part == "c" else bank[u % 4][:]
                    for k in range(KD):
                        src = hTc[:, k, :] if part == "c" else hT[:, k, part * HALF:(part + 1) * HALF]
                        mm = pe.matmul(o_, wring[:, n % 3, k, :], src, start=k == 0, stop=k == KD - 1)
                    mm.then_inc(s_z, 1)
                    last = mm
                return last

            def gates(i):
                pe.wait_ge(s_conv, i + 1)
                for d in range(2):
                    for g in range(2):
                        for q, (a, w) in enumerate(GPARTS):
                            n = GUNITS.index((i, d, g, q))
                            if n >= 3:
                                pe.wait_ge(s_gu, n - 2)
                            pe.matmul(bank[4 + n % 3][:, 0:w], bdg[:, 2 * d + g, i, :], U[i % 2][:, a:a + w],
                                      start=True, stop=True).then_inc(s_g, 1)

            def mod_product(m):
                pe.wait_ge(s_macc, m - 1)
                k0 = {2: 0, 3: 2, 4: 3, 5: 4}[m]
                if m in (2, 5):
                    for h in range(2):
                        if k0 + h:
                            pe.wait_ge(s_mrow, k0 + h)
                        pe.matmul(bank[7][:], ones, macc[:, h * HALF:(h + 1) * HALF], start=True,
                                  stop=True).then_inc(s_m25, 1)
                else:
                    pe.wait_ge(s_mrow, k0)
                    for k in range(KD):
                        mm = pe.matmul(bank[7][:, k:k + 1], macc[:, k * P:(k + 1) * P], ones[:, 0:1], start=True,
                                       stop=True)
                    mm.then_inc(s_m25, 1)

            MOD_AFTER = {5: 2, 7: 3, 9: 4, 11: 5}
            pe.wait_ge(s_cswc, 1)
            for n, ct in enumerate(COLT):
                z_tile(n)
                if ct in GATES_AFTER:
                    gates(GATES_AFTER[ct])
                if n in MOD_AFTER:
                    mod_product(MOD_AFTER[n])

            NU = len(UNITS)
            pe.wait_ge(s_zu, NU)
            pe.wait_ge(s_pd, 2)
            for i in range(NT):
                u = NU + i
                pe.wait_ge(s_zu, u - 3)
                for m, zf in enumerate((zf0, zf1)):
                    mm = pe.matmul(bank[u % 4][:, m * 256:(m + 1) * 256], zf[:, i * P:(i + 1) * P], csw[:, m, :],
                                   start=True, stop=True)
                mm.then_inc(s_z, 1)

            pe.wait_ge(s_mrow, 6)
            pe.wait_ge(s_gu, len(GUNITS))
            for m in range(2):
                for h in range(2):
                    q = 2 * m + h
                    if q >= 2:
                        pe.wait_ge(s_py, q - 1)
                    pe.matmul(bank[6 + q % 2][:], wpb[:, m, :], yT[:, 4 + m, h * HALF:(h + 1) * HALF], start=True,
                              stop=True).then_inc(s_pm, 1)

            pe.wait_ge(s_zu, NU + NT)
            for k in range(NT):
                pe.wait_ge(s_dft[k % 3], 16 * (k // 3 + 1))
                for m in range(2):
                    pe.matmul(bank[4 + m][:, 0:1], Vf[:, k, m, 0:P], K("alt"), start=k == 0, stop=k == NT - 1)
                    pe.matmul(bank[m][:], Vf[:, k, m, 0:P], dring[:, k % 3, 0:HALF], start=k == 0, stop=k == NT - 1)
                    mm = pe.matmul(bank[2 + m][:], Vf[:, k, m, P:2 * P], dring[:, k % 3, HALF:], start=k == 0,
                                   stop=k == NT - 1)
                mm.then_inc(s_dftu, 1)

            pe.wait_ge(s_wout, 32)
            pe.wait_ge(s_y, NI)
            pe.wait_ge(s_py, 4)
            pe.wait_ge(s_fy, 2)

            def out_proj(t):
                for h in range(2):
                    u = 2 * t + h
                    if u >= 4:
                        pe.wait_ge(s_mixu, u - 3)
                    for k in range(KD):
                        mm = pe.matmul(bank[u % 4][:], yT[:, k, t * P:(t + 1) * P],
                                       wout_sb[:, k, h * HALF:(h + 1) * HALF], start=k == 0, stop=k == KD - 1)
                    mm.then_inc(s_mix, 1)

            def turn(t):
                pe.wait_ge(s_xn, t + 1)
                if t >= 1:
                    pe.wait_ge(s_h2, t)
                for k in range(KD):
                    mm = pe.transpose(bank[4 + k // 4][:, (k % 4) * P:(k % 4 + 1) * P], xs[t % 2][:, k * P:(k + 1) * P],
                                      ident)
                mm.then_inc(s_t2, 1)

            def logits(t):
                pe.wait_ge(s_h2, t + 1)
                if t >= 1:
                    pe.wait_ge(s_lg, t)
                for k in range(KD):
                    mm = pe.matmul(bank[6][:, 0:NG + NE], h2[:, k, :], rw[:, k, :], start=k == 0, stop=k == KD - 1)
                mm.then_inc(s_lgp, 1)

            for t in range(NT + 2):
                if t < NT:
                    out_proj(t)
                if 1 <= t <= NT:
                    turn(t - 1)
                if t >= 2:
                    logits(t - 2)

            pe.wait_ge(s_tri, 2)
            pe.wait_ge(s_mk, 1)
            mb = oh[:, 0, :]
            for i in range(NT):
                for j in range(i + 1):
                    pe.matmul(bank[4][:, NE * i:NE * (i + 1)], (tri_b if j == i else ones_b)[:],
                              mb[:, NE * j:NE * (j + 1)], start=j == 0, stop=j == i)
            for j in range(NT):
                mm = pe.matmul(bank[5][:, 0:NE], ones_b[:], mb[:, NE * j:NE * (j + 1)], start=j == 0,
                               stop=j == NT - 1)
            mm.then_inc(s_rk, 1)

            def slot_numbers(q, E1, first=False):
                pe.wait_ge(s_oh, q + 1)
                if not first:
                    pe.wait_ge(s_idf, q)
                for i in range(NT):
                    mm = pe.matmul(bank[7][:, 0:6], oh[:, i, :],
                                   RV[:, E1, i, :] if first else RV[:, bass.ds(E1, 1), i, :].rearrange("p a n -> p (a n)"),
                                   start=i == 0, stop=i == NT - 1)
                mm.then_inc(s_idx, 1)

            def turn_rows(q, r, first=False):
                if r == 0:
                    pe.wait_ge(s_xg, 16 * q + 16)
                if not first or r:
                    pe.wait_ge(s_xgf, 2 * q + r)
                for k in range(4):
                    kk = 4 * r + k
                    mm = pe.transpose(bank[6][:, k * P:(k + 1) * P], xg[:, kk * P:(kk + 1) * P], ident)
                mm.then_inc(s_xgt, 1)

            def gate_up(s, E, par, j):
                pe.wait_ge(s_logu[j], E + 1)
                pe.wait_ge(s_hid, 4 * s + j + 1)
                for g in range(2):
                    o_ = bank[j][:, g * P:(g + 1) * P]
                    for k in range(KD):
                        a = g * D + k * P
                        w_hi, w_lo = WP[:, j, 0, a:a + P], WP[:, j, 1, a:a + P]
                        x_hi, x_lo = xp[:, par, 0, k, :], xp[:, par, 1, k, :]
                        pe.matmul(o_, w_hi, x_hi, start=k == 0, stop=False)
                        pe.matmul(o_, w_hi, x_lo, start=False, stop=False)
                        mm = pe.matmul(o_, w_lo, x_hi, start=False, stop=k == KD - 1)
                mm.then_inc(s_gud, 1)

            def down(s, E, j):
                pe.wait_ge(s_lod[j], E + 1)
                pe.wait_ge(s_hps, 4 * s + j + 5)
                if j == 0:
                    pe.wait_ge(s_ye, 2 * s + 2)
                for h in range(2):
                    w_hi = WP[:, j, 0, 2 * D + h * HALF:2 * D + (h + 1) * HALF]
                    w_lo = WP[:, j, 1, 2 * D + h * HALF:2 * D + (h + 1) * HALF]
                    pe.matmul(bank[4 + h][:], hp[:, j, 0, :], w_hi, start=j == 0, stop=False)
                    pe.matmul(bank[4 + h][:], hp[:, j, 0, :], w_lo, start=False, stop=False)
                    mm = pe.matmul(bank[4 + h][:], hp[:, j, 1, :], w_hi, start=False, stop=j == KE - 1)
                mm.then_inc(s_dd, 1)

            pe.sem_inc(s_gud, 4)
            pe.sem_inc(s_dd, 4)
            slot_numbers(0, 0, first=True)
            for r in range(2):
                turn_rows(0, r, first=True)
            pe.wait_ge(s_tab, 1)
            W = pe.value_load(tab[0:1, 3, 0:1], min_val=NE, max_val=MAXT)
            with pe.Fori(0, MAXT // 2) as it:
                with pe.If(2 * it < W):
                    for par in range(2):
                        s = 2 * it + par
                        E = pe.value_load(tab[0:1, 0, bass.ds(s, 1)], min_val=0, max_val=NE - 1)
                        E1 = pe.value_load(tab[0:1, 0, bass.ds(s + 1, 1)], min_val=0, max_val=NE - 1)
                        pe.wait_ge(s_xgr, 2 * s + 2)
                        gate_up(s, E, par, 0)
                        slot_numbers(s + 1, E1)
                        gate_up(s, E, par, 1)
                        gate_up(s, E, par, 2)
                        down(s, E, 0)
                        turn_rows(s + 1, 0)
                        gate_up(s, E, par, 3)
                        down(s, E, 1)
                        turn_rows(s + 1, 1)
                        down(s, E, 2)
                        down(s, E, 3)

        @block.scalar
        def _(act):
            A_ = act.activation
            act.wait_ge(s_pv, 1)
            A_(silu_c[:].rearrange("p a k -> p (a k)"), pv[:, 0:2 * KD], ACT.Tanh, scale=0.5).then_inc(s_sil, 1)
            act.wait_ge(s_lam, 1)
            A_(lamw[:, 1], lamw[:, 0], ACT.Exp, scale=-1.0).then_inc(s_lame, 1)
            act.wait_ge(s_x, 48)
            for t in range(NT + NC_):
                src = ctxt[:, t] if t < NC_ else xt[:, t - NC_]
                if t >= 2:
                    act.wait_ge(s_ss, t - 1)
                A_(AA[t % 2][:, 0:D], src, ACT.Square, accum_out=stat[:, t:t + 1]).then_inc(s_ss, 1)
            act.wait_ge(s_ms, 1)
            A_(stat[:, 0:10], stat[:, 0:10], ACT.Sqrt).then_inc(s_sq, 1)

            def h_unit(n):
                part = n // KD
                k = n % KD
                g = 1 if part == 0 else 0
                dst = hTc[:, k, :] if part == 0 else hT[:, k, (part - 1) * HALF:part * HALF]
                return k, g, dst, bank[n % 4][:, 0:CTX if part == 0 else HALF]

            act.wait_ge(s_scsh, 1)
            for n in range(0, 3 * KD, 2):
                k, g, dst, src = h_unit(n)
                act.wait_ge(s_tpe, n + 1)
                A_(dst, src, ACT.Identity, scale=sc_mix[:, k, g:g + 1], bias=sh_mix[:, k, g:g + 1]).then_inc(s_tpa, 1)
            act.wait_ge(s_csw, 1)
            A_(csw[:].rearrange("p m n -> p (m n)"), bank[7][:], ACT.Copy).then_inc(s_cswc, 1)

            def take_x(i):
                if i == 0:
                    act.wait_ge(s_zp, 1)
                else:
                    act.wait_ge(s_conv, i)
                if i >= 2:
                    act.wait_ge(s_y, i - 1)
                for part in ("c", 0, 1):
                    u = UNIT[(("x", i), part)]
                    act.wait_ge(s_z, u + 1)
                    w = CTX if part == "c" else HALF
                    zo = 2 if part == "c" else CTX + 5 + part * HALF
                    uo = 0 if part == "c" else CTX + part * HALF
                    A_(zpad[:, zo:zo + w], bank[u % 4][:, 0:w], ACT.Copy)
                    A_(U[i % 2][:, uo:uo + w], bank[u % 4][:, 0:w], ACT.Identity, scale=V("convw", 2 * NI + i),
                       bias=V("convb", i)).then_inc(s_zu, 1)

            def take_g(i):
                if i >= 2:
                    act.wait_ge(s_y, i - 1)
                if i >= 1:
                    act.wait_ge(s_gel, i)
                for part in (0, 1):
                    u = UNIT[(("g", i), part)]
                    act.wait_ge(s_z, u + 1)
                    A_(gz[i % 2][:, part * HALF:(part + 1) * HALF], bank[u % 4][:], ACT.Copy)
                    A_(gt[:, part * HALF:(part + 1) * HALF], bank[u % 4][:], ACT.Square).then_inc(s_zu, 1)

            def gelu_tanh(i):
                act.wait_ge(s_gp, i + 1)
                A_(gt[:], gt[:], ACT.Tanh, scale=GELU_C).then_inc(s_gth, 1)

            def take_p(m):
                for part in (0, 1):
                    u = UNIT[(("p", m), part)]
                    act.wait_ge(s_z, u + 1)
                    A_(yT[:, 4 + m, part * HALF:(part + 1) * HALF], bank[u % 4][:], ACT.Copy).then_inc(s_zu, 1)

            def take_f(m):
                if m == 0:
                    act.wait_ge(s_m25, 6)
                else:
                    act.wait_ge(s_conv, NI)
                for part in (0, 1):
                    u = UNIT[(("f", m), part)]
                    act.wait_ge(s_z, u + 1)
                    A_((zf0, zf1)[m][:, part * HALF:(part + 1) * HALF], bank[u % 4][:], ACT.Copy).then_inc(s_zu, 1)

            def rec_gates(i):
                if i >= 1:
                    act.wait_ge(s_y, i)
                else:
                    act.wait_ge(s_lamc, 1)
                for d in range(2):
                    for g in range(2):
                        for q, (a, w) in enumerate(GPARTS):
                            n = GUNITS.index((i, d, g, q))
                            act.wait_ge(s_g, n + 1)
                            A_((RH, IH)[g][d][:, a:a + w], bank[4 + n % 3][:, 0:w], ACT.Tanh, scale=0.5,
                               bias=hb_[:, 2 * d + g, i:i + 1]).then_inc(s_gu, 1)
                    act.wait_ge(s_gu, GUNITS.index((i, d, 1, 2)) + 1)
                    A_(AA[d][:], RH[d][:], ACT.Exp, scale=lamw[:, 5, d * NI + i:d * NI + i + 1],
                       bias=lamw[:, 5, d * NI + i:d * NI + i + 1])
                    A_(RH[d][:], RH[d][:], ACT.Tanh, scale=lamw[:, 4, d * NI + i:d * NI + i + 1],
                       bias=lamw[:, 4, d * NI + i:d * NI + i + 1]).then_inc(s_ra, 1)

            def rec_root(i):
                for d in range(2):
                    act.wait_ge(s_rm, 2 * i + d + 1)
                    A_(RH[d][:], RH[d][:], ACT.Sqrt, scale=0.25).then_inc(s_rr, 1)

            take_x(0)
            take_g(0)
            gelu_tanh(0)
            take_p(0)
            rec_gates(0)
            take_x(1)
            rec_root(0)
            take_g(1)
            gelu_tanh(1)
            take_p(1)
            rec_gates(1)
            take_x(2)
            rec_root(1)
            take_g(2)
            gelu_tanh(2)
            rec_gates(2)
            take_x(3)
            rec_root(2)
            take_g(3)
            gelu_tanh(3)
            rec_gates(3)
            rec_root(3)
            take_f(0)
            take_f(1)
            NU = len(UNITS)
            for i in range(NT):
                act.wait_ge(s_z, NU + i + 1)
                A_(Vf[:, i].rearrange("p m n -> p (m n)"), bank[(NU + i) % 4][:], ACT.Copy).then_inc(s_zu, 1)
            for q in range(4):
                m, h = q // 2, q % 2
                act.wait_ge(s_pm, q + 1)
                A_(yT[:, 4 + m, h * HALF:(h + 1) * HALF], bank[6 + q % 2][:], ACT.Copy, scale=V("psc", m)).then_inc(s_py, 1)
            act.wait_ge(s_dftu, NT)
            act.wait_ge(s_y, NI)
            for m in range(2):
                A_((gt, Q)[m][:, 0:HALF], bank[m][:], ACT.Copy).then_inc(s_fc, 1)

            for t in range(NT):
                act.wait_ge(s_x1, t + 1)
                A_(xm[t % 2][:], xr[t % NX][:], ACT.Square, accum_out=stat[:, 10 + t:11 + t]).then_inc(s_ss2, 1)
                act.wait_ge(s_ms2, t + 1)
                A_(stat[:, 18 + t:19 + t], stat[:, 10 + t:11 + t], ACT.Sqrt).then_inc(s_rt2, 1)
                act.wait_ge(s_t2, t + 1)
                if t >= 1:
                    act.wait_ge(s_lgp, t)
                for k in range(KD):
                    ins = A_(h2[:, k, :], bank[4 + k // 4][:, (k % 4) * P:(k % 4 + 1) * P], ACT.Identity,
                             scale=sc_ffn[:, k:k + 1], bias=sh_ffn[:, k:k + 1])
                ins.then_inc(s_h2, 1)

            act.wait_ge(s_e1, 1)
            A_(R_["d"], R_["d"], ACT.Exp).then_inc(s_e2, 1)
            act.wait_ge(s_e1, 2)
            A_(R_["ex"], R_["ex"], ACT.Exp).then_inc(s_e2, 1)

            def hi_gate_up(e1, j):
                act.wait_ge(s_raw[j], 48 * e1 + 48)
                A_(WP[:, j, 0, 0:2 * D], raw[:, j, 0:2 * D], ACT.Copy).then_inc(s_hgu, 1)

            def hi_down(e1, j):
                A_(WP[:, j, 0, 2 * D:], raw[:, j, 2 * D:], ACT.Copy).then_inc(s_hdn, 1)

            act.sem_inc(s_ye, 2)
            for j in range(KE):
                hi_gate_up(0, j)
                hi_down(0, j)

            def hi_rows(q, p2, r):
                act.wait_ge(s_xgf, 2 * q + r + 1)
                A_(xp[:, p2, 0, 4 * r:4 * r + 4, :], xt_f[:].rearrange("p (k n) -> p k n", n=P),
                   ACT.Copy).then_inc(s_xgh, 1)

            for r in range(2):
                hi_rows(0, 0, r)
            act.wait_ge(s_tab, 1)
            W = act.value_load(tab[0:1, 3, 0:1], min_val=NE, max_val=MAXT)
            with act.Fori(0, MAXT // 2) as it:
                with act.If(2 * it < W):
                    for par in range(2):
                        s = 2 * it + par
                        L = act.value_load(tab[0:1, 2, bass.ds(s, 1)], min_val=0, max_val=1)
                        E1 = act.value_load(tab[0:1, 0, bass.ds(s + 1, 1)], min_val=0, max_val=NE - 1)

                        def silu(j):
                            act.wait_ge(s_gud, 4 * s + j + 5)
                            act.wait_ge(s_hid, 4 * s + j + 3)
                            A_(sg[:, j % 2, :], bank[j][:, 0:P], ACT.Silu).then_inc(s_sg, 1)

                        def hi_hidden(j):
                            act.wait_ge(s_hid, 4 * s + j + 5)
                            act.wait_ge(s_dd, 4 * s + j + 1)
                            A_(hp[:, j, 0, :], hf[:, j % 2, :], ACT.Copy).then_inc(s_hfr, 1)

                        silu(0)
                        with act.If(L > 0):
                            hi_gate_up(E1, 0)
                        silu(1)
                        hi_hidden(0)
                        with act.If(L > 0):
                            hi_gate_up(E1, 1)
                        silu(2)
                        hi_hidden(1)
                        hi_rows(s + 1, 1 - par, 0)
                        with act.If(L > 0):
                            hi_gate_up(E1, 2)
                        silu(3)
                        hi_hidden(2)
                        hi_hidden(3)
                        hi_rows(s + 1, 1 - par, 1)
                        with act.If(L > 0):
                            hi_gate_up(E1, 3)
                            for j in range(KE):
                                act.wait_ge(s_dd, 4 * s + j + 5)
                                hi_down(E1, j)
                        act.wait_ge(s_dd, 4 * s + 8)
                        act.wait_ge(s_ys, 16 * s + 16)
                        for h in range(2):
                            A_(ysc[:, h * HALF:(h + 1) * HALF], bank[4 + h][:], ACT.Copy,
                               scale=gcol[:, par, 0:1]).then_inc(s_ye, 1)

            for t in range(NT):
                act.wait_ge(s_fx1, t + 1)
                if t:
                    act.wait_ge(s_fs, t)
                A_(fj[:], fx[t % NF][:], ACT.Square, accum_out=stat[:, 28 + t:29 + t]).then_inc(s_fs, 1)
                act.wait_ge(s_fm, t + 1)
                A_(stat[:, 36 + t:37 + t], stat[:, 28 + t:29 + t], ACT.Sqrt).then_inc(s_fr, 1)

        @block.vector
        def _(dve):
            chain = [0]

            def link(ins):
                chain[0] += 1
                ins.then_inc(s_dv, 1)
                dve.wait_ge(s_dv, chain[0])

            tt, ts, stt = dve.tensor_tensor, dve.tensor_scalar, dve.scalar_tensor_tensor
            dve.wait_ge(s_pvp, 1)
            link(dve.tensor_copy(pv[:], bank[7][:, 0:NPV]))
            lamv = V("lam")
            link(ts(lamw[:, 2], lamv, -1.0, None, ALU.mult))
            link(tt(lamw[:, 0], lamw[:, 2], lamv, ALU.max))
            ts(lamw[:, 2], lamw[:, 2], 0.0, None, ALU.max).then_inc(s_lam, 1)
            for d in range(2):
                ts(hb_[:, 2 * d], V("ba")[:, d * NI:(d + 1) * NI], 0.5, None, ALU.mult)
                ts(hb_[:, 2 * d + 1], V("bx")[:, d * NI:(d + 1) * NI], 0.5, None, ALU.mult)
            link(dve.memset(stat[:], 0.0))
            dve.memset(stat[:, 62:63], 0.0).then_inc(s_pv, 1)
            dve.wait_ge(s_sil, 1)
            sc_ = silu_c[:].rearrange("p a k -> p (a k)")
            link(stt(out=sc_, in0=sc_, scalar=1.0, in1=pv[:, 0:2 * KD], op0=ALU.add, op1=ALU.mult))
            ts(sc_, sc_, 0.5, None, ALU.mult).then_inc(s_silu, 1)
            dve.wait_ge(s_lame, 1)
            e_, s2_, p_, s_ = lamw[:, 1], lamw[:, 3], lamw[:, 4], lamw[:, 5]
            link(ts(s_, e_, 2.0, None, ALU.add))
            link(dve.reciprocal(s_, s_))
            link(tt(s_, s_, e_, ALU.mult))
            link(tt(s2_, s_, s_, ALU.mult))
            link(dve.memset(p_, 0.0))
            for n in range(19, 1, -2):
                link(stt(out=p_, in0=p_, scalar=1.0 / n, in1=s2_, op0=ALU.add, op1=ALU.mult))
            link(stt(out=p_, in0=p_, scalar=1.0, in1=s_, op0=ALU.add, op1=ALU.mult))
            link(stt(out=p_, in0=p_, scalar=2.0, in1=lamw[:, 2], op0=ALU.mult, op1=ALU.add))
            link(ts(p_, p_, 1e-25, None, ALU.max))
            ts(s_, p_, -4.0, None, ALU.mult)
            ts(p_, p_, 4.0, None, ALU.mult).then_inc(s_lamc, 1)

            dve.wait_ge(s_ss, NT + NC_)
            ts(stat[:, 0:10], stat[:, 0:10], 1.0 / D, EPS, ALU.mult, ALU.add).then_inc(s_ms, 1)
            dve.wait_ge(s_sq, 1)
            link(dve.reciprocal(stat[:, 0:10], stat[:, 0:10]))
            for t in range(NT + NC_):
                src = ctxt[:, t] if t < NC_ else xt[:, t - NC_]
                ts(src, src, stat[:, t:t + 1], None, ALU.mult).then_inc(s_xs, 1)

            dve.wait_ge(s_modu, 2 * MCH)
            m01 = bank[6][:, 0:4 * KD].rearrange("p (j g) -> p j g", g=2)
            mb_ = V("modb").unsqueeze(2)
            tt(sh_mix[:], m01[:, 0:KD], mb_[:, 0:KD].to_broadcast([P, KD, 2]), ALU.add)
            link(tt(sc_mix[:], m01[:, KD:2 * KD], mb_[:, KD:2 * KD].to_broadcast([P, KD, 2]), ALU.add))
            stt(out=sc_mix[:], in0=sc_mix[:], scalar=1.0, in1=V("gmix").unsqueeze(2).to_broadcast([P, KD, 2]),
                op0=ALU.add, op1=ALU.mult).then_inc(s_scsh, 1)
            dve.wait_ge(s_scsh, 1)
            for n in range(1, 3 * KD, 2):
                part, k = n // KD, n % KD
                g = 1 if part == 0 else 0
                dst = hTc[:, k, :] if part == 0 else hT[:, k, (part - 1) * HALF:part * HALF]
                dve.wait_ge(s_tpe, n + 1)
                ts(dst, bank[n % 4][:, 0:CTX if part == 0 else HALF], sc_mix[:, k, g:g + 1], sh_mix[:, k, g:g + 1],
                   ALU.mult, ALU.add).then_inc(s_tpv, 1)

            def conv(i):
                dve.wait_ge(s_zu, UNIT[(("x", i), 1)] + 1)
                for a, b, w in ((0, 0, CTX), (CTX, CTX + 3, SEQ)):
                    u = U[i % 2][:, a:a + w]
                    for tap in (0, 1, 3):
                        ins = stt(out=u, in0=zpad[:, b + tap:b + tap + w], scalar=V("convw", tap * NI + i), in1=u,
                                  op0=ALU.mult, op1=ALU.add)
                        if tap != 3:
                            link(ins)
                ins.then_inc(s_conv, 1)

            def gelu_poly(i):
                dve.wait_ge(s_zu, UNIT[(("g", i), 1)] + 1)
                link(ts(gt[:], gt[:], 0.044715, 1.0, ALU.mult, ALU.add))
                tt(gt[:], gt[:], gz[i % 2][:], ALU.mult).then_inc(s_gp, 1)

            def gelu_end(i):
                dve.wait_ge(s_gth, i + 1)
                stt(out=gz[i % 2][:], in0=gt[:], scalar=1.0, in1=gz[i % 2][:], op0=ALU.add,
                    op1=ALU.mult).then_inc(s_gel, 1)

            def rec_input(i):
                for d in range(2):
                    dve.wait_ge(s_ra, 2 * i + d + 1)
                    stt(out=IH[d][:], in0=IH[d][:], scalar=1.0, in1=U[i % 2][:], op0=ALU.add, op1=ALU.mult)
                    if d:
                        dve.wait_ge(s_rm, 2 * i + 1)
                    link(tt(Q[:], AA[d][:], AA[d][:], ALU.mult))
                    stt(out=RH[d][:], in0=Q[:], scalar=1.0, in1=RH[d][:], op0=ALU.add, op1=ALU.mult).then_inc(s_rm, 1)

            def rec_scan(i):
                for d in range(2):
                    dve.wait_ge(s_rr, 2 * i + d + 1)
                    link(tt(IH[d][:], IH[d][:], RH[d][:], ALU.mult))
                    if d == 0:
                        link(dve.tensor_tensor_scan(RH[0][:], AA[0][:], IH[0][:], 0.0, ALU.mult, ALU.add))
                    else:
                        r = lambda b_, lo, hi: b_[:, lo:hi][:, ::-1]
                        link(dve.tensor_tensor_scan(r(RH[1], 0, CTX), r(AA[1], 0, CTX), r(IH[1], 0, CTX), 0.0,
                                                    ALU.mult, ALU.add))
                        link(dve.tensor_tensor_scan(r(RH[1], CTX, TOT), r(AA[1], CTX, TOT), r(IH[1], CTX, TOT),
                                                    RH[1][:, 0:1], ALU.mult, ALU.add))
                link(tt(RH[0][:, CTX:], RH[0][:, CTX:], RH[1][:, CTX:], ALU.add))
                stt(out=yT[:, i, :], in0=gz[i % 2][:], scalar=0.5, in1=RH[0][:, CTX:], op0=ALU.mult,
                    op1=ALU.mult).then_inc(s_y, 1)

            def mod_sums(m):
                for q in range(MCH):
                    n = m * MCH + q
                    dve.wait_ge(s_mod[n % 2], 16 * (n // 2 + 1))
                    dst = macc[:, q * 256:(q + 1) * 256]
                    for k in range(KD):
                        ck = silu_c[:, 0, k:k + 1]
                        if k == 0:
                            link(ts(dst, mring[:, n % 2, k, :], ck, None, ALU.mult))
                        else:
                            ins = stt(out=dst, in0=mring[:, n % 2, k, :], scalar=ck, in1=dst, op0=ALU.mult,
                                      op1=ALU.add)
                            if k < KD - 1:
                                link(ins)
                    ins.then_inc(s_modv, 1)
                    dve.wait_ge(s_modv, n + 1 - 2 * MCH)
                dve.memset(stat[:, 62:63], 0.0).then_inc(s_macc, 1)

            def mod_end(m):
                if m in (2, 5):
                    g = g2 if m == 2 else g5
                    dve.wait_ge(s_gb2 if m == 2 else s_gb5, 16)
                    for h in range(2):
                        dve.wait_ge(s_m25, {2: 1, 5: 5}[m] + h)
                        tt(g[:, h * HALF:(h + 1) * HALF], g[:, h * HALF:(h + 1) * HALF], bank[7][:],
                           ALU.add).then_inc(s_mrow, 1)
                elif m == 3:
                    dve.wait_ge(s_m25, 3)
                    tt(sh_ffn[:], bank[7][:, 0:KD], V("modb")[:, 3 * KD:4 * KD], ALU.add).then_inc(s_mrow, 1)
                else:
                    dve.wait_ge(s_m25, 4)
                    link(tt(sc_ffn[:], bank[7][:, 0:KD], V("modb")[:, 4 * KD:5 * KD], ALU.add))
                    stt(out=sc_ffn[:], in0=sc_ffn[:], scalar=1.0, in1=V("gffn"), op0=ALU.add,
                        op1=ALU.mult).then_inc(s_mrow, 1)

            conv(0)
            gelu_poly(0)
            mod_sums(2)
            gelu_end(0)
            rec_input(0)
            conv(1)
            rec_scan(0)
            gelu_poly(1)
            mod_end(2)
            mod_sums(3)
            gelu_end(1)
            rec_input(1)
            conv(2)
            rec_scan(1)
            gelu_poly(2)
            mod_end(3)
            mod_sums(4)
            gelu_end(2)
            rec_input(2)
            conv(3)
            rec_scan(2)
            gelu_poly(3)
            mod_end(4)
            mod_sums(5)
            gelu_end(3)
            rec_input(3)
            rec_scan(3)
            mod_end(5)

            for m in range(2):
                dve.wait_ge(s_fc, m + 1)
                cs = (gt, Q)[m]
                tt(yT[:, 6 + m, 0:HALF], cs[:, 0:HALF], bank[2 + m][:], ALU.add)
                tt(yT[:, 6 + m, HALF + 1:SEQ][:, ::-1], cs[:, 1:HALF], bank[2 + m][:, 1:HALF], ALU.subtract)
                dve.tensor_copy(yT[:, 6 + m, HALF:HALF + 1], bank[4 + m][:, 0:1]).then_inc(s_fy, 1)

            for t in range(NT + 1):
                if t < NT:
                    xb, tmp = xr[t % NX], xm[t % 2]
                    dve.wait_ge(s_xr[t % NX], 16 * (t // NX + 1))
                    for h in range(2):
                        dve.wait_ge(s_mix, 2 * t + h + 1)
                        tt(tmp[:, h * HALF:(h + 1) * HALF], bank[(2 * t + h) % 4][:], g2[:, h * HALF:(h + 1) * HALF],
                           ALU.mult).then_inc(s_mixu, 1)
                    dve.wait_ge(s_mixu, 2 * t + 2)
                    tt(xb[:], xb[:], tmp[:], ALU.add).then_inc(s_x1, 1)
                    dve.wait_ge(s_ss2, t + 1)
                    ts(stat[:, 10 + t:11 + t], stat[:, 10 + t:11 + t], 1.0 / D, EPS, ALU.mult,
                       ALU.add).then_inc(s_ms2, 1)
                    dve.wait_ge(s_rt2, t + 1)
                    link(dve.reciprocal(stat[:, 18 + t:19 + t], stat[:, 18 + t:19 + t]))
                    if t >= 2:
                        dve.wait_ge(s_xnd[t % 2], 16 * (t // 2))
                        dve.wait_ge(s_t2, t - 1)
                    ts(xs[t % 2][:], xb[:], stat[:, 18 + t:19 + t], None, ALU.mult).then_inc(s_xn, 1)
                if t >= 1:
                    if t == 1:
                        dve.wait_ge(s_rw, 64)
                    dve.wait_ge(s_lgp, t)
                    tt(LG[:, t - 1, :], bank[6][:, 0:NG + NE], rb[:], ALU.add).then_inc(s_lg, 1)

            dve.wait_ge(s_lg, NT)
            lg, le = LG[:, :, 0:NG], LG[:, :, NG:].rearrange("p t (g j) -> p t g j", g=NG)
            f4 = K("first4").unsqueeze(1).to_broadcast([P, NT, 4])

            def b4(a):
                return a.unsqueeze(2).to_broadcast([P, NT, 4])

            def first_max(src, mx, hot, key, km):
                link(dve.tensor_reduce(mx, src, AX.X, ALU.max))
                link(tt(key, src, b4(mx), ALU.is_equal))
                link(tt(key, key, f4, ALU.mult))
                link(dve.tensor_reduce(km, key, AX.X, ALU.max))
                link(tt(hot, key, b4(km), ALU.is_equal))

            first_max(lg, R_["m"], R_["goh"], R_["key"], R_["km"])
            tt(R_["d"], lg, b4(R_["m"]), ALU.subtract).then_inc(s_e1, 1)
            link(tt(R_["big"], le, R_["goh"].unsqueeze(3).to_broadcast([P, NT, NG, EPG]), ALU.mult))
            link(dve.tensor_reduce(R_["les"], R_["big"].rearrange("p t g j -> p t j g"), AX.X, ALU.add))
            first_max(R_["les"], R_["m1"], R_["oh1"], R_["key"], R_["km"])
            link(stt(out=R_["les"], in0=R_["oh1"], scalar=-3e38, in1=R_["les"], op0=ALU.mult, op1=ALU.add))
            first_max(R_["les"], R_["m2"], R_["oh2"], R_["key"], R_["km"])
            tt(R_["ex"], R_["m2"], R_["m1"], ALU.subtract).then_inc(s_e1, 1)
            dve.wait_ge(s_e2, 1)
            link(dve.tensor_reduce(R_["pg"], R_["d"], AX.X, ALU.add))
            dve.wait_ge(s_e2, 2)
            link(ts(R_["w1"], R_["ex"], 1.0, None, ALU.add))
            link(tt(R_["w1"], R_["w1"], R_["pg"], ALU.mult))
            link(dve.reciprocal(R_["w1"], R_["w1"]))
            link(tt(R_["w2"], R_["w1"], R_["ex"], ALU.mult))
            M1, M2, G = R_["M1"], R_["M2"], R_["G"]
            g_b = R_["goh"].unsqueeze(3).to_broadcast([P, NT, NG, EPG])
            for M_, o_, w_ in ((M1, "oh1", "w1"), (M2, "oh2", "w2")):
                link(dve.tensor_copy(R_["big"], R_[o_].unsqueeze(2).to_broadcast([P, NT, NG, EPG])))
                link(tt(M_, R_["big"], g_b, ALU.mult))
            m16 = lambda a: a.rearrange("p t g j -> p t (g j)")
            w16 = lambda a: a.unsqueeze(2).to_broadcast([P, NT, NE])
            link(tt(m16(G), m16(M1), w16(R_["w1"]), ALU.mult))
            link(tt(m16(R_["big"]), m16(M2), w16(R_["w2"]), ALU.mult))
            link(tt(G, G, R_["big"], ALU.add))
            link(tt(M1, M1, M2, ALU.add))
            dve.tensor_copy(oh[:, 0, :].rearrange("p (t e) -> p t e", e=NE), m16(M1)).then_inc(s_mk, 1)
            ge = G.rearrange("p t g j -> p (g j) t")
            rem = R_["rem"]
            dve.tensor_copy(RV[:, :, :, 0], K("pidx").unsqueeze(2).to_broadcast([P, NE, NT]))
            dve.tensor_copy(RV[:, :, :, 1], K("tok0").unsqueeze(1).to_broadcast([P, NE, NT]))
            dve.memset(RV[:, :, :, 2], 1.0)
            link(dve.tensor_copy(RV[:, :, :, 3], ge))
            link(tt(rem, ge, RV[:, :, :, 3], ALU.subtract))
            link(dve.tensor_copy(RV[:, :, :, 4], rem))
            link(tt(rem, rem, RV[:, :, :, 4], ALU.subtract))
            link(dve.tensor_copy(RV[:, :, :, 5], rem))
            dve.wait_ge(s_rk, 1)
            rk = bank[4][:, 0:P].rearrange("p (t e) -> p e t", e=NE)
            me = M1.rearrange("p t g j -> p (g j) t")
            link(stt(out=RK[:], in0=rk, scalar=1.0, in1=me, op0=ALU.add, op1=ALU.mult))
            link(ts(RK[:], RK[:], -1.0, None, ALU.add))

            row = lambda a, n: rs[0:1, a:a + n]
            cnt, nt_, inc, sq_ = row(1200, NE), row(1216, NE), row(1232, NE), row(1248, NE)
            t7 = row(0, NE * 7).rearrange("p (e k) -> p e k", k=7)
            link(dve.tensor_copy(cnt, bank[5][0:1, 0:NE]))
            link(tt(t7, cnt.unsqueeze(2).to_broadcast([1, NE, 7]),
                    K("tcount")[0:1].unsqueeze(1).to_broadcast([1, NE, 7]), ALU.is_gt))
            link(dve.tensor_reduce(nt_, t7, AX.X, ALU.add))
            link(ts(nt_, nt_, 1.0, None, ALU.add))
            link(dve.tensor_tensor_scan(inc, K("ones")[0:1, 0:NE], nt_, 0.0, ALU.mult, ALU.add))
            link(tt(sq_, inc, nt_, ALU.subtract))
            big = row(0, TAB * NE).rearrange("p (s e) -> p s e", e=NE)
            eT, mT, lT = row(1264, TAB), row(1300, TAB), row(1340, TAB)
            sq_b = sq_.unsqueeze(1).to_broadcast([1, TAB, NE])
            link(tt(big, sq_b, K("sidx")[0:1].unsqueeze(2).to_broadcast([1, TAB, NE]), ALU.is_le))
            link(dve.tensor_reduce(eT, big, AX.X, ALU.add))
            link(ts(eT, eT, -1.0, None, ALU.add))
            link(tt(big, big, sq_b, ALU.mult))
            link(dve.tensor_reduce(mT, big, AX.X, ALU.max))
            link(tt(mT, K("sidx")[0:1], mT, ALU.subtract))
            link(dve.memset(lT, 0.0))
            link(tt(lT[:, 0:TAB - 1], eT[:, 1:TAB], eT[:, 0:TAB - 1], ALU.subtract))
            pr = row(1400, MAXT // 2)
            link(ts(pr, K("slot0")[0:1, 0:MAXT // 2], 2.0 / P, None, ALU.mult))
            link(tt(pr, pr, inc[:, NE - 1:NE].to_broadcast([1, MAXT // 2]), ALU.is_lt))
            link(dve.tensor_reduce(row(1440, 1), pr, AX.X, ALU.add))
            link(ts(row(1440, 1), row(1440, 1), 2.0, None, ALU.mult))
            link(dve.tensor_copy(tab[0:1, 0, :], eT))
            link(dve.tensor_copy(tab[0:1, 1, :], mT))
            link(dve.tensor_copy(tab[0:1, 2, :], lT))
            link(dve.tensor_copy(tab[0:1, 3, 0:1], inc[:, NE - 1:NE]))
            dve.tensor_copy(tab[0:1, 3, 1:2], row(1440, 1)).then_inc(s_tab, 1)
            dve.wait_ge(s_tab, 1)

            def lo_gate_up(e1, j):
                dve.wait_ge(s_hgu, 4 * e1 + j + 1)
                tt(WP[:, j, 1, 0:2 * D], raw[:, j, 0:2 * D], WP[:, j, 0, 0:2 * D].bitcast(F32),
                   ALU.subtract).then_inc(s_logu[j], 1)

            NLINK = 7

            def prepare_slots(q, E1, T1, first=False):
                def plink(ins, k):
                    ins.then_inc(s_pch, 1)
                    dve.wait_ge(s_pch, NLINK * q + k)
                rk1 = RK[:, 0, :] if first else RK[:, bass.ds(E1, 1), :].rearrange("p a n -> p (a n)")
                s0 = K("slot0")[:, 0:1] if first else K("slot0")[:, bass.ds(T1, 1)]
                plink(ts(rkt[:], rk1, s0, None, ALU.subtract), 1)
                if not first:
                    dve.wait_ge(s_idx, q)
                tt(oh[:], K("iota").unsqueeze(1).to_broadcast([P, NT, P]),
                   rkt[:].unsqueeze(2).to_broadcast([P, NT, P]), ALU.is_equal).then_inc(s_oh, 1)

            def slot_ids(q, p2, first=False):
                def plink(ins, k):
                    ins.then_inc(s_pch, 1)
                    dve.wait_ge(s_pch, NLINK * q + k)
                dve.wait_ge(s_idx, q + 1)
                if not first:
                    dve.wait_ge(s_pch, NLINK * q - 2)
                dve.tensor_copy(idf[:, 0:6], bank[7][:, 0:6]).then_inc(s_idf, 1)
                dve.wait_ge(s_idf, q + 1)
                if not first:
                    dve.wait_ge(s_xg, 16 * q)
                tt(idg[:], idf[:, 0:1], idf[:, 1:2], ALU.add).then_inc(s_ids, 1)
                plink(tt(idf[:, 6:7], idf[:, 0:1], idf[:, 1:2], ALU.add), 2)
                plink(stt(out=idf[:, 7:8], in0=idf[:, 2:3], scalar=K("dump"), in1=idf[:, 6:7], op0=ALU.mult,
                          op1=ALU.subtract), 3)
                if not first:
                    dve.wait_ge(s_ys, 16 * q)
                plink(ts(ids[:, p2], idf[:, 7:8], -1.0, K("dump"), ALU.mult, ALU.add), 4)
                dve.tensor_reduce(gcol[:, p2], idf[:, 3:6], AX.X, ALU.add).then_inc(s_pch, 1)

            def modulate_rows(q, r, first=False):
                def plink(ins, k):
                    ins.then_inc(s_pch, 1)
                    dve.wait_ge(s_pch, NLINK * q + k)
                k4 = slice(4 * r, 4 * r + 4)
                dve.wait_ge(s_xgt, 2 * q + r + 1)
                if not first or r:
                    dve.wait_ge(s_xgr, 2 * q + r)
                v3 = xt_f[:].rearrange("p (k n) -> p k n", n=P)
                plink(tt(v3, bank[6][:].rearrange("p (k n) -> p k n", n=P),
                         sc_ffn[:, k4].unsqueeze(2).to_broadcast([P, 4, P]), ALU.mult), 6 + r)
                tt(v3, v3, sh_ffn[:, k4].unsqueeze(2).to_broadcast([P, 4, P]), ALU.add).then_inc(s_xgf, 1)

            def lo_rows(q, p2, r):
                dve.wait_ge(s_xgh, 2 * q + r + 1)
                tt(xp[:, p2, 1, 4 * r:4 * r + 4, :], xt_f[:].rearrange("p (k n) -> p k n", n=P),
                   xp[:, p2, 0, 4 * r:4 * r + 4, :].bitcast(F32), ALU.subtract).then_inc(s_xgr, 1)

            dve.sem_inc(s_hid, 4)
            dve.sem_inc(s_hps, 4)
            prepare_slots(0, 0, 0, first=True)
            slot_ids(0, 0, first=True)
            for j in range(KE):
                lo_gate_up(0, j)
            for r in range(2):
                modulate_rows(0, r, first=True)
                lo_rows(0, 0, r)
            W = dve.value_load(tab[0:1, 3, 0:1], min_val=NE, max_val=MAXT)
            with dve.Fori(0, MAXT // 2) as it:
                with dve.If(2 * it < W):
                    for par in range(2):
                        s = 2 * it + par
                        L = dve.value_load(tab[0:1, 2, bass.ds(s, 1)], min_val=0, max_val=1)
                        E1 = dve.value_load(tab[0:1, 0, bass.ds(s + 1, 1)], min_val=0, max_val=NE - 1)
                        T1 = dve.value_load(tab[0:1, 1, bass.ds(s + 1, 1)], min_val=0, max_val=TAB - 1)

                        def product(j):
                            dve.wait_ge(s_sg, 4 * s + j + 1)
                            dve.wait_ge(s_hps, 4 * s + j + 3)
                            tt(hf[:, j % 2, :], bank[j][:, P:2 * P], sg[:, j % 2, :], ALU.mult).then_inc(s_hid, 1)

                        def lo_hidden(j):
                            dve.wait_ge(s_hfr, 4 * s + j + 1)
                            tt(hp[:, j, 1, :], hf[:, j % 2, :], hp[:, j, 0, :].bitcast(F32),
                               ALU.subtract).then_inc(s_hps, 1)

                        prepare_slots(s + 1, E1, T1)
                        product(0)
                        slot_ids(s + 1, 1 - par)
                        with dve.If(L > 0):
                            lo_gate_up(E1, 0)
                        product(1)
                        lo_hidden(0)
                        with dve.If(L > 0):
                            lo_gate_up(E1, 1)
                        product(2)
                        lo_hidden(1)
                        dve.wait_ge(s_gud, 4 * s + 4)
                        modulate_rows(s + 1, 0)
                        lo_rows(s + 1, 1 - par, 0)
                        with dve.If(L > 0):
                            lo_gate_up(E1, 2)
                        product(3)
                        lo_hidden(2)
                        lo_hidden(3)
                        modulate_rows(s + 1, 1)
                        lo_rows(s + 1, 1 - par, 1)
                        with dve.If(L > 0):
                            lo_gate_up(E1, 3)

            dve.wait_ge(s_gf, 16)
            for t in range(NT):
                n = t % NF
                dve.wait_ge(s_fl[n], 32 * (t // NF + 1))
                link(tt(fa[n][:], fa[n][:], g5[:], ALU.mult))
                tt(fx[n][:], fx[n][:], fa[n][:], ALU.add).then_inc(s_fx1, 1)
                dve.wait_ge(s_fs, t + 1)
                ts(stat[:, 28 + t:29 + t], stat[:, 28 + t:29 + t], 1.0 / D, EPS, ALU.mult, ALU.add).then_inc(s_fm, 1)
                dve.wait_ge(s_fr, t + 1)
                link(dve.reciprocal(stat[:, 36 + t:37 + t], stat[:, 36 + t:37 + t]))
                if t >= NF:
                    dve.wait_ge(s_out[n], 16 * (t // NF))
                stt(out=fo[n][:], in0=fx[n][:], scalar=stat[:, 36 + t:37 + t], in1=gfin[:], op0=ALU.mult,
                    op1=ALU.mult).then_inc(s_fo, 1)


_INS = ["x", "c", "ctx", "c_ctx", "mod_w", "mod_b", "norm_mix_g", "norm_ffn_g", "w_in", "conv_w", "conv_b",
        "rec_gate_a_w", "rec_gate_a_b", "rec_gate_x_w", "rec_gate_x_b", "rec_lambda", "pool_w", "pool_scale",
        "fourier_w", "w_out", "router_group_w", "router_group_b", "router_expert_w", "router_expert_b",
        "expert_w_gate", "expert_w_up", "expert_w_down", "final_norm_g"]


def kernel(**inputs):
    import concourse.bacc as bacc
    from concourse.bass_utils import run_bass_kernel_spmd

    nc = bacc.Bacc("TRN2", target_bir_lowering=False, num_devices=1)
    arrays, args = {}, []
    packed, dft = constants()
    for name in _INS + ["consts", "dft"]:
        a = {"consts": packed, "dft": dft}[name] if name in ("consts", "dft") else np.ascontiguousarray(inputs[name])
        arrays[f"in_{name}"] = a
        args.append(nc.dram_tensor(f"in_{name}", a.shape, mybir.dt.from_np(a.dtype), kind="ExternalInput").ap())
    args.append(nc.dram_tensor("result", (1, SEQ, D), F32, kind="ExternalOutput").ap())
    build(nc, *args)
    r = run_bass_kernel_spmd(nc, [arrays], core_ids=[0])
    return r.results[0]["result"]
```

```python
from contextlib import ExitStack

import numpy as np
import concourse.bass as bass
from concourse import mybir

F32 = mybir.dt.float32
F32R = mybir.dt.float32r
BF16 = mybir.dt.bfloat16
I32 = mybir.dt.int32
ALU = mybir.AluOpType
ACT = mybir.ActivationFunctionType
AX = mybir.AxisListType

P = 128
D = 1024
KD = D // P
SEQ = 1024
NT = SEQ // P
CTX = 256
NC_ = CTX // P
ROWS, COLS = 16, 64
D_REC, D_POOL, D_FOUR = 512, 256, 256
D_IN = 2 * D_REC + D_POOL + D_FOUR
NI = D_REC // P
TOT = CTX + SEQ
HALF = 512
GRID_PAD = 8
NE, NG, EPG = 16, 4, 4
DE = 512
KE = DE // P
EPS = 1e-6
GELU_C = float(np.sqrt(2.0 / np.pi))
MAXT = SEQ * 2 // P + NE
TAB = MAXT + 2
NFLD = 5

CO = {}
_at = 0
for _n, _w in (("ident", P), ("ones", P), ("tri", P), ("iota", P), ("cos64", P), ("sin64", P), ("icr", 2 * ROWS),
               ("icc", 2 * COLS), ("alt", 1), ("pidx", 1), ("slot0", TAB), ("tok0", NT), ("first4", 4),
               ("tcount", 7), ("sidx", TAB), ("dump", 1)):
    CO[_n] = (_at, _at + _w)
    _at += _w
NCONST = _at

PV = {}
_at = 0
for _n, _w in (("c", KD), ("cc", KD), ("gmix", KD), ("gffn", KD), ("modb", 6 * KD), ("convw", 4 * NI), ("convb", NI),
               ("ba", 2 * NI), ("bx", 2 * NI), ("lam", 2 * NI), ("psc", 2)):
    PV[_n] = (_at, _at + _w)
    _at += _w
NPV = _at


def constants():
    c = np.zeros((P, NCONST), np.float32)

    def put(name, value):
        c[:, CO[name][0]:CO[name][1]] = value

    put("ident", np.eye(P))
    put("ones", 1.0)
    put("tri", np.triu(np.ones((P, P)), 1))
    put("iota", np.arange(P)[None])
    h = np.arange(64)
    ang = 2 * np.pi * np.outer(h, h) / 64
    scale = 1.0 / np.sqrt(SEQ * 64)
    put("cos64", np.kron(np.eye(2), np.cos(ang) * scale))
    put("sin64", np.kron(np.eye(2), -np.sin(ang) * scale))
    for m in range(2):
        for half in range(2):
            w = (2, 4, 8, 16)[2 * m + half]
            for name, n in (("icr", ROWS), ("icc", COLS)):
                t = np.arange(n)
                cnt = np.clip(t + w // 2, 0, n) - np.clip(t - w // 2, 0, n)
                c[64 * half:64 * half + 64, CO[name][0] + m * n:CO[name][0] + (m + 1) * n] = 1.0 / cnt
    p = np.arange(P)[:, None]
    put("alt", 1.0 - 2.0 * (p % 2))
    put("pidx", p)
    put("slot0", P * np.arange(TAB)[None])
    put("tok0", P * np.arange(NT)[None])
    put("first4", np.array([[4, 3, 2, 1]]))
    put("tcount", P * np.arange(1, 8)[None])
    put("sidx", np.arange(TAB)[None])
    put("dump", SEQ + p)
    n = np.arange(SEQ)
    ang = 2 * np.pi * (np.outer(n, np.arange(HALF)) % SEQ) / SEQ
    dft = np.concatenate([np.cos(ang), np.sin(ang)], axis=1).astype(np.float32)
    return c, dft


def build(nc, x, c, ctx, c_ctx, mod_w, mod_b, norm_mix_g, norm_ffn_g, w_in, conv_w, conv_b, gate_a_w, gate_a_b,
          gate_x_w, gate_x_b, lam, pool_w, pool_scale, fourier_w, w_out, rg_w, rg_b, re_w, re_b, wg, wu, wd,
          final_g, consts, dft, out):
    xn_d = nc.dram_tensor("normed_rows", [SEQ, D], F32).ap()
    x1_d = nc.dram_tensor("mixed_rows", [SEQ, D], F32).ap()
    y_d = nc.dram_tensor("expert_rows", [MAXT, P, D], F32).ap()

    es = ExitStack()
    with es:
        free_at = [0]
        base = (nc.sbuf_usable_end - nc.sbuf_bytes_remaining + 63) // 64 * 64
        end = nc.sbuf_usable_end

        def at(name, shape, dt, off):
            size = int(np.prod(shape[1:])) * (2 if dt == BF16 else 4)
            assert base + off + size <= end, (name, base + off + size - end)
            free_at[0] = max(free_at[0], off + size)
            return nc.alloc_sbuf_tensor_at(name, list(shape), dt, offset=base + off)

        cursor = [0]

        def keep(name, shape, dt=F32):
            off = cursor[0]
            size = int(np.prod(shape[1:])) * (2 if dt == BF16 else 4)
            cursor[0] += (size + 31) // 32 * 32
            return at(name, shape, dt, off)

        def sem(name):
            return es.enter_context(nc.semaphore(name))

        bank = [es.enter_context(nc.psum_tensor(f"bank{i}", [P, HALF], F32)) for i in range(8)]

        cst = keep("cst", [P, NCONST])
        pv = keep("pv", [P, NPV])
        g2 = keep("g2", [P, D])
        g5 = keep("g5", [P, D])
        sc_mix = keep("sc_mix", [P, KD, 2])
        sh_mix = keep("sh_mix", [P, KD, 2])
        silu_c = keep("silu_c", [P, 2, KD])
        rw = keep("rw", [P, KD, NG + NE])
        rb = keep("rb", [P, NG + NE])
        stat = keep("stat", [P, 64])
        LG = keep("LG", [P, NT, NG + NE])
        tri_b = keep("tri_b", [P, P], BF16)
        ones_b = keep("ones_b", [P, P], BF16)
        held = keep("held", [P, 1])
        pos = keep("pos", [P, 2, NT], I32)
        PHASE = cursor[0]

        def K(name):
            return cst[:, CO[name][0]:CO[name][1]]

        ident, ones = K("ident"), K("ones")

        def V(name, i=None):
            a, b = PV[name]
            return pv[:, a:b] if i is None else pv[:, a + i:a + i + 1]

        o = PHASE
        hT = at("hT", [P, KD, SEQ], F32, o)
        wout_sb = at("wout_sb", [P, KD, D], F32, o); o += 32768
        yT = at("yT", [P, KD, SEQ], F32, o)
        xt = at("xt", [P, NT, D], F32, o); o += 32768
        hTc = at("hTc", [P, KD, CTX], F32, o)
        scr = at("scr", [P, D], F32, o)
        shr = at("shr", [P, D], F32, o + 4096); o += 8192
        wring = at("wring", [P, 3, KD, P], F32, o); o += 12288
        dring = at("dring", [P, 3, SEQ], F32, o - 12288)
        mring = at("mring", [P, 2, KD, 256], F32, o)
        gff = at("gff", [P, D], F32, o); o += 16384
        macc = at("macc", [P, D], F32, o); o += 4096
        rec0 = o
        RH = [at(f"RH{d}", [P, TOT], F32, o + 5120 * d) for d in range(2)]
        IH = [at(f"IH{d}", [P, TOT], F32, o + 10240 + 5120 * d) for d in range(2)]
        AA = [at(f"AA{d}", [P, TOT], F32, o + 20480 + 5120 * d) for d in range(2)]
        Q = at("Q", [P, TOT], F32, o + 30720); o += 35840
        U = [at(f"U{d}", [P, TOT], F32, o + 5120 * d) for d in range(2)]; o += 10240
        ZPL = TOT + 6
        zpad = at("zpad", [P, ZPL], F32, o)
        zf1 = at("zf1", [P, SEQ], F32, o); o += 5152
        gz = [at(f"gz{d}", [P, SEQ], F32, o + 4096 * d) for d in range(2)]
        gt = at("gt", [P, SEQ], F32, o + 8192); o += 12288
        P0 = at("P0", [P, 2 * ROWS, COLS], F32, o)
        P1 = at("P1", [P, 2 * ROWS, COLS], F32, o + 8192)
        C0 = at("C0", [P, ROWS, COLS + 16], F32, o)
        C1 = at("C1", [P, ROWS, COLS + 16], F32, o + 8192)
        Vf = at("Vf", [P, NT, 2, 256], F32, o)
        ctxt = at("ctxt", [P, NC_, D], F32, o); o += 16384
        prow = at("prow", [P, P], F32, o - 4096)
        zf0 = at("zf0", [P, SEQ], F32, rec0 - 4096)
        bdg = at("bdg", [P, 4, NI, P], F32, o); o += 8192
        wfb = at("wfb", [P, 2, P], F32, o); o += 1024
        csw = at("csw", [P, 2, 256], F32, PHASE + 32768 + 6 * 4096)
        wpb = at("wpb", [P, 2, P], F32, o); o += 1024
        lamw = at("lamw", [P, 6, 2 * NI], F32, o); o += 192
        hb_ = at("hb_", [P, 4, NI], F32, o); o += 64
        NX = 3
        xr = [at(f"xr{n}", [P, D], F32, rec0 + 4096 * n) for n in range(NX)]
        xm = [at(f"xm{n}", [P, D], F32, rec0 + 12288 + 4096 * n) for n in range(2)]
        xs = [at(f"xs{n}", [P, D], F32, rec0 + 20480 + 4096 * n) for n in range(2)]
        h2 = at("h2", [P, KD, P], F32, rec0 + 28672)

        o = PHASE
        WP = at("WP", [P, KE, 2, 3 * D], F32R, o); o += KE * 2 * 3 * D * 4
        raw = at("raw", [P, KE, 3 * D], F32, o); o += KE * 3 * D * 4
        xg = at("xg", [P, D], F32, o); o += 4096
        xp = at("xp", [P, 2, 2, KD, P], F32R, o); o += 16384
        sg = at("sg", [P, HALF], F32, o); o += 2048
        hp = at("hp", [P, 2, KE, P], F32R, o); o += 4096
        ysc = at("ysc", [P, 2, D], F32, o); o += 8192
        oh = at("oh", [P, NT, P], BF16, o); o += 2048
        RK = at("RK", [P, NE, NT], F32, o); o += 512
        rkt = at("rkt", [P, NT], F32, o); o += 32
        RV = at("RV", [P, NE, NT, NFLD], BF16, o); o += 1280
        idf = at("idf", [P, 8], F32, o); o += 32
        idg = at("idg", [P, 1], I32, o); o += 32
        gcol = at("gcol", [P, 2, 1], F32, o); o += 32
        tab = at("tab", [1, 4, TAB], I32, o); o += 640
        rs = at("rs", [P, 1800], F32, o)
        R_ = {}
        ra = 0
        for n_, sh_ in (("m", ()), ("goh", (4,)), ("key", (4,)), ("km", ()), ("d", (4,)), ("les", (4,)), ("m1", ()),
                        ("oh1", (4,)), ("m2", ()), ("oh2", (4,)), ("ex", ()), ("pg", ()), ("w1", ()), ("w2", ()),
                        ("big", (4, 4)), ("M1", (4, 4)), ("M2", (4, 4)), ("G", (4, 4)), ("rem", (NE, NT))):
            size = NT * int(np.prod(sh_)) if n_ != "rem" else NE * NT
            v_ = rs[:, ra:ra + size]
            if n_ == "rem":
                v_ = v_.rearrange("p (e t) -> p e t", t=NT)
            elif len(sh_) == 1:
                v_ = v_.rearrange("p (t a) -> p t a", a=4)
            elif len(sh_) == 2:
                v_ = v_.rearrange("p (t a b) -> p t a b", a=4, b=4)
            R_[n_] = v_
            ra += size
        NF = 4
        fa = [at(f"fa{n}", [P, D], F32, PHASE + 4096 * n) for n in range(NF)]
        fb = [at(f"fb{n}", [P, D], F32, PHASE + 16384 + 4096 * n) for n in range(NF)]
        fx = [at(f"fx{n}", [P, D], F32, PHASE + 32768 + 4096 * n) for n in range(NF)]
        gfin = at("gfin", [P, D], F32, PHASE + 49152)
        fj = at("fj", [P, D], F32, PHASE + 53248)

        s_cst = sem("consts_in")
        s_prow = sem("param_rows_in")
        s_x = sem("x_in")
        s_rw = sem("router_in")
        s_bd = sem("blockdiag_in")
        s_gb2 = sem("mix_gate_bias_in")
        s_gb5 = sem("ffn_gate_bias_in")
        s_gf = sem("final_gain_in")
        s_bd0 = sem("blockdiag_zeroed")
        s_mod = [sem(f"modw_in{n}") for n in range(2)]
        s_modu = sem("modw_used_by_pe")
        s_modv = sem("modw_used_by_dve")
        s_win = [sem(f"win_in{n}") for n in range(3)]
        s_dft = [sem(f"dft_in{n}") for n in range(3)]
        s_dftu = sem("dft_used")
        s_wout = sem("wout_in")
        s_zero = sem("zero_row")
        s_zero_d = sem("sums_zeroed")
        s_pvp = sem("params_transposed")
        s_pv = sem("params_ready")
        s_sil = sem("silu_tanh")
        s_silu = sem("silu_ready")
        s_ss = sem("x_square_sums")
        s_ms = sem("x_mean_squares")
        s_sq = sem("x_root")
        s_xs = sem("x_scaled")
        s_scsh = sem("mix_scale_shift")
        s_tpe = sem("x_transposed")
        s_z = sem("z_ready")
        s_zu = sem("z_taken")
        s_conv = sem("u_ready")
        s_g = sem("gates_ready")
        s_gu = sem("gates_taken")
        s_ra = sem("decay_ready")
        s_rm = sem("input_scaled")
        s_rr = sem("root_ready")
        s_y = sem("recurrent_done")
        s_gp = sem("gelu_poly")
        s_gth = sem("gelu_tanh")
        s_gel = sem("gelu_ready")
        s_pd = sem("pool_diff")
        s_pm = sem("pool_product")
        s_py = sem("pool_ready")
        s_csw = sem("csw_product")
        s_cswc = sem("csw_ready")
        s_fc = sem("dft_copied")
        s_fy = sem("fourier_ready")
        s_lam = sem("lam_abs")
        s_lame = sem("lam_exp")
        s_lamc = sem("lam_ready")
        s_macc = sem("mod_summed")
        s_m25 = sem("mod_product")
        s_mrow = sem("mod_ready")
        s_mix = sem("mix_ready")
        s_mixu = sem("mix_taken")
        s_xr = [sem(f"x_again{n}") for n in range(NX)]
        s_x1 = sem("x1_ready")
        s_x1d = [sem(f"x1_stored{n}") for n in range(NX)]
        s_ss2 = sem("x1_square_sum")
        s_ms2 = sem("x1_mean_square")
        s_rt2 = sem("x1_root")
        s_xn = sem("xn_ready")
        s_xnd = [sem(f"xn_stored{n}") for n in range(2)]
        s_t2 = sem("xn_transposed")
        s_h2 = sem("h2_ready")
        s_lgp = sem("logits_summed")
        s_lg = sem("logits_ready")
        s_e1 = sem("router_exponents")
        s_e2 = sem("router_exps")
        s_mk = sem("masks_ready")
        s_rk = sem("ranks_summed")
        s_tab = sem("tables_ready")
        s_dv = sem("vector_chain")
        s_pc = sem("pool_engine_chain")
        s_rgu = [sem(f"raw_gate_up_in{j}") for j in range(KE)]
        s_rdn = [sem(f"raw_down_in{j}") for j in range(KE)]
        s_logu = [sem(f"gate_up_split{j}") for j in range(KE)]
        s_lod = [sem(f"down_split{j}") for j in range(KE)]
        s_gate = sem("gate_done")
        s_gud = sem("gate_up_done")
        s_dd = sem("down_done")
        s_hT = sem("hidden_transposed")
        s_sg = sem("silu_done")
        s_hid = sem("hidden_product")
        s_hfr = sem("hidden_hi")
        s_hps = sem("hidden_ready")
        s_oh = sem("onehot_ready")
        s_idx = sem("slots_summed")
        s_idf = sem("slot_fields")
        s_ids = sem("slot_ids_ready")
        s_xg = sem("rows_gathered")
        s_xgt = sem("rows_transposed")
        s_xgh = sem("rows_hi")
        s_xgr = sem("rows_ready")
        s_ye = sem("y_scaled")
        s_ys = [sem(f"y_stored{n}") for n in range(2)]
        s_held = sem("pool_held")
        s_end = sem("experts_finished")
        s_zp = sem("conv_pads_zeroed")
        s_tri = sem("bf16_constants")
        s_tpa = sem("h_ready_scalar")
        s_tpv = sem("h_ready_vector")
        s_hgu = sem("gate_up_hi")
        s_hdn = sem("down_hi")
        s_pch = sem("prepare_chain")
        s_fg = [sem(f"expert_rows_in{n}") for n in range(NF)]
        s_gb3 = sem("shift_bias_in")
        s_gb4 = sem("scale_bias_in")
        s_gff = sem("ffn_gain_in")
        s_fl = [sem(f"sums_in{n}") for n in range(NF)]
        s_fx1 = sem("final_sum")
        s_fs = sem("final_square")
        s_fm = sem("final_mean")
        s_fr = sem("final_root")
        s_fo = sem("final_row")
        s_out = [sem(f"out_stored{n}") for n in range(NF)]

        COLT = [("x", 0), ("g", 0), ("p", 0), ("x", 1), ("g", 1), ("p", 1), ("x", 2), ("g", 2), ("x", 3), ("g", 3),
                ("f", 0), ("f", 1)]
        OFF = {"x": 0, "g": D_REC, "p": 2 * D_REC, "f": 2 * D_REC + D_POOL}
        GATES_AFTER = {("p", 0): 0, ("p", 1): 1, ("g", 2): 2, ("g", 3): 3}
        UNITS = [(ct, part) for ct in COLT for part in ((("c",) if ct[0] == "x" else ()) + (0, 1))]
        UNIT = {u: n for n, u in enumerate(UNITS)}
        GPARTS = [(CTX, HALF), (CTX + HALF, HALF), (0, CTX)]
        GUNITS = [(i, d, g, q) for i in range(NI) for d in range(2) for g in range(2) for q in range(3)]
        NMC = 6 * D // 256
        MORD = (0, 1, 2, 5, 3, 4)
        MCH = D // 256

        block = es.enter_context(nc.Block())

        @block.sync
        def _(sp):
            sp.dma_start(cst[:], consts).then_inc(s_cst, 16)
            rows = lambda a: a.rearrange("(r q) -> r q", q=P)
            prows = [("c", rows(c[0])), ("cc", rows(c_ctx)), ("gmix", rows(norm_mix_g[0])),
                     ("gffn", rows(norm_ffn_g[0])), ("modb", rows(mod_b[0])),
                     ("convw", conv_w[0].rearrange("k (i q) -> (k i) q", q=P)), ("convb", rows(conv_b[0])),
                     ("ba", gate_a_b[0].rearrange("d (i q) -> (d i) q", q=P)),
                     ("bx", gate_x_b[0].rearrange("d (i q) -> (d i) q", q=P)),
                     ("lam", lam[0].rearrange("d (i q) -> (d i) q", q=P)), ("psc", rows(pool_scale[0]))]
            for name, src in prows:
                sp.dma_start(prow[PV[name][0]:PV[name][1], :], src).then_inc(s_prow, 16)
            xv = x[0].rearrange("(t p) d -> p t d", p=P)
            cv = ctx[0].rearrange("(t p) d -> p t d", p=P)
            mv = mod_w[0].rearrange("(k p) n -> p k n", p=P)

            def load_mod(n):
                if 2 <= n < 2 * MCH + 2:
                    sp.wait_ge(s_modu, n - 1)
                if n >= 2 * MCH + 2:
                    sp.wait_ge(s_modv, n - 1 - 2 * MCH)
                a = MORD[n // MCH] * D + n % MCH * 256
                sp.dma_start(mring[:, n % 2], mv[:, :, a:a + 256]).then_inc(s_mod[n % 2], 16)

            load_mod(0)
            load_mod(1)
            sp.dma_start(ctxt[:], cv).then_inc(s_x, 16)
            sp.dma_start(xt[:, 0:4], xv[:, 0:4]).then_inc(s_x, 16)
            sp.dma_start(xt[:, 4:8], xv[:, 4:8]).then_inc(s_x, 16)
            for n in range(2, 2 * MCH):
                load_mod(n)
            wv = w_in[0].rearrange("(k p) n -> p k n", p=P)

            def load_win(n):
                if n >= 3:
                    sp.wait_ge(s_z, UNIT[(COLT[n - 3], 1)] + 1)
                a = OFF[COLT[n][0]] + COLT[n][1] * P
                sp.dma_start(wring[:, n % 3], wv[:, :, a:a + P]).then_inc(s_win[n % 3], 16)

            for n in range(3):
                load_win(n)
            sp.wait_ge(s_bd0, 3)
            for d in range(2):
                for g, w in enumerate((gate_a_w, gate_x_w)):
                    for h in range(2):
                        sp.dma_start(bdg[64 * h:64 * h + 64, 2 * d + g, :, 64 * h:64 * h + 64],
                                     w[0, d].rearrange("(i h) a b -> h a i b", h=2)[h]).then_inc(s_bd, 16)
            for h in range(2):
                sp.dma_start(wfb[64 * h:64 * h + 64, :, 64 * h:64 * h + 64],
                             fourier_w[0].rearrange("(m h) a b -> h a m b", h=2)[h]).then_inc(s_bd, 16)
                sp.dma_start(wpb[64 * h:64 * h + 64, :, 64 * h:64 * h + 64],
                             pool_w[0].rearrange("(m h) a b -> h a m b", h=2)[h]).then_inc(s_bd, 16)
            sp.dma_start(rw[:, :, 0:NG], rg_w[0].rearrange("(k p) n -> p k n", p=P)).then_inc(s_rw, 16)
            sp.dma_start(rw[:, :, NG:], re_w[0].rearrange("(k p) n -> p k n", p=P)).then_inc(s_rw, 16)
            sp.dma_start(rb[:, 0:NG], rg_b.partition_broadcast(P).rearrange("p a n -> p (a n)")).then_inc(s_rw, 16)
            sp.dma_start(rb[:, NG:], re_b.partition_broadcast(P).rearrange("p a n -> p (a n)")).then_inc(s_rw, 16)
            sp.dma_start(g2[:], mod_b[0:1, 2 * D:3 * D].partition_broadcast(P).rearrange("p a n -> p (a n)"))\
                .then_inc(s_gb2, 16)
            sp.wait_ge(s_zero, 1)
            for r in range(NE, MAXT):
                sp.dma_start(y_d[r], g5[:]).then_inc(s_zero_d, 16)
            mod_next = 2 * MCH
            everywhere = lambda a: a.partition_broadcast(P).rearrange("p a n -> p (a n)")
            for n in range(3, len(COLT)):
                load_win(n)
                for _ in range(2):
                    if mod_next < NMC - 2:
                        load_mod(mod_next)
                        mod_next += 1
                if n == 5:
                    sp.wait_ge(s_zero_d, 16 * (MAXT - NE))
                    sp.dma_start(g5[:], everywhere(mod_b[0:1, 5 * D:6 * D])).then_inc(s_gb5, 16)
            sp.dma_start(shr[:], everywhere(mod_b[0:1, 3 * D:4 * D])).then_inc(s_gb3, 16)
            sp.dma_start(scr[:], everywhere(mod_b[0:1, 4 * D:5 * D])).then_inc(s_gb4, 16)
            load_mod(NMC - 2)
            load_mod(NMC - 1)
            sp.wait_ge(s_z, len(UNITS))
            for k in range(NT):
                if k >= 3:
                    sp.wait_ge(s_dftu, k - 2)
                sp.dma_start(dring[:, k % 3], dft[k * P:(k + 1) * P, :]).then_inc(s_dft[k % 3], 16)
                if k == 2:
                    sp.wait_ge(s_modv, 4 * MCH)
                    sp.dma_start(gff[:], everywhere(norm_ffn_g[0:1])).then_inc(s_gff, 16)
            for half in range(2):
                sp.dma_start(wout_sb[:, 4 * half:4 * half + 4],
                             w_out[0].rearrange("(k p) n -> p k n", p=P)[:, 4 * half:4 * half + 4]).then_inc(s_wout, 16)
            sp.wait_ge(s_y, NI)
            for t in range(NX):
                sp.dma_start(xr[t][:], xv[:, t]).then_inc(s_xr[t], 16)
            x1v = x1_d.rearrange("(t p) d -> p t d", p=P)
            xnv = xn_d.rearrange("(t p) d -> p t d", p=P)
            for t in range(NT):
                sp.wait_ge(s_x1, t + 1)
                sp.dma_start(x1v[:, t], xr[t % NX][:]).then_inc(s_x1d[t % NX], 16)
                sp.wait_ge(s_xn, t + 1)
                sp.dma_start(xnv[:, t], xs[t % 2][:]).then_inc(s_xnd[t % 2], 16)
                if t + NX < NT:
                    sp.wait_ge(s_x1d[t % NX], 16 * (t // NX + 1))
                    sp.dma_start(xr[t % NX][:], xv[:, t + NX]).then_inc(s_xr[t % NX], 16)

            def load_gate_up(e, j):
                for g, w in enumerate((wg, wu)):
                    a = w[0, e] if isinstance(e, int) else w[0, e].rearrange("a k n -> (a k) n")
                    sp.dma_start(raw[:, j, g * D:(g + 1) * D].rearrange("p (k n) -> p k n", n=HALF),
                                 a[2 * P * j:2 * P * (j + 1), :].rearrange("(k p) n -> p k n", p=P)).then_inc(s_rgu[j], 16)

            def load_down(e, j):
                a = wd[0, e] if isinstance(e, int) else wd[0, e].rearrange("a h n -> (a h) n")
                sp.dma_start(raw[:, j, 2 * D:], a[j * P:(j + 1) * P, :]).then_inc(s_rdn[j], 16)

            sp.wait_ge(s_lg, NT)
            for n in range(NX):
                sp.wait_ge(s_x1d[n], 16 * len(range(n, NT, NX)))
            for n in range(2):
                sp.wait_ge(s_xnd[n], 16 * (NT // 2))
            sp.wait_ge(s_mrow, 8)
            for j in range(KE):
                load_gate_up(0, j)
            for j in range(KE):
                load_down(0, j)
            with sp.Fori(1, NE) as e:
                for j in range(KE):
                    sp.wait_ge(s_logu[j], e)
                    load_gate_up(bass.ds(e, 1), j)
                for j in range(KE):
                    sp.wait_ge(s_lod[j], e)
                    load_down(bass.ds(e, 1), j)
            sp.wait_ge(s_end, 1)
            ov = out[0].rearrange("(t p) d -> p t d", p=P)
            for t in range(NF):
                sp.dma_start(fx[t][:], x1v[:, t]).then_inc(s_fl[t], 16)
            sp.dma_start(gfin[:], final_g.partition_broadcast(P)).then_inc(s_gf, 16)
            for t in range(NT):
                n = t % NF
                sp.wait_ge(s_fo, t + 1)
                sp.dma_start(ov[:, t], fb[n][:]).then_inc(s_out[n], 16)
                if t + NF < NT:
                    sp.dma_start(fx[n][:], x1v[:, t + NF]).then_inc(s_fl[n], 16)
            for n in range(NF):
                sp.wait_ge(s_out[n], 16 * (NT // NF))

        @block.gpsimd
        def _(pool):
            pool.memset(g5[:], 0.0).then_inc(s_zero, 1)
            pool.memset(held[:], 0.0).then_inc(s_held, 1)
            pool.memset(zpad[:], 0.0).then_inc(s_zp, 1)
            pool.memset(bdg[:], 0.0).then_inc(s_bd0, 1)
            pool.memset(wfb[:], 0.0).then_inc(s_bd0, 1)
            pool.memset(wpb[:], 0.0).then_inc(s_bd0, 1)
            pool.wait_ge(s_cst, 16)
            pool.tensor_copy(tri_b[:], K("tri")).then_inc(s_tri, 1)
            pool.tensor_copy(ones_b[:], ones).then_inc(s_tri, 1)

            chain = [0]

            def link(ins):
                chain[0] += 1
                ins.then_inc(s_pc, 1)
                pool.wait_ge(s_pc, chain[0])

            def add(o_, a_, b_):
                return pool.tensor_tensor(o_, a_, b_, ALU.add)

            for m in range(2):
                z = yT[:, 4 + m, :].rearrange("p (r c) -> p r c", c=COLS)
                pool.wait_ge(s_zu, UNIT[(("p", m), 1)] + 1)
                if m == 1:
                    pool.wait_ge(s_pd, 1)
                if m == 0:
                    pool.wait_ge(s_tpe, 3 * KD)
                link(pool.memset(P0[:, 0:GRID_PAD, :], 0.0))
                link(pool.memset(P0[:, GRID_PAD + ROWS:, :], 0.0))
                link(pool.tensor_copy(P0[:, GRID_PAD:GRID_PAD + ROWS, :], z))
                link(add(P1[:, 0:31, :], P0[:, 0:31, :], P0[:, 1:32, :]))
                if m == 1:
                    link(add(P0[:, 0:29, :], P1[:, 0:29, :], P1[:, 2:31, :]))
                    link(add(P1[:, 0:25, :], P0[:, 0:25, :], P0[:, 4:29, :]))
                a, b, c_ = ((7, 6, 8), (4, 0, 8))[m]
                link(pool.memset(C0[:, :, 0:8], 0.0))
                link(pool.memset(C0[:, :, 8 + COLS:], 0.0))
                link(pool.tensor_copy(C0[0:64, :, 8:8 + COLS], P1[0:64, a:a + ROWS, :]))
                link(add(C0[64:128, :, 8:8 + COLS], P1[64:128, b:b + ROWS, :], P1[64:128, c_:c_ + ROWS, :]))
                link(add(C1[:, :, 0:79], C0[:, :, 0:79], C0[:, :, 1:80]))
                if m == 1:
                    link(add(C0[:, :, 0:77], C1[:, :, 0:77], C1[:, :, 2:79]))
                    link(add(C1[:, :, 0:73], C0[:, :, 0:73], C0[:, :, 4:77]))
                icr = K("icr")[:, m * ROWS:(m + 1) * ROWS].unsqueeze(2)
                icc = K("icc")[:, m * COLS:(m + 1) * COLS].unsqueeze(1)
                link(add(C0[64:128, :, 0:COLS], C1[64:128, :, b:b + COLS], C1[64:128, :, c_:c_ + COLS]))
                link(pool.tensor_tensor(C0[64:128, :, 0:COLS], C0[64:128, :, 0:COLS],
                                        icr[64:128].to_broadcast([64, ROWS, COLS]), ALU.mult))
                link(pool.tensor_tensor(C0[0:64, :, 0:COLS], C1[0:64, :, a:a + COLS],
                                        icr[0:64].to_broadcast([64, ROWS, COLS]), ALU.mult))
                link(pool.tensor_tensor(C0[:, :, 0:COLS], C0[:, :, 0:COLS], icc.to_broadcast([P, ROWS, COLS]),
                                        ALU.mult))
                pool.tensor_tensor(z, C0[:, :, 0:COLS], z, ALU.subtract).then_inc(s_pd, 1)

            def hold(n):
                pool.wait_ge(s_held, n + 1)
                pool.tensor_tensor(held[:], held[:], held[:], ALU.mult).then_inc(s_held, 1)

            def split_down(e1, j):
                pool.wait_ge(s_hdn, 4 * e1 + j + 1)
                pool.tensor_tensor(WP[:, j, 1, 2 * D:], raw[:, j, 2 * D:], WP[:, j, 0, 2 * D:].bitcast(F32),
                                   ALU.subtract).then_inc(s_lod[j], 1)

            def gather(q):
                pool.wait_ge(s_ids, q + 1)
                if not isinstance(q, int):
                    hold(q - 2)
                pool.indirect_dma_start(out=xg[:], out_offset=None, in_=xn_d,
                                        in_offset=bass.IndirectOffsetOnAxis(ap=idg[:, 0:1], axis=0)).then_inc(s_xg, 16)

            for n in range(2):
                pool.wait_ge(s_xnd[n], 16 * (NT // 2))
            gather(0)
            pool.wait_ge(s_xgt, 2)
            gather(1)
            for j in range(KE):
                split_down(0, j)
            W = pool.value_load(tab[0:1, 3, 0:1], min_val=NE, max_val=MAXT)
            with pool.Fori(0, MAXT // 2) as it:
                with pool.If(2 * it < W):
                    for par in range(2):
                        s = 2 * it + par
                        L = pool.value_load(tab[0:1, 2, bass.ds(s, 1)], min_val=0, max_val=1)
                        E1 = pool.value_load(tab[0:1, 0, bass.ds(s + 1, 1)], min_val=0, max_val=NE - 1)
                        pool.wait_ge(s_xgt, 2 * s + 4)
                        gather(s + 2)
                        with pool.If(L > 0):
                            for j in range(KE):
                                split_down(E1, j)
            Wl = pool.value_load(tab[0:1, 3, 1:2], min_val=NE, max_val=MAXT)
            for n in range(2):
                pool.wait_ge(s_ys[n], 8 * Wl + 16)
            pool.wait_ge(s_xg, 16 * Wl + 32)
            hold(Wl)
            pool.memset(stat[:, 63:64], 0.0).then_inc(s_end, 1)
            y_rows = y_d.rearrange("s p d -> (s p) d")
            for t in range(NT):
                n = t % NF
                if t >= NF:
                    pool.wait_ge(s_out[n], 16 * (t // NF))
                for a, buf in enumerate((fa, fb)):
                    pool.indirect_dma_start(out=buf[n][:], out_offset=None, in_=y_rows,
                                            in_offset=bass.IndirectOffsetOnAxis(ap=pos[:, a, t:t + 1], axis=0))\
                        .then_inc(s_fg[n], 16)

        @block.tensor
        def _(pe):
            pe.wait_ge(s_cst, 16)
            pe.wait_ge(s_prow, 16 * len(PV))
            pe.transpose(bank[7][:, 0:NPV], prow[0:NPV, :], ident[0:NPV, 0:NPV]).then_inc(s_pvp, 1)

            pe.wait_ge(s_silu, 1)
            for n in range(2 * MCH):
                pe.wait_ge(s_mod[n % 2], 16 * (n // 2 + 1))
                for h in range(2):
                    for k in range(KD):
                        mm = pe.matmul(bank[6][:, 2 * (2 * n + h):2 * (2 * n + h) + 2],
                                       mring[:, n % 2, k, h * P:(h + 1) * P], silu_c[:, :, k],
                                       start=k == 0, stop=k == KD - 1)
                mm.then_inc(s_modu, 1)

            n = 0
            for part in ("c", 0, 1):
                for k in range(KD):
                    cnt = NC_ if part == "c" else 4
                    if k == 0:
                        pe.wait_ge(s_xs, {"c": 2, 0: 6, 1: 10}[part])
                    if n >= 4:
                        m_ = n - 4
                        pe.wait_ge(s_tpa if m_ % 2 == 0 else s_tpv, m_ // 2 + 1)
                    for t in range(cnt):
                        src = ctxt[:, t] if part == "c" else xt[:, 4 * part + t]
                        mm = pe.transpose(bank[n % 4][:, t * P:(t + 1) * P], src[:, k * P:(k + 1) * P], ident)
                    n += 1
                    mm.then_inc(s_tpe, 1)

            pe.wait_ge(s_bd, 16 * 12)
            pe.wait_ge(s_pv, 1)
            for m in range(2):
                for q, name in enumerate(("cos64", "sin64")):
                    mm = pe.matmul(bank[7][:, (2 * m + q) * P:(2 * m + q + 1) * P], K(name), wfb[:, m, :],
                                   start=True, stop=True)
            mm.then_inc(s_csw, 1)

            pe.wait_ge(s_tpa, 12)
            pe.wait_ge(s_tpv, 12)

            def z_tile(n):
                ct = COLT[n]
                pe.wait_ge(s_win[n % 3], 16 * (n // 3 + 1))
                for part in ((("c",) if ct[0] == "x" else ()) + (0, 1)):
                    u = UNIT[(ct, part)]
                    if u >= 4:
                        pe.wait_ge(s_zu, u - 3)
                    o_ = bank[u % 4][:, 0:CTX] if part == "c" else bank[u % 4][:]
                    for k in range(KD):
                        src = hTc[:, k, :] if part == "c" else hT[:, k, part * HALF:(part + 1) * HALF]
                        mm = pe.matmul(o_, wring[:, n % 3, k, :], src, start=k == 0, stop=k == KD - 1)
                    mm.then_inc(s_z, 1)
                    last = mm
                return last

            def gates(i):
                pe.wait_ge(s_conv, i + 1)
                for d in range(2):
                    for g in range(2):
                        for q, (a, w) in enumerate(GPARTS):
                            n = GUNITS.index((i, d, g, q))
                            if n >= 3:
                                pe.wait_ge(s_gu, n - 2)
                            pe.matmul(bank[4 + n % 3][:, 0:w], bdg[:, 2 * d + g, i, :], U[i % 2][:, a:a + w],
                                      start=True, stop=True).then_inc(s_g, 1)

            def mod_product(m):
                i = MORD.index(m) - 2
                pe.wait_ge(s_macc, i + 1)
                for h in range(2):
                    if i + h:
                        pe.wait_ge(s_mrow, 2 * i + h)
                    pe.matmul(bank[7][:], ones, macc[:, h * HALF:(h + 1) * HALF], start=True,
                              stop=True).then_inc(s_m25, 1)

            MOD_AFTER = {5: 2, 7: 5, 9: 3, 11: 4}
            pe.wait_ge(s_cswc, 1)
            for n, ct in enumerate(COLT):
                z_tile(n)
                if ct in GATES_AFTER:
                    gates(GATES_AFTER[ct])
                if n in MOD_AFTER:
                    mod_product(MOD_AFTER[n])

            NU = len(UNITS)
            pe.wait_ge(s_zu, NU)
            pe.wait_ge(s_pd, 2)
            for i in range(NT):
                u = NU + i
                pe.wait_ge(s_zu, u - 3)
                for m, zf in enumerate((zf0, zf1)):
                    mm = pe.matmul(bank[u % 4][:, m * 256:(m + 1) * 256], zf[:, i * P:(i + 1) * P], csw[:, m, :],
                                   start=True, stop=True)
                mm.then_inc(s_z, 1)

            pe.wait_ge(s_mrow, 8)
            pe.wait_ge(s_gu, len(GUNITS))
            for m in range(2):
                for h in range(2):
                    q = 2 * m + h
                    if q >= 2:
                        pe.wait_ge(s_py, q - 1)
                    pe.matmul(bank[6 + q % 2][:], wpb[:, m, :], yT[:, 4 + m, h * HALF:(h + 1) * HALF], start=True,
                              stop=True).then_inc(s_pm, 1)

            pe.wait_ge(s_zu, NU + NT)
            for k in range(NT):
                pe.wait_ge(s_dft[k % 3], 16 * (k // 3 + 1))
                for m in range(2):
                    pe.matmul(bank[4 + m][:, 0:1], Vf[:, k, m, 0:P], K("alt"), start=k == 0, stop=k == NT - 1)
                    pe.matmul(bank[m][:], Vf[:, k, m, 0:P], dring[:, k % 3, 0:HALF], start=k == 0, stop=k == NT - 1)
                    mm = pe.matmul(bank[2 + m][:], Vf[:, k, m, P:2 * P], dring[:, k % 3, HALF:], start=k == 0,
                                   stop=k == NT - 1)
                mm.then_inc(s_dftu, 1)

            pe.wait_ge(s_wout, 32)
            pe.wait_ge(s_y, NI)
            pe.wait_ge(s_py, 4)
            pe.wait_ge(s_fy, 2)

            def out_proj(t):
                for h in range(2):
                    u = 2 * t + h
                    if u >= 4:
                        pe.wait_ge(s_mixu, u - 3)
                    for k in range(KD):
                        mm = pe.matmul(bank[u % 4][:], yT[:, k, t * P:(t + 1) * P],
                                       wout_sb[:, k, h * HALF:(h + 1) * HALF], start=k == 0, stop=k == KD - 1)
                    mm.then_inc(s_mix, 1)

            def turn(t):
                pe.wait_ge(s_xn, t + 1)
                if t >= 1:
                    pe.wait_ge(s_h2, t)
                for k in range(KD):
                    mm = pe.transpose(bank[4 + k // 4][:, (k % 4) * P:(k % 4 + 1) * P], xs[t % 2][:, k * P:(k + 1) * P],
                                      ident)
                mm.then_inc(s_t2, 1)

            def logits(t):
                pe.wait_ge(s_h2, t + 1)
                if t >= 1:
                    pe.wait_ge(s_lg, t)
                for k in range(KD):
                    mm = pe.matmul(bank[6][:, 0:NG + NE], h2[:, k, :], rw[:, k, :], start=k == 0, stop=k == KD - 1)
                mm.then_inc(s_lgp, 1)

            for t in range(NT + 2):
                if t < NT:
                    out_proj(t)
                if 1 <= t <= NT:
                    turn(t - 1)
                if t >= 2:
                    logits(t - 2)

            pe.wait_ge(s_tri, 2)
            pe.wait_ge(s_mk, 1)
            mb = oh[:, 0, :]
            for i in range(NT):
                for j in range(i + 1):
                    pe.matmul(bank[4][:, NE * i:NE * (i + 1)], (tri_b if j == i else ones_b)[:],
                              mb[:, NE * j:NE * (j + 1)], start=j == 0, stop=j == i)
            for j in range(NT):
                mm = pe.matmul(bank[5][:, 0:NE], ones_b[:], mb[:, NE * j:NE * (j + 1)], start=j == 0,
                               stop=j == NT - 1)
            mm.then_inc(s_rk, 1)

            def slot_numbers(q, E1, first=False):
                pe.wait_ge(s_oh, q + 1)
                if not first or q:
                    pe.wait_ge(s_idf, q)
                for i in range(NT):
                    mm = pe.matmul(bank[2][:, 0:NFLD], oh[:, i, :],
                                   RV[:, E1, i, :] if isinstance(E1, int) else
                                   RV[:, bass.ds(E1, 1), i, :].rearrange("p a n -> p (a n)"),
                                   start=i == 0, stop=i == NT - 1)
                mm.then_inc(s_idx, 1)

            def turn_rows(q, r):
                if r == 0:
                    pe.wait_ge(s_xg, 16 * q + 16)
                for k in range(4):
                    kk = 4 * r + k
                    mm = pe.transpose(bank[(3, 6)[r]][:, k * P:(k + 1) * P], xg[:, kk * P:(kk + 1) * P], ident)
                mm.then_inc(s_xgt, 1)

            def gate_up(E, par, j):
                pe.wait_ge(s_logu[j], E + 1)
                order = [(g, kk) for kk in range(2) for g in range(2)] if j < KE - 1 else \
                    [(g, kk) for g in range(2) for kk in range(2)]
                for g, kk in order:
                    k, a = 2 * j + kk, g * D + kk * HALF
                    w_hi, w_lo = WP[:, j, 0, a:a + HALF], WP[:, j, 1, a:a + HALF]
                    x_hi, x_lo = xp[:, par, 0, k, :], xp[:, par, 1, k, :]
                    pe.matmul(bank[g][:], x_hi, w_hi, start=k == 0, stop=False)
                    pe.matmul(bank[g][:], x_hi, w_lo, start=False, stop=False)
                    mm = pe.matmul(bank[g][:], x_lo, w_hi, start=False, stop=k == KD - 1)
                    if g == 0 and k == KD - 1:
                        mm.then_inc(s_gate, 1)
                mm.then_inc(s_gud, 1)

            def turn_hidden(s, h):
                pe.wait_ge(s_hid, 2 * s + h + 1)
                if h:
                    pe.wait_ge(s_idf, s + 3)
                for j in range(2 * h, 2 * h + 2):
                    mm = pe.transpose(bank[(7, 2)[h]][:, j * P:(j + 1) * P], sg[:, j * P:(j + 1) * P], ident)
                mm.then_inc(s_hT, 1)

            def down(s, E, j):
                pe.wait_ge(s_lod[j], E + 1)
                if j % 2 == 0:
                    pe.wait_ge(s_hps, 2 * s + j // 2 + 1)
                if j == 0:
                    pe.wait_ge(s_ye, 2 * s + 2)
                for h in range(2):
                    w_hi = WP[:, j, 0, 2 * D + h * HALF:2 * D + (h + 1) * HALF]
                    w_lo = WP[:, j, 1, 2 * D + h * HALF:2 * D + (h + 1) * HALF]
                    pe.matmul(bank[4 + h][:], hp[:, 0, j, :], w_hi, start=j == 0, stop=False)
                    pe.matmul(bank[4 + h][:], hp[:, 0, j, :], w_lo, start=False, stop=False)
                    mm = pe.matmul(bank[4 + h][:], hp[:, 1, j, :], w_hi, start=False, stop=j == KE - 1)
                mm.then_inc(s_dd, 1)

            slot_numbers(0, 0, first=True)
            pe.wait_ge(s_tab, 1)
            W = pe.value_load(tab[0:1, 3, 0:1], min_val=NE, max_val=MAXT)
            slot_numbers(1, pe.value_load(tab[0:1, 0, 1:2], min_val=0, max_val=NE - 1))
            for r in range(2):
                turn_rows(0, r)
            with pe.Fori(0, MAXT // 2) as it:
                with pe.If(2 * it < W):
                    for par in range(2):
                        s = 2 * it + par
                        E = pe.value_load(tab[0:1, 0, bass.ds(s, 1)], min_val=0, max_val=NE - 1)
                        E2 = pe.value_load(tab[0:1, 0, bass.ds(s + 2, 1)], min_val=0, max_val=NE - 1)
                        pe.wait_ge(s_xgr, 2 * s + 2)
                        gate_up(E, par, 0)
                        gate_up(E, par, 1)
                        slot_numbers(s + 2, E2)
                        gate_up(E, par, 2)
                        gate_up(E, par, 3)
                        turn_rows(s + 1, 0)
                        turn_rows(s + 1, 1)
                        turn_hidden(s, 0)
                        turn_hidden(s, 1)
                        for j in range(KE):
                            down(s, E, j)

        @block.scalar
        def _(act):
            A_ = act.activation
            act.wait_ge(s_pv, 1)
            A_(silu_c[:].rearrange("p a k -> p (a k)"), pv[:, 0:2 * KD], ACT.Tanh, scale=0.5).then_inc(s_sil, 1)
            act.wait_ge(s_lam, 1)
            A_(lamw[:, 1], lamw[:, 0], ACT.Exp, scale=-1.0).then_inc(s_lame, 1)
            act.wait_ge(s_x, 48)
            for t in range(NT + NC_):
                src = ctxt[:, t] if t < NC_ else xt[:, t - NC_]
                if t >= 2:
                    act.wait_ge(s_ss, t - 1)
                A_(AA[t % 2][:, 0:D], src, ACT.Square, accum_out=stat[:, t:t + 1]).then_inc(s_ss, 1)
            act.wait_ge(s_ms, 1)
            A_(stat[:, 0:10], stat[:, 0:10], ACT.Sqrt).then_inc(s_sq, 1)

            def h_unit(n):
                part = n // KD
                k = n % KD
                g = 1 if part == 0 else 0
                dst = hTc[:, k, :] if part == 0 else hT[:, k, (part - 1) * HALF:part * HALF]
                return k, g, dst, bank[n % 4][:, 0:CTX if part == 0 else HALF]

            act.wait_ge(s_scsh, 1)
            for n in range(0, 3 * KD, 2):
                k, g, dst, src = h_unit(n)
                act.wait_ge(s_tpe, n + 1)
                A_(dst, src, ACT.Identity, scale=sc_mix[:, k, g:g + 1], bias=sh_mix[:, k, g:g + 1]).then_inc(s_tpa, 1)
            act.wait_ge(s_csw, 1)
            A_(csw[:].rearrange("p m n -> p (m n)"), bank[7][:], ACT.Copy).then_inc(s_cswc, 1)

            def take_x(i):
                if i == 0:
                    act.wait_ge(s_zp, 1)
                else:
                    act.wait_ge(s_conv, i)
                if i >= 2:
                    act.wait_ge(s_y, i - 1)
                for part in ("c", 0, 1):
                    u = UNIT[(("x", i), part)]
                    act.wait_ge(s_z, u + 1)
                    w = CTX if part == "c" else HALF
                    zo = 2 if part == "c" else CTX + 5 + part * HALF
                    uo = 0 if part == "c" else CTX + part * HALF
                    A_(zpad[:, zo:zo + w], bank[u % 4][:, 0:w], ACT.Copy)
                    A_(U[i % 2][:, uo:uo + w], bank[u % 4][:, 0:w], ACT.Identity, scale=V("convw", 2 * NI + i),
                       bias=V("convb", i)).then_inc(s_zu, 1)

            def take_g(i):
                if i >= 2:
                    act.wait_ge(s_y, i - 1)
                if i >= 1:
                    act.wait_ge(s_gel, i)
                for part in (0, 1):
                    u = UNIT[(("g", i), part)]
                    act.wait_ge(s_z, u + 1)
                    A_(gz[i % 2][:, part * HALF:(part + 1) * HALF], bank[u % 4][:], ACT.Copy)
                    A_(gt[:, part * HALF:(part + 1) * HALF], bank[u % 4][:], ACT.Square).then_inc(s_zu, 1)

            def gelu_tanh(i):
                act.wait_ge(s_gp, i + 1)
                A_(gt[:], gt[:], ACT.Tanh, scale=GELU_C).then_inc(s_gth, 1)

            def take_p(m):
                for part in (0, 1):
                    u = UNIT[(("p", m), part)]
                    act.wait_ge(s_z, u + 1)
                    A_(yT[:, 4 + m, part * HALF:(part + 1) * HALF], bank[u % 4][:], ACT.Copy).then_inc(s_zu, 1)

            def take_f(m):
                if m == 0:
                    act.wait_ge(s_m25, 8)
                else:
                    act.wait_ge(s_conv, NI)
                for part in (0, 1):
                    u = UNIT[(("f", m), part)]
                    act.wait_ge(s_z, u + 1)
                    A_((zf0, zf1)[m][:, part * HALF:(part + 1) * HALF], bank[u % 4][:], ACT.Copy).then_inc(s_zu, 1)

            def rec_gates(i):
                if i >= 1:
                    act.wait_ge(s_y, i)
                else:
                    act.wait_ge(s_lamc, 1)
                for d in range(2):
                    for g in range(2):
                        for q, (a, w) in enumerate(GPARTS):
                            n = GUNITS.index((i, d, g, q))
                            act.wait_ge(s_g, n + 1)
                            A_((RH, IH)[g][d][:, a:a + w], bank[4 + n % 3][:, 0:w], ACT.Tanh, scale=0.5,
                               bias=hb_[:, 2 * d + g, i:i + 1]).then_inc(s_gu, 1)
                    act.wait_ge(s_gu, GUNITS.index((i, d, 1, 2)) + 1)
                    A_(AA[d][:], RH[d][:], ACT.Exp, scale=lamw[:, 5, d * NI + i:d * NI + i + 1],
                       bias=lamw[:, 5, d * NI + i:d * NI + i + 1])
                    A_(RH[d][:], RH[d][:], ACT.Tanh, scale=lamw[:, 4, d * NI + i:d * NI + i + 1],
                       bias=lamw[:, 4, d * NI + i:d * NI + i + 1]).then_inc(s_ra, 1)

            def rec_root(i):
                for d in range(2):
                    act.wait_ge(s_rm, 2 * i + d + 1)
                    A_(RH[d][:], RH[d][:], ACT.Sqrt, scale=0.25).then_inc(s_rr, 1)

            take_x(0)
            take_g(0)
            gelu_tanh(0)
            take_p(0)
            rec_gates(0)
            take_x(1)
            rec_root(0)
            take_g(1)
            gelu_tanh(1)
            take_p(1)
            rec_gates(1)
            take_x(2)
            rec_root(1)
            take_g(2)
            gelu_tanh(2)
            rec_gates(2)
            take_x(3)
            rec_root(2)
            take_g(3)
            gelu_tanh(3)
            rec_gates(3)
            rec_root(3)
            take_f(0)
            take_f(1)
            NU = len(UNITS)
            for i in range(NT):
                act.wait_ge(s_z, NU + i + 1)
                A_(Vf[:, i].rearrange("p m n -> p (m n)"), bank[(NU + i) % 4][:], ACT.Copy).then_inc(s_zu, 1)
            for q in range(4):
                m, h = q // 2, q % 2
                act.wait_ge(s_pm, q + 1)
                A_(yT[:, 4 + m, h * HALF:(h + 1) * HALF], bank[6 + q % 2][:], ACT.Copy, scale=V("psc", m)).then_inc(s_py, 1)
            act.wait_ge(s_dftu, NT)
            act.wait_ge(s_y, NI)
            for m in range(2):
                A_((gt, Q)[m][:, 0:HALF], bank[m][:], ACT.Copy).then_inc(s_fc, 1)

            for t in range(NT):
                act.wait_ge(s_x1, t + 1)
                A_(xm[t % 2][:], xr[t % NX][:], ACT.Square, accum_out=stat[:, 10 + t:11 + t]).then_inc(s_ss2, 1)
                act.wait_ge(s_ms2, t + 1)
                A_(stat[:, 18 + t:19 + t], stat[:, 10 + t:11 + t], ACT.Sqrt).then_inc(s_rt2, 1)
                act.wait_ge(s_t2, t + 1)
                if t >= 1:
                    act.wait_ge(s_lgp, t)
                for h in range(2):
                    ins = A_(h2[:, 4 * h:4 * h + 4, :], bank[4 + h][:].rearrange("p (k n) -> p k n", n=P), ACT.Copy)
                ins.then_inc(s_h2, 1)

            act.wait_ge(s_e1, 1)
            A_(R_["d"], R_["d"], ACT.Exp).then_inc(s_e2, 1)
            act.wait_ge(s_e1, 2)
            A_(R_["ex"], R_["ex"], ACT.Exp).then_inc(s_e2, 1)

            def hi_gate_up(e1, j):
                act.wait_ge(s_rgu[j], 32 * e1 + 32)
                A_(WP[:, j, 0, 0:2 * D], raw[:, j, 0:2 * D], ACT.Copy).then_inc(s_hgu, 1)

            def hi_down(e1, j):
                act.wait_ge(s_rdn[j], 16 * e1 + 16)
                A_(WP[:, j, 0, 2 * D:], raw[:, j, 2 * D:], ACT.Copy).then_inc(s_hdn, 1)

            def hi_rows(q, p2, r):
                act.wait_ge(s_xgt, 2 * q + r + 1)
                A_(xp[:, p2, 0, 4 * r:4 * r + 4, :], bank[(3, 6)[r]][:].rearrange("p (k n) -> p k n", n=P),
                   ACT.Copy).then_inc(s_xgh, 1)

            for n in range(2):
                act.sem_inc(s_ys[n], 16)
            for j in range(KE):
                hi_gate_up(0, j)
            for r in range(2):
                hi_rows(0, 0, r)
            for j in range(KE):
                hi_down(0, j)
            act.wait_ge(s_tab, 1)
            W = act.value_load(tab[0:1, 3, 0:1], min_val=NE, max_val=MAXT)
            with act.Fori(0, MAXT // 2) as it:
                with act.If(2 * it < W):
                    for par in range(2):
                        s = 2 * it + par
                        L = act.value_load(tab[0:1, 2, bass.ds(s, 1)], min_val=0, max_val=1)
                        E1 = act.value_load(tab[0:1, 0, bass.ds(s + 1, 1)], min_val=0, max_val=NE - 1)
                        with act.If(L > 0):
                            for j in range(KE - 1):
                                act.wait_ge(s_gud, 4 * s + j + 1)
                                hi_gate_up(E1, j)
                        act.wait_ge(s_gate, s + 1)
                        A_(sg[:], bank[0][:], ACT.Silu).then_inc(s_sg, 1)
                        for h in range(2):
                            act.wait_ge(s_hT, 2 * s + h + 1)
                            A_(hp[:, 0, 2 * h:2 * h + 2, :],
                               bank[(7, 2)[h]][:, h * 2 * P:(h + 1) * 2 * P].rearrange("p (k n) -> p k n", n=P),
                               ACT.Copy).then_inc(s_hfr, 1)
                        for r in range(2):
                            hi_rows(s + 1, 1 - par, r)
                        with act.If(L > 0):
                            act.wait_ge(s_gud, 4 * s + 4)
                            hi_gate_up(E1, KE - 1)
                            for j in range(KE):
                                act.wait_ge(s_dd, 4 * s + j + 1)
                                hi_down(E1, j)
                        act.wait_ge(s_ye, 2 * s + 4)
                        act.dma_start(y_d[bass.ds(s, 1)].rearrange("a p d -> (a p) d"),
                                      ysc[:, par, :]).then_inc(s_ys[par], 16)

            for t in range(NT):
                act.wait_ge(s_fx1, t + 1)
                if t:
                    act.wait_ge(s_fs, t)
                A_(fj[:], fx[t % NF][:], ACT.Square, accum_out=stat[:, 28 + t:29 + t]).then_inc(s_fs, 1)
                act.wait_ge(s_fm, t + 1)
                A_(stat[:, 36 + t:37 + t], stat[:, 28 + t:29 + t], ACT.Sqrt).then_inc(s_fr, 1)

        @block.vector
        def _(dve):
            chain = [0]

            def link(ins):
                chain[0] += 1
                ins.then_inc(s_dv, 1)
                dve.wait_ge(s_dv, chain[0])

            tt, ts, stt = dve.tensor_tensor, dve.tensor_scalar, dve.scalar_tensor_tensor
            dve.wait_ge(s_pvp, 1)
            link(dve.tensor_copy(pv[:], bank[7][:, 0:NPV]))
            lamv = V("lam")
            link(ts(lamw[:, 2], lamv, -1.0, None, ALU.mult))
            link(tt(lamw[:, 0], lamw[:, 2], lamv, ALU.max))
            ts(lamw[:, 2], lamw[:, 2], 0.0, None, ALU.max).then_inc(s_lam, 1)
            for d in range(2):
                ts(hb_[:, 2 * d], V("ba")[:, d * NI:(d + 1) * NI], 0.5, None, ALU.mult)
                ts(hb_[:, 2 * d + 1], V("bx")[:, d * NI:(d + 1) * NI], 0.5, None, ALU.mult)
            link(dve.memset(stat[:], 0.0))
            dve.memset(stat[:, 62:63], 0.0).then_inc(s_pv, 1)
            dve.wait_ge(s_sil, 1)
            sc_ = silu_c[:].rearrange("p a k -> p (a k)")
            link(stt(out=sc_, in0=sc_, scalar=1.0, in1=pv[:, 0:2 * KD], op0=ALU.add, op1=ALU.mult))
            ts(sc_, sc_, 0.5, None, ALU.mult).then_inc(s_silu, 1)
            dve.wait_ge(s_lame, 1)
            e_, s2_, p_, s_ = lamw[:, 1], lamw[:, 3], lamw[:, 4], lamw[:, 5]
            link(ts(s_, e_, 2.0, None, ALU.add))
            link(dve.reciprocal(s_, s_))
            link(tt(s_, s_, e_, ALU.mult))
            link(tt(s2_, s_, s_, ALU.mult))
            link(dve.memset(p_, 0.0))
            for n in range(19, 1, -2):
                link(stt(out=p_, in0=p_, scalar=1.0 / n, in1=s2_, op0=ALU.add, op1=ALU.mult))
            link(stt(out=p_, in0=p_, scalar=1.0, in1=s_, op0=ALU.add, op1=ALU.mult))
            link(stt(out=p_, in0=p_, scalar=2.0, in1=lamw[:, 2], op0=ALU.mult, op1=ALU.add))
            link(ts(p_, p_, 1e-25, None, ALU.max))
            ts(s_, p_, -4.0, None, ALU.mult)
            ts(p_, p_, 4.0, None, ALU.mult).then_inc(s_lamc, 1)

            dve.wait_ge(s_ss, NT + NC_)
            ts(stat[:, 0:10], stat[:, 0:10], 1.0 / D, EPS, ALU.mult, ALU.add).then_inc(s_ms, 1)
            dve.wait_ge(s_sq, 1)
            link(dve.reciprocal(stat[:, 0:10], stat[:, 0:10]))
            for t in range(NT + NC_):
                src = ctxt[:, t] if t < NC_ else xt[:, t - NC_]
                ts(src, src, stat[:, t:t + 1], None, ALU.mult).then_inc(s_xs, 1)

            dve.wait_ge(s_modu, 2 * MCH)
            m01 = bank[6][:, 0:4 * KD].rearrange("p (j g) -> p j g", g=2)
            mb_ = V("modb").unsqueeze(2)
            tt(sh_mix[:], m01[:, 0:KD], mb_[:, 0:KD].to_broadcast([P, KD, 2]), ALU.add)
            link(tt(sc_mix[:], m01[:, KD:2 * KD], mb_[:, KD:2 * KD].to_broadcast([P, KD, 2]), ALU.add))
            stt(out=sc_mix[:], in0=sc_mix[:], scalar=1.0, in1=V("gmix").unsqueeze(2).to_broadcast([P, KD, 2]),
                op0=ALU.add, op1=ALU.mult).then_inc(s_scsh, 1)
            dve.wait_ge(s_scsh, 1)
            for n in range(1, 3 * KD, 2):
                part, k = n // KD, n % KD
                g = 1 if part == 0 else 0
                dst = hTc[:, k, :] if part == 0 else hT[:, k, (part - 1) * HALF:part * HALF]
                dve.wait_ge(s_tpe, n + 1)
                ts(dst, bank[n % 4][:, 0:CTX if part == 0 else HALF], sc_mix[:, k, g:g + 1], sh_mix[:, k, g:g + 1],
                   ALU.mult, ALU.add).then_inc(s_tpv, 1)

            def conv(i):
                dve.wait_ge(s_zu, UNIT[(("x", i), 1)] + 1)
                for a, b, w in ((0, 0, CTX), (CTX, CTX + 3, SEQ)):
                    u = U[i % 2][:, a:a + w]
                    for tap in (0, 1, 3):
                        ins = stt(out=u, in0=zpad[:, b + tap:b + tap + w], scalar=V("convw", tap * NI + i), in1=u,
                                  op0=ALU.mult, op1=ALU.add)
                        if tap != 3:
                            link(ins)
                ins.then_inc(s_conv, 1)

            def gelu_poly(i):
                dve.wait_ge(s_zu, UNIT[(("g", i), 1)] + 1)
                link(ts(gt[:], gt[:], 0.044715, 1.0, ALU.mult, ALU.add))
                tt(gt[:], gt[:], gz[i % 2][:], ALU.mult).then_inc(s_gp, 1)

            def gelu_end(i):
                dve.wait_ge(s_gth, i + 1)
                stt(out=gz[i % 2][:], in0=gt[:], scalar=1.0, in1=gz[i % 2][:], op0=ALU.add,
                    op1=ALU.mult).then_inc(s_gel, 1)

            def rec_input(i):
                for d in range(2):
                    dve.wait_ge(s_ra, 2 * i + d + 1)
                    stt(out=IH[d][:], in0=IH[d][:], scalar=1.0, in1=U[i % 2][:], op0=ALU.add, op1=ALU.mult)
                    if d:
                        dve.wait_ge(s_rm, 2 * i + 1)
                    link(tt(Q[:], AA[d][:], AA[d][:], ALU.mult))
                    stt(out=RH[d][:], in0=Q[:], scalar=1.0, in1=RH[d][:], op0=ALU.add, op1=ALU.mult).then_inc(s_rm, 1)

            def rec_scan(i):
                for d in range(2):
                    dve.wait_ge(s_rr, 2 * i + d + 1)
                    link(tt(IH[d][:], IH[d][:], RH[d][:], ALU.mult))
                    if d == 0:
                        link(dve.tensor_tensor_scan(RH[0][:], AA[0][:], IH[0][:], 0.0, ALU.mult, ALU.add))
                    else:
                        r = lambda b_, lo, hi: b_[:, lo:hi][:, ::-1]
                        link(dve.tensor_tensor_scan(r(RH[1], 0, CTX), r(AA[1], 0, CTX), r(IH[1], 0, CTX), 0.0,
                                                    ALU.mult, ALU.add))
                        link(dve.tensor_tensor_scan(r(RH[1], CTX, TOT), r(AA[1], CTX, TOT), r(IH[1], CTX, TOT),
                                                    RH[1][:, 0:1], ALU.mult, ALU.add))
                link(tt(RH[0][:, CTX:], RH[0][:, CTX:], RH[1][:, CTX:], ALU.add))
                stt(out=yT[:, i, :], in0=gz[i % 2][:], scalar=0.5, in1=RH[0][:, CTX:], op0=ALU.mult,
                    op1=ALU.mult).then_inc(s_y, 1)

            def mod_sums(m):
                for q in range(MCH):
                    n = MORD.index(m) * MCH + q
                    dve.wait_ge(s_mod[n % 2], 16 * (n // 2 + 1))
                    dst = macc[:, q * 256:(q + 1) * 256]
                    for k in range(KD):
                        ck = silu_c[:, 0, k:k + 1]
                        if k == 0:
                            link(ts(dst, mring[:, n % 2, k, :], ck, None, ALU.mult))
                        else:
                            ins = stt(out=dst, in0=mring[:, n % 2, k, :], scalar=ck, in1=dst, op0=ALU.mult,
                                      op1=ALU.add)
                            if k < KD - 1:
                                link(ins)
                    ins.then_inc(s_modv, 1)
                    dve.wait_ge(s_modv, n + 1 - 2 * MCH)
                dve.memset(stat[:, 62:63], 0.0).then_inc(s_macc, 1)

            def mod_end(m):
                i = MORD.index(m) - 2
                g = {2: g2, 5: g5, 3: shr, 4: scr}[m]
                dve.wait_ge({2: s_gb2, 5: s_gb5, 3: s_gb3, 4: s_gb4}[m], 16)
                for h in range(2):
                    dve.wait_ge(s_m25, 2 * i + h + 1)
                    tt(g[:, h * HALF:(h + 1) * HALF], g[:, h * HALF:(h + 1) * HALF], bank[7][:],
                       ALU.add).then_inc(s_mrow, 1)
                if m == 4:
                    dve.wait_ge(s_mrow, 8)
                    dve.wait_ge(s_gff, 16)
                    link(stt(out=scr[:], in0=scr[:], scalar=1.0, in1=gff[:], op0=ALU.add, op1=ALU.mult))

            conv(0)
            gelu_poly(0)
            mod_sums(2)
            gelu_end(0)
            rec_input(0)
            conv(1)
            rec_scan(0)
            gelu_poly(1)
            mod_end(2)
            mod_sums(5)
            gelu_end(1)
            rec_input(1)
            conv(2)
            rec_scan(1)
            gelu_poly(2)
            mod_end(5)
            mod_sums(3)
            gelu_end(2)
            rec_input(2)
            conv(3)
            rec_scan(2)
            gelu_poly(3)
            mod_end(3)
            mod_sums(4)
            gelu_end(3)
            rec_input(3)
            rec_scan(3)
            mod_end(4)

            for m in range(2):
                dve.wait_ge(s_fc, m + 1)
                cs = (gt, Q)[m]
                tt(yT[:, 6 + m, 0:HALF], cs[:, 0:HALF], bank[2 + m][:], ALU.add)
                tt(yT[:, 6 + m, HALF + 1:SEQ][:, ::-1], cs[:, 1:HALF], bank[2 + m][:, 1:HALF], ALU.subtract)
                dve.tensor_copy(yT[:, 6 + m, HALF:HALF + 1], bank[4 + m][:, 0:1]).then_inc(s_fy, 1)

            for t in range(NT + 1):
                if t < NT:
                    xb, tmp = xr[t % NX], xm[t % 2]
                    dve.wait_ge(s_xr[t % NX], 16 * (t // NX + 1))
                    for h in range(2):
                        dve.wait_ge(s_mix, 2 * t + h + 1)
                        tt(tmp[:, h * HALF:(h + 1) * HALF], bank[(2 * t + h) % 4][:], g2[:, h * HALF:(h + 1) * HALF],
                           ALU.mult).then_inc(s_mixu, 1)
                    dve.wait_ge(s_mixu, 2 * t + 2)
                    tt(xb[:], xb[:], tmp[:], ALU.add).then_inc(s_x1, 1)
                    dve.wait_ge(s_ss2, t + 1)
                    ts(stat[:, 10 + t:11 + t], stat[:, 10 + t:11 + t], 1.0 / D, EPS, ALU.mult,
                       ALU.add).then_inc(s_ms2, 1)
                    dve.wait_ge(s_rt2, t + 1)
                    link(dve.reciprocal(stat[:, 18 + t:19 + t], stat[:, 18 + t:19 + t]))
                    if t >= 2:
                        dve.wait_ge(s_xnd[t % 2], 16 * (t // 2))
                        dve.wait_ge(s_t2, t - 1)
                    link(stt(out=xs[t % 2][:], in0=xb[:], scalar=stat[:, 18 + t:19 + t], in1=scr[:], op0=ALU.mult,
                             op1=ALU.mult))
                    tt(xs[t % 2][:], xs[t % 2][:], shr[:], ALU.add).then_inc(s_xn, 1)
                if t >= 1:
                    if t == 1:
                        dve.wait_ge(s_rw, 64)
                    dve.wait_ge(s_lgp, t)
                    tt(LG[:, t - 1, :], bank[6][:, 0:NG + NE], rb[:], ALU.add).then_inc(s_lg, 1)

            dve.wait_ge(s_lg, NT)
            lg, le = LG[:, :, 0:NG], LG[:, :, NG:].rearrange("p t (g j) -> p t g j", g=NG)
            f4 = K("first4").unsqueeze(1).to_broadcast([P, NT, 4])

            def b4(a):
                return a.unsqueeze(2).to_broadcast([P, NT, 4])

            def first_max(src, mx, hot, key, km):
                link(dve.tensor_reduce(mx, src, AX.X, ALU.max))
                link(tt(key, src, b4(mx), ALU.is_equal))
                link(tt(key, key, f4, ALU.mult))
                link(dve.tensor_reduce(km, key, AX.X, ALU.max))
                link(tt(hot, key, b4(km), ALU.is_equal))

            first_max(lg, R_["m"], R_["goh"], R_["key"], R_["km"])
            tt(R_["d"], lg, b4(R_["m"]), ALU.subtract).then_inc(s_e1, 1)
            link(tt(R_["big"], le, R_["goh"].unsqueeze(3).to_broadcast([P, NT, NG, EPG]), ALU.mult))
            link(dve.tensor_reduce(R_["les"], R_["big"].rearrange("p t g j -> p t j g"), AX.X, ALU.add))
            first_max(R_["les"], R_["m1"], R_["oh1"], R_["key"], R_["km"])
            link(stt(out=R_["les"], in0=R_["oh1"], scalar=-3e38, in1=R_["les"], op0=ALU.mult, op1=ALU.add))
            first_max(R_["les"], R_["m2"], R_["oh2"], R_["key"], R_["km"])
            tt(R_["ex"], R_["m2"], R_["m1"], ALU.subtract).then_inc(s_e1, 1)
            dve.wait_ge(s_e2, 1)
            link(dve.tensor_reduce(R_["pg"], R_["d"], AX.X, ALU.add))
            dve.wait_ge(s_e2, 2)
            link(ts(R_["w1"], R_["ex"], 1.0, None, ALU.add))
            link(tt(R_["w1"], R_["w1"], R_["pg"], ALU.mult))
            link(dve.reciprocal(R_["w1"], R_["w1"]))
            link(tt(R_["w2"], R_["w1"], R_["ex"], ALU.mult))
            M1, M2, G = R_["M1"], R_["M2"], R_["G"]
            g_b = R_["goh"].unsqueeze(3).to_broadcast([P, NT, NG, EPG])
            for M_, o_, w_ in ((M1, "oh1", "w1"), (M2, "oh2", "w2")):
                link(dve.tensor_copy(R_["big"], R_[o_].unsqueeze(2).to_broadcast([P, NT, NG, EPG])))
                link(tt(M_, R_["big"], g_b, ALU.mult))
            m16 = lambda a: a.rearrange("p t g j -> p t (g j)")
            w16 = lambda a: a.unsqueeze(2).to_broadcast([P, NT, NE])
            link(tt(m16(G), m16(M1), w16(R_["w1"]), ALU.mult))
            link(tt(m16(R_["big"]), m16(M2), w16(R_["w2"]), ALU.mult))
            link(tt(G, G, R_["big"], ALU.add))
            link(tt(M1, M1, M2, ALU.add))
            dve.tensor_copy(oh[:, 0, :].rearrange("p (t e) -> p t e", e=NE), m16(M1)).then_inc(s_mk, 1)
            ge = G.rearrange("p t g j -> p (g j) t")
            rem = R_["rem"]
            dve.tensor_copy(RV[:, :, :, 0], K("pidx").unsqueeze(2).to_broadcast([P, NE, NT]))
            dve.tensor_copy(RV[:, :, :, 1], K("tok0").unsqueeze(1).to_broadcast([P, NE, NT]))
            link(dve.tensor_copy(RV[:, :, :, 2], ge))
            link(tt(rem, ge, RV[:, :, :, 2], ALU.subtract))
            link(dve.tensor_copy(RV[:, :, :, 3], rem))
            link(tt(rem, rem, RV[:, :, :, 3], ALU.subtract))
            link(dve.tensor_copy(RV[:, :, :, 4], rem))
            dve.wait_ge(s_rk, 1)
            rk = bank[4][:, 0:P].rearrange("p (t e) -> p e t", e=NE)
            me = M1.rearrange("p t g j -> p (g j) t")
            link(stt(out=RK[:], in0=rk, scalar=1.0, in1=me, op0=ALU.add, op1=ALU.mult))
            link(ts(RK[:], RK[:], -1.0, None, ALU.add))

            row = lambda a, n: rs[0:1, a:a + n]
            every = lambda a, n: rs[:, a:a + n]
            cnt, nt_, inc, sq_ = every(1200, NE), every(1216, NE), every(1232, NE), every(1248, NE)
            t7 = every(0, NE * 7).rearrange("p (e k) -> p e k", k=7)
            link(dve.tensor_copy(cnt, bank[5][:, 0:NE]))
            link(tt(t7, cnt.unsqueeze(2).to_broadcast([P, NE, 7]), K("tcount").unsqueeze(1).to_broadcast([P, NE, 7]),
                    ALU.is_gt))
            link(dve.tensor_reduce(nt_, t7, AX.X, ALU.add))
            link(ts(nt_, nt_, 1.0, None, ALU.add))
            link(dve.tensor_tensor_scan(inc, K("ones")[:, 0:NE], nt_, 0.0, ALU.mult, ALU.add))
            link(tt(sq_, inc, nt_, ALU.subtract))
            Gp, sq128, p2, p1 = m16(G), every(1500, NE), every(1520, NT), every(1530, NT)
            link(ts(sq128, sq_, float(P), None, ALU.mult))
            link(tt(Gp, RK[:].rearrange("p e t -> p t e"), sq128.unsqueeze(1).to_broadcast([P, NT, NE]), ALU.add))
            link(tt(m16(R_["big"]), m16(M2), Gp, ALU.mult))
            link(dve.tensor_reduce(p2, m16(R_["big"]), AX.X, ALU.add))
            link(tt(Gp, m16(M1), Gp, ALU.mult))
            link(dve.tensor_reduce(p1, Gp, AX.X, ALU.add))
            link(tt(p1, p1, p2, ALU.subtract))
            link(dve.tensor_copy(pos[:, 0, :], p1))
            link(dve.tensor_copy(pos[:, 1, :], p2))
            inc, sq_ = inc[0:1], sq_[0:1]
            big = row(0, TAB * NE).rearrange("p (s e) -> p s e", e=NE)
            eT, mT, lT = row(1264, TAB), row(1300, TAB), row(1340, TAB)
            sq_b = sq_.unsqueeze(1).to_broadcast([1, TAB, NE])
            link(tt(big, sq_b, K("sidx")[0:1].unsqueeze(2).to_broadcast([1, TAB, NE]), ALU.is_le))
            link(dve.tensor_reduce(eT, big, AX.X, ALU.add))
            link(ts(eT, eT, -1.0, None, ALU.add))
            link(tt(big, big, sq_b, ALU.mult))
            link(dve.tensor_reduce(mT, big, AX.X, ALU.max))
            link(tt(mT, K("sidx")[0:1], mT, ALU.subtract))
            link(dve.memset(lT, 0.0))
            link(tt(lT[:, 0:TAB - 1], eT[:, 1:TAB], eT[:, 0:TAB - 1], ALU.subtract))
            pr = row(1400, MAXT // 2)
            link(ts(pr, K("slot0")[0:1, 0:MAXT // 2], 2.0 / P, None, ALU.mult))
            link(tt(pr, pr, inc[:, NE - 1:NE].to_broadcast([1, MAXT // 2]), ALU.is_lt))
            link(dve.tensor_reduce(row(1440, 1), pr, AX.X, ALU.add))
            link(ts(row(1440, 1), row(1440, 1), 2.0, None, ALU.mult))
            link(dve.tensor_copy(tab[0:1, 0, :], eT))
            link(dve.tensor_copy(tab[0:1, 1, :], mT))
            link(dve.tensor_copy(tab[0:1, 2, :], lT))
            link(dve.tensor_copy(tab[0:1, 3, 0:1], inc[:, NE - 1:NE]))
            dve.tensor_copy(tab[0:1, 3, 1:2], row(1440, 1)).then_inc(s_tab, 1)
            dve.wait_ge(s_tab, 1)

            def lo_gate_up(e1, j):
                dve.wait_ge(s_hgu, 4 * e1 + j + 1)
                tt(WP[:, j, 1, 0:2 * D], raw[:, j, 0:2 * D], WP[:, j, 0, 0:2 * D].bitcast(F32),
                   ALU.subtract).then_inc(s_logu[j], 1)

            NLINK = 2

            def plink(q, ins, k):
                ins.then_inc(s_pch, 1)
                dve.wait_ge(s_pch, NLINK * q + k)

            def prepare_slots(q, E1, T1):
                rk1 = RK[:, E1, :] if isinstance(E1, int) else RK[:, bass.ds(E1, 1), :].rearrange("p a n -> p (a n)")
                s0 = K("slot0")[:, 0:1] if isinstance(T1, int) else K("slot0")[:, bass.ds(T1, 1)]
                plink(q, ts(rkt[:], rk1, s0, None, ALU.subtract), 1)
                if not isinstance(q, int) or q:
                    dve.wait_ge(s_idx, q)
                tt(oh[:], K("iota").unsqueeze(1).to_broadcast([P, NT, P]),
                   rkt[:].unsqueeze(2).to_broadcast([P, NT, P]), ALU.is_equal).then_inc(s_oh, 1)

            def slot_ids(q):
                dve.wait_ge(s_idx, q + 1)
                if not isinstance(q, int) or q:
                    dve.wait_ge(s_pch, NLINK * q)
                dve.tensor_copy(idf[:, 0:NFLD], bank[2][:, 0:NFLD]).then_inc(s_idf, 1)
                dve.wait_ge(s_idf, q + 1)
                if not isinstance(q, int) or q:
                    dve.wait_ge(s_xg, 16 * q)
                tt(idg[:], idf[:, 0:1], idf[:, 1:2], ALU.add).then_inc(s_ids, 1)

            def slot_gates(q, p2):
                dve.tensor_reduce(gcol[:, p2], idf[:, 2:5], AX.X, ALU.add).then_inc(s_pch, 1)

            def lo_rows(q, p2, r):
                dve.wait_ge(s_xgh, 2 * q + r + 1)
                tt(xp[:, p2, 1, 4 * r:4 * r + 4, :], bank[(3, 6)[r]][:].rearrange("p (k n) -> p k n", n=P),
                   xp[:, p2, 0, 4 * r:4 * r + 4, :].bitcast(F32), ALU.subtract).then_inc(s_xgr, 1)

            dve.sem_inc(s_ye, 2)
            E1 = dve.value_load(tab[0:1, 0, 1:2], min_val=0, max_val=NE - 1)
            T1 = dve.value_load(tab[0:1, 1, 1:2], min_val=0, max_val=TAB - 1)
            prepare_slots(0, 0, 0)
            slot_ids(0)
            slot_gates(0, 0)
            prepare_slots(1, E1, T1)
            slot_ids(1)
            slot_gates(1, 1)
            for j in range(KE):
                lo_gate_up(0, j)
            for r in range(2):
                lo_rows(0, 0, r)
            W = dve.value_load(tab[0:1, 3, 0:1], min_val=NE, max_val=MAXT)
            with dve.Fori(0, MAXT // 2) as it:
                with dve.If(2 * it < W):
                    for par in range(2):
                        s = 2 * it + par
                        L = dve.value_load(tab[0:1, 2, bass.ds(s, 1)], min_val=0, max_val=1)
                        E1 = dve.value_load(tab[0:1, 0, bass.ds(s + 1, 1)], min_val=0, max_val=NE - 1)
                        E2 = dve.value_load(tab[0:1, 0, bass.ds(s + 2, 1)], min_val=0, max_val=NE - 1)
                        T2 = dve.value_load(tab[0:1, 1, bass.ds(s + 2, 1)], min_val=0, max_val=TAB - 1)
                        prepare_slots(s + 2, E2, T2)
                        with dve.If(L > 0):
                            lo_gate_up(E1, 0)
                        slot_ids(s + 2)
                        with dve.If(L > 0):
                            lo_gate_up(E1, 1)
                        dve.wait_ge(s_sg, s + 1)
                        dve.wait_ge(s_gud, 4 * s + 4)
                        for h in range(2):
                            hs = slice(h * 2 * P, (h + 1) * 2 * P)
                            tt(sg[:, hs], bank[1][:, hs], sg[:, hs], ALU.mult).then_inc(s_hid, 1)
                        for h in range(2):
                            dve.wait_ge(s_hfr, 2 * s + h + 1)
                            tt(hp[:, 1, 2 * h:2 * h + 2, :],
                               bank[(7, 2)[h]][:, h * 2 * P:(h + 1) * 2 * P].rearrange("p (k n) -> p k n", n=P),
                               hp[:, 0, 2 * h:2 * h + 2, :].bitcast(F32), ALU.subtract).then_inc(s_hps, 1)
                        for r in range(2):
                            lo_rows(s + 1, 1 - par, r)
                        with dve.If(L > 0):
                            lo_gate_up(E1, 2)
                            lo_gate_up(E1, 3)
                        dve.wait_ge(s_dd, 4 * s + 4)
                        dve.wait_ge(s_ys[par], 16 * it + 16)
                        for h in range(2):
                            hs = slice(h * HALF, (h + 1) * HALF)
                            stt(out=ysc[:, par, hs], in0=bank[4 + h][:], scalar=gcol[:, par, 0:1], in1=g5[:, hs],
                                op0=ALU.mult, op1=ALU.mult).then_inc(s_ye, 1)
                        dve.wait_ge(s_ye, 2 * s + 4)
                        slot_gates(s + 2, par)

            dve.wait_ge(s_gf, 16)
            for t in range(NT):
                n, k = t % NF, t // NF + 1
                dve.wait_ge(s_fg[n], 32 * k)
                link(tt(fa[n][:], fa[n][:], fb[n][:], ALU.add))
                dve.wait_ge(s_fl[n], 16 * k)
                tt(fx[n][:], fx[n][:], fa[n][:], ALU.add).then_inc(s_fx1, 1)
                dve.wait_ge(s_fs, t + 1)
                ts(stat[:, 28 + t:29 + t], stat[:, 28 + t:29 + t], 1.0 / D, EPS, ALU.mult, ALU.add).then_inc(s_fm, 1)
                dve.wait_ge(s_fr, t + 1)
                link(dve.reciprocal(stat[:, 36 + t:37 + t], stat[:, 36 + t:37 + t]))
                stt(out=fb[n][:], in0=fx[n][:], scalar=stat[:, 36 + t:37 + t], in1=gfin[:], op0=ALU.mult,
                    op1=ALU.mult).then_inc(s_fo, 1)


_INS = ["x", "c", "ctx", "c_ctx", "mod_w", "mod_b", "norm_mix_g", "norm_ffn_g", "w_in", "conv_w", "conv_b",
        "rec_gate_a_w", "rec_gate_a_b", "rec_gate_x_w", "rec_gate_x_b", "rec_lambda", "pool_w", "pool_scale",
        "fourier_w", "w_out", "router_group_w", "router_group_b", "router_expert_w", "router_expert_b",
        "expert_w_gate", "expert_w_up", "expert_w_down", "final_norm_g"]


def kernel(**inputs):
    import concourse.bacc as bacc
    from concourse.bass_utils import run_bass_kernel_spmd

    nc = bacc.Bacc("TRN2", target_bir_lowering=False, num_devices=1)
    arrays, args = {}, []
    packed, dft = constants()
    for name in _INS + ["consts", "dft"]:
        a = {"consts": packed, "dft": dft}[name] if name in ("consts", "dft") else np.ascontiguousarray(inputs[name])
        arrays[f"in_{name}"] = a
        args.append(nc.dram_tensor(f"in_{name}", a.shape, mybir.dt.from_np(a.dtype), kind="ExternalInput").ap())
    args.append(nc.dram_tensor("result", (1, SEQ, D), F32, kind="ExternalOutput").ap())
    build(nc, *args)
    r = run_bass_kernel_spmd(nc, [arrays], core_ids=[0])
    return r.results[0]["result"]
```

```python
from contextlib import ExitStack

import numpy as np
import concourse.bass as bass
from concourse import mybir

F32 = mybir.dt.float32
F32R = mybir.dt.float32r
BF16 = mybir.dt.bfloat16
I32 = mybir.dt.int32
ALU = mybir.AluOpType
ACT = mybir.ActivationFunctionType
AX = mybir.AxisListType

P = 128
D = 1024
KD = D // P
SEQ = 1024
NT = SEQ // P
CTX = 256
NC_ = CTX // P
ROWS, COLS = 16, 64
D_REC, D_POOL, D_FOUR = 512, 256, 256
D_IN = 2 * D_REC + D_POOL + D_FOUR
NI = D_REC // P
TOT = CTX + SEQ
HALF = 512
GRID_PAD = 8
NE, NG, EPG = 16, 4, 4
DE = 512
KE = DE // P
EPS = 1e-6
GELU_C = float(np.sqrt(2.0 / np.pi))
MAXT = SEQ * 2 // P + NE
TAB = MAXT + 3
NFLD = 5

CO = {}
_at = 0
for _n, _w in (("ident", P), ("ones", P), ("tri", P), ("iota", P), ("cos64", P), ("sin64", P), ("icr", 2 * ROWS),
               ("icc", 2 * COLS), ("alt", 1), ("pidx", 1), ("slot0", TAB), ("tok0", NT), ("first4", 4),
               ("tcount", 7), ("sidx", TAB), ("dump", 1)):
    CO[_n] = (_at, _at + _w)
    _at += _w
NCONST = _at

PV = {}
_at = 0
for _n, _w in (("c", KD), ("cc", KD), ("gmix", KD), ("gffn", KD), ("modb", 6 * KD), ("convw", 4 * NI), ("convb", NI),
               ("ba", 2 * NI), ("bx", 2 * NI), ("lam", 2 * NI), ("psc", 2)):
    PV[_n] = (_at, _at + _w)
    _at += _w
NPV = _at


def constants():
    c = np.zeros((P, NCONST), np.float32)

    def put(name, value):
        c[:, CO[name][0]:CO[name][1]] = value

    put("ident", np.eye(P))
    put("ones", 1.0)
    put("tri", np.triu(np.ones((P, P)), 1))
    put("iota", np.arange(P)[None])
    h = np.arange(64)
    ang = 2 * np.pi * np.outer(h, h) / 64
    scale = 1.0 / np.sqrt(SEQ * 64)
    put("cos64", np.kron(np.eye(2), np.cos(ang) * scale))
    put("sin64", np.kron(np.eye(2), -np.sin(ang) * scale))
    for m in range(2):
        for half in range(2):
            w = (2, 4, 8, 16)[2 * m + half]
            for name, n in (("icr", ROWS), ("icc", COLS)):
                t = np.arange(n)
                cnt = np.clip(t + w // 2, 0, n) - np.clip(t - w // 2, 0, n)
                c[64 * half:64 * half + 64, CO[name][0] + m * n:CO[name][0] + (m + 1) * n] = 1.0 / cnt
    p = np.arange(P)[:, None]
    put("alt", 1.0 - 2.0 * (p % 2))
    put("pidx", p)
    put("slot0", P * np.arange(TAB)[None])
    put("tok0", P * np.arange(NT)[None])
    put("first4", np.array([[4, 3, 2, 1]]))
    put("tcount", P * np.arange(1, 8)[None])
    put("sidx", np.arange(TAB)[None])
    put("dump", SEQ + p)
    n = np.arange(SEQ)
    ang = 2 * np.pi * (np.outer(n, np.arange(HALF)) % SEQ) / SEQ
    dft = np.concatenate([np.cos(ang), np.sin(ang)], axis=1).astype(np.float32)
    return c, dft


def build(nc, x, c, ctx, c_ctx, mod_w, mod_b, norm_mix_g, norm_ffn_g, w_in, conv_w, conv_b, gate_a_w, gate_a_b,
          gate_x_w, gate_x_b, lam, pool_w, pool_scale, fourier_w, w_out, rg_w, rg_b, re_w, re_b, wg, wu, wd,
          final_g, consts, dft, out):
    xn_d = nc.dram_tensor("normed_rows", [SEQ, D], F32).ap()
    x1_d = nc.dram_tensor("mixed_rows", [SEQ, D], F32).ap()
    y_d = nc.dram_tensor("expert_rows", [MAXT, P, D], F32).ap()

    es = ExitStack()
    with es:
        free_at = [0]
        base = (nc.sbuf_usable_end - nc.sbuf_bytes_remaining + 63) // 64 * 64
        end = nc.sbuf_usable_end

        def at(name, shape, dt, off):
            size = int(np.prod(shape[1:])) * (2 if dt == BF16 else 4)
            assert base + off + size <= end, (name, base + off + size - end)
            free_at[0] = max(free_at[0], off + size)
            return nc.alloc_sbuf_tensor_at(name, list(shape), dt, offset=base + off)

        cursor = [0]

        def keep(name, shape, dt=F32):
            off = cursor[0]
            size = int(np.prod(shape[1:])) * (2 if dt == BF16 else 4)
            cursor[0] += (size + 31) // 32 * 32
            return at(name, shape, dt, off)

        def sem(name):
            return es.enter_context(nc.semaphore(name))

        bank = [es.enter_context(nc.psum_tensor(f"bank{i}", [P, HALF], F32)) for i in range(8)]

        cst = keep("cst", [P, NCONST])
        pv = keep("pv", [P, NPV])
        g2 = keep("g2", [P, D])
        g5 = keep("g5", [P, D])
        sc_mix = keep("sc_mix", [P, KD, 2])
        sh_mix = keep("sh_mix", [P, KD, 2])
        silu_c = keep("silu_c", [P, 2, KD])
        rw = keep("rw", [P, KD, NG + NE])
        rb = keep("rb", [P, NG + NE])
        stat = keep("stat", [P, 64])
        LG = keep("LG", [P, NT, NG + NE])
        tri_b = keep("tri_b", [P, P], BF16)
        ones_b = keep("ones_b", [P, P], BF16)
        held = keep("held", [P, 1])
        pos = keep("pos", [P, 2, NT], I32)
        PHASE = cursor[0]

        def K(name):
            return cst[:, CO[name][0]:CO[name][1]]

        ident, ones = K("ident"), K("ones")

        def V(name, i=None):
            a, b = PV[name]
            return pv[:, a:b] if i is None else pv[:, a + i:a + i + 1]

        o = PHASE
        hT = at("hT", [P, KD, SEQ], F32, o)
        wout_sb = at("wout_sb", [P, KD, D], F32, o); o += 32768
        yT = at("yT", [P, KD, SEQ], F32, o)
        xt = at("xt", [P, NT, D], F32, o); o += 32768
        hTc = at("hTc", [P, KD, CTX], F32, o)
        scr = at("scr", [P, D], F32, o)
        shr = at("shr", [P, D], F32, o + 4096); o += 8192
        wring = at("wring", [P, 3, KD, P], F32, o); o += 12288
        dring = at("dring", [P, 3, SEQ], F32, o - 12288)
        mring = at("mring", [P, 2, KD, 256], F32, o)
        gff = at("gff", [P, D], F32, o); o += 16384
        macc = at("macc", [P, D], F32, o); o += 4096
        rec0 = o
        w_hi = at("w_hi", [P, KD, D], F32R, PHASE + 73728)
        y_hi = at("y_hi", [P, KD, SEQ], F32R, rec0 + 35840)
        w_lo = at("w_lo", [P, KD, D], F32R, PHASE)
        y_lo = at("y_lo", [P, KD, SEQ], F32R, PHASE + 32768)
        RH = [at(f"RH{d}", [P, TOT], F32, o + 5120 * d) for d in range(2)]
        IH = [at(f"IH{d}", [P, TOT], F32, o + 10240 + 5120 * d) for d in range(2)]
        AA = [at(f"AA{d}", [P, TOT], F32, o + 20480 + 5120 * d) for d in range(2)]
        Q = at("Q", [P, TOT], F32, o + 30720); o += 35840
        mrow = at("mrow", [2, 2 * D], F32, rec0)
        U = [at(f"U{d}", [P, TOT], F32, o + 5120 * d) for d in range(2)]; o += 10240
        ZPL = TOT + 6
        zpad = at("zpad", [P, ZPL], F32, o)
        zf1 = at("zf1", [P, SEQ], F32, o); o += 5152
        gz = [at(f"gz{d}", [P, SEQ], F32, o + 4096 * d) for d in range(2)]
        gt = at("gt", [P, SEQ], F32, o + 8192); o += 12288
        P0 = at("P0", [P, 2 * ROWS, COLS], F32, o)
        P1 = at("P1", [P, 2 * ROWS, COLS], F32, o + 8192)
        C0 = at("C0", [P, ROWS, COLS + 16], F32, o)
        C1 = at("C1", [P, ROWS, COLS + 16], F32, o + 8192)
        Vf = at("Vf", [P, NT, 2, 256], F32, o)
        ctxt = at("ctxt", [P, NC_, D], F32, o); o += 16384
        mslot = [mring[:, 0], mring[:, 1],
                 at("mslot2", [P, KD, 256], F32, rec0 + 10240)[:], at("mslot3", [P, KD, 256], F32, rec0 + 35840)[:]]
        prow = at("prow", [P, P], F32, o - 4096)
        zf0 = at("zf0", [P, SEQ], F32, rec0 - 4096)
        bdg = at("bdg", [P, 4, NI, P], F32, o); o += 8192
        wfb = at("wfb", [P, 2, P], F32, o); o += 1024
        csw = at("csw", [P, 2, 256], F32, PHASE + 32768 + 6 * 4096)
        wpb = at("wpb", [P, 2, P], F32, o); o += 1024
        lamw = at("lamw", [P, 6, 2 * NI], F32, o); o += 192
        hb_ = at("hb_", [P, 4, NI], F32, o); o += 64
        NX = 3
        xr = [at(f"xr{n}", [P, D], F32, rec0 + 4096 * n) for n in range(NX)]
        xm = [at(f"xm{n}", [P, D], F32, rec0 + 12288 + 4096 * n) for n in range(2)]
        xs = [at(f"xs{n}", [P, D], F32, rec0 + 20480 + 4096 * n) for n in range(2)]
        h2 = at("h2", [P, KD, P], F32, rec0 + 28672)

        o = PHASE
        WP = at("WP", [P, KE, 2, 3 * D], F32R, o); o += KE * 2 * 3 * D * 4
        raw = at("raw", [P, KE, 3 * D], F32, o); o += KE * 3 * D * 4
        xg = at("xg", [P, D], F32, o); o += 4096
        xp = at("xp", [P, 2, 2, KD, P], F32R, o); o += 16384
        sg = at("sg", [P, HALF], F32, o); o += 2048
        hp = at("hp", [P, 2, KE, P], F32R, o); o += 4096
        ysc = at("ysc", [P, 2, D], F32, o); o += 8192
        oh = at("oh", [P, NT, P], BF16, o); o += 2048
        RK = at("RK", [P, NE, NT], F32, o); o += 512
        rkt = at("rkt", [P, NT], F32, o); o += 32
        RV = at("RV", [P, NE, NT, NFLD], BF16, o); o += 1280
        idf = at("idf", [P, 8], F32, o); o += 32
        idg = at("idg", [P, 1], I32, o); o += 32
        gcol = at("gcol", [P, 2, 1], F32, o); o += 32
        tab = at("tab", [1, 4, TAB], I32, o); o += 640
        rs = at("rs", [P, 2360], F32, o)
        R_ = {}
        ra = 0
        for n_, sh_ in (("m", ()), ("goh", (4,)), ("key", (4,)), ("km", ()), ("d", (4,)), ("les", (4,)), ("m1", ()),
                        ("oh1", (4,)), ("m2", ()), ("oh2", (4,)), ("ex", ()), ("pg", ()), ("w1", ()), ("w2", ()),
                        ("big", (4, 4)), ("M1", (4, 4)), ("M2", (4, 4)), ("G", (4, 4)), ("rem", (NE, NT))):
            size = NT * int(np.prod(sh_)) if n_ != "rem" else NE * NT
            v_ = rs[:, ra:ra + size]
            if n_ == "rem":
                v_ = v_.rearrange("p (e t) -> p e t", t=NT)
            elif len(sh_) == 1:
                v_ = v_.rearrange("p (t a) -> p t a", a=4)
            elif len(sh_) == 2:
                v_ = v_.rearrange("p (t a b) -> p t a b", a=4, b=4)
            R_[n_] = v_
            ra += size
        fa = [at(f"fa{n}", [P, D], F32, PHASE + 4096 * n) for n in range(NT)]
        fb = [at(f"fb{n}", [P, D], F32, PHASE + 32768 + 4096 * n) for n in range(NT)]
        fj = [at(f"fj{n}", [P, D], F32, PHASE + 65536 + 4096 * n) for n in range(2)]
        fx = at("fx", [P, NT, D], F32, PHASE + 98304)
        gfin = at("gfin", [P, D], F32, PHASE + 98304 + 32768)

        s_prow = sem("constants_and_parameters_in")
        s_x = [sem(f"x_in{n}") for n in range(3)]
        s_mcol = sem("mod_rows_copied")
        s_mtr = sem("mod_rows_transposed")
        s_rw = sem("router_in")
        s_bd = sem("blockdiag_in")
        s_gb2 = sem("mix_gate_bias_in")
        s_gb5 = sem("ffn_gate_bias_in")
        s_gf = sem("final_gain_in")
        s_bd0 = sem("blockdiag_zeroed")
        s_mod = [sem(f"modw_in{n}") for n in range(4)]
        s_modu = sem("modw_used_by_pe")
        s_modv = sem("modw_used_by_dve")
        s_win = [sem(f"win_in{n}") for n in range(3)]
        s_dft = [sem(f"dft_in{n}") for n in range(3)]
        s_dftu = sem("dft_used")
        s_wout = [sem(f"wout_in{n}") for n in range(2)]
        s_sph, s_spl, s_scr = sem("split_hi"), sem("split_lo"), sem("ffn_scale_ready")
        s_zero = sem("zero_row")
        s_zero_d = sem("sums_zeroed")
        s_pvp = sem("params_transposed")
        s_pv = sem("params_ready")
        s_sil = sem("silu_tanh")
        s_silu = sem("silu_ready")
        s_ss = sem("x_square_sums")
        s_ms = sem("x_mean_squares")
        s_sq = sem("x_root")
        s_xs = sem("x_scaled")
        s_scsh = sem("mix_scale_shift")
        s_tpe = sem("x_transposed")
        s_z = sem("z_ready")
        s_zu = sem("z_taken")
        s_conv = sem("u_ready")
        s_g = sem("gates_ready")
        s_gu = sem("gates_taken")
        s_ra = sem("decay_ready")
        s_rm = sem("input_scaled")
        s_rr = sem("root_ready")
        s_y = sem("recurrent_done")
        s_gp = sem("gelu_poly")
        s_gth = sem("gelu_tanh")
        s_gel = sem("gelu_ready")
        s_pd = sem("pool_diff")
        s_pm = sem("pool_product")
        s_py = sem("pool_ready")
        s_csw = sem("csw_product")
        s_cswc = sem("csw_ready")
        s_fc = sem("dft_copied")
        s_fy = sem("fourier_ready")
        s_lam = sem("lam_abs")
        s_lame = sem("lam_exp")
        s_lamc = sem("lam_ready")
        s_macc = sem("mod_summed")
        s_m25 = sem("mod_product")
        s_mrow = sem("mod_ready")
        s_mix = sem("mix_ready")
        s_mixu = sem("mix_taken")
        s_xr = [sem(f"x_again{n}") for n in range(NX)]
        s_x1 = sem("x1_ready")
        s_x1d = [sem(f"x1_stored{n}") for n in range(NX)]
        s_ss2 = sem("x1_square_sum")
        s_ms2 = sem("x1_mean_square")
        s_rt2 = sem("x1_root")
        s_xn = sem("xn_ready")
        s_xnd = [sem(f"xn_stored{n}") for n in range(2)]
        s_t2 = sem("xn_transposed")
        s_h2 = sem("h2_ready")
        s_lgp = sem("logits_summed")
        s_lg = sem("logits_ready")
        s_e1 = sem("router_exponents")
        s_e2 = sem("router_exps")
        s_mk = sem("masks_ready")
        s_rk = sem("ranks_summed")
        s_tab = sem("tables_ready")
        s_dv = sem("vector_chain")
        s_pc = sem("pool_engine_chain")
        s_rgu = [sem(f"raw_gate_up_in{j}") for j in range(KE)]
        s_rdn = [sem(f"raw_down_in{j}") for j in range(KE)]
        s_logu = [sem(f"gate_up_split{j}") for j in range(KE)]
        s_lod = [sem(f"down_split{j}") for j in range(KE)]
        s_gate = sem("gate_done")
        s_gud = sem("gate_up_done")
        s_dd = sem("down_done")
        s_hT = sem("hidden_transposed")
        s_sil2 = sem("silu_ready_twice")
        s_sg = sem("silu_done")
        s_hid = sem("hidden_product")
        s_hfr = sem("hidden_hi")
        s_hps = sem("hidden_ready")
        s_oh = sem("onehot_ready")
        s_idx = sem("slots_summed")
        s_idf = sem("slot_fields")
        s_ids = sem("slot_ids_ready")
        s_xg = sem("rows_gathered")
        s_xgt = sem("rows_transposed")
        s_xgh = sem("rows_hi")
        s_xgr = sem("rows_ready")
        s_ye = sem("y_scaled")
        s_ys = [sem(f"y_stored{n}") for n in range(2)]
        s_held = sem("pool_held")
        s_end = sem("experts_finished")
        s_zp = sem("conv_pads_zeroed")
        s_tri = sem("bf16_constants")
        s_tpa = sem("h_ready_scalar")
        s_tpv = sem("h_ready_vector")
        s_hgu = sem("gate_up_hi")
        s_hdn = sem("down_hi")
        s_pch = sem("prepare_chain")
        s_fps = sem("expert_rows_added")
        s_fg = [sem(f"expert_rows_in{n}") for n in range(NT)]
        s_gb3 = sem("shift_scale_bias_in")
        s_gff = sem("ffn_gain_in")
        s_fl = [sem(f"x1_back{n}") for n in range(2)]
        s_fx1 = sem("final_sum")
        s_fs = sem("final_square")
        s_fm = sem("final_mean")
        s_fr = sem("final_root")
        s_fo = sem("final_row")
        s_out = sem("out_stored")

        SPLIT = [("w", 4), ("w", 5), ("w", 6), ("w", 7), ("y", 0), ("y", 1), ("y", 2), ("y", 3), ("w", 3), ("y", 4),
                 ("w", 0), ("w", 1), ("w", 2), ("y", 5), ("y", 6), ("y", 7)]
        EARLY = 10
        K_ORDER = (4, 3, 0, 1, 2, 5, 6, 7)
        COLT = [("x", 0), ("g", 0), ("p", 0), ("x", 1), ("g", 1), ("p", 1), ("x", 2), ("g", 2), ("x", 3), ("g", 3),
                ("f", 0), ("f", 1)]
        OFF = {"x": 0, "g": D_REC, "p": 2 * D_REC, "f": 2 * D_REC + D_POOL}
        GATES_AFTER = {("p", 0): 0, ("p", 1): 1, ("g", 2): 2, ("g", 3): 3}
        UNITS = [(ct, part) for ct in COLT for part in ((("c",) if ct[0] == "x" else ()) + (0, 1))]
        UNIT = {u: n for n, u in enumerate(UNITS)}
        GPARTS = [(CTX, HALF), (CTX + HALF, HALF), (0, CTX)]
        GUNITS = [(i, d, g, q) for i in range(NI) for d in range(2) for g in range(2) for q in range(3)]
        NMC = 6 * D // 256
        MORD = (0, 1, 2, 5, 3, 4)
        mod_slot = lambda n: n % 4 if n < 2 * MCH else n % 2
        mod_fill = lambda n: n // 4 + 1 if n < 2 * MCH else 2 * MCH // 4 + (n - 2 * MCH) // 2 + 1
        POOL_SUMS = (3, 4, 5, 6)
        XPARTS = (range(0, 2), range(2, 6), range(6, 10))
        MCH = D // 256

        block = es.enter_context(nc.Block())

        @block.sync
        def _(sp):
            sp.dma_start(cst[:], consts).then_inc(s_prow, 16)
            rows = lambda a: a.rearrange("(r q) -> r q", q=P)
            prows = [("c", rows(c[0])), ("cc", rows(c_ctx)), ("gmix", rows(norm_mix_g[0])),
                     ("gffn", rows(norm_ffn_g[0])), ("modb", rows(mod_b[0])),
                     ("convw", conv_w[0].rearrange("k (i q) -> (k i) q", q=P)), ("convb", rows(conv_b[0])),
                     ("ba", gate_a_b[0].rearrange("d (i q) -> (d i) q", q=P)),
                     ("bx", gate_x_b[0].rearrange("d (i q) -> (d i) q", q=P)),
                     ("lam", lam[0].rearrange("d (i q) -> (d i) q", q=P)), ("psc", rows(pool_scale[0]))]
            for name, src in prows:
                sp.dma_start(prow[PV[name][0]:PV[name][1], :], src).then_inc(s_prow, 16)
            xv = x[0].rearrange("(t p) d -> p t d", p=P)
            mv = mod_w[0].rearrange("(k p) n -> p k n", p=P)

            def load_mod(n):
                if 4 <= n < 2 * MCH + 2:
                    sp.wait_ge(s_modu, n - 3)
                if n >= 2 * MCH + 2:
                    sp.wait_ge(s_modv, n - 1 - 2 * MCH)
                a = MORD[n // MCH] * D + n % MCH * 256
                slot = mod_slot(n)
                sp.dma_start(mslot[slot], mv[:, :, a:a + 256]).then_inc(s_mod[slot], 16)

            for n in range(2 * MCH):
                load_mod(n)
            wv = w_in[0].rearrange("(k p) n -> p k n", p=P)

            def load_win(n):
                if n >= 3:
                    sp.wait_ge(s_z, UNIT[(COLT[n - 3], 1)] + 1)
                a = OFF[COLT[n][0]] + COLT[n][1] * P
                sp.dma_start(wring[:, n % 3], wv[:, :, a:a + P]).then_inc(s_win[n % 3], 16)

            for n in range(3):
                load_win(n)
            sp.wait_ge(s_bd0, 3)
            for d in range(2):
                for g, w in enumerate((gate_a_w, gate_x_w)):
                    for h in range(2):
                        sp.dma_start(bdg[64 * h:64 * h + 64, 2 * d + g, :, 64 * h:64 * h + 64],
                                     w[0, d].rearrange("(i h) a b -> h a i b", h=2)[h]).then_inc(s_bd, 16)
            for h in range(2):
                sp.dma_start(wfb[64 * h:64 * h + 64, :, 64 * h:64 * h + 64],
                             fourier_w[0].rearrange("(m h) a b -> h a m b", h=2)[h]).then_inc(s_bd, 16)
                sp.dma_start(wpb[64 * h:64 * h + 64, :, 64 * h:64 * h + 64],
                             pool_w[0].rearrange("(m h) a b -> h a m b", h=2)[h]).then_inc(s_bd, 16)
            sp.dma_start(rw[:, :, 0:NG], rg_w[0].rearrange("(k p) n -> p k n", p=P)).then_inc(s_rw, 16)
            sp.dma_start(rw[:, :, NG:], re_w[0].rearrange("(k p) n -> p k n", p=P)).then_inc(s_rw, 16)
            sp.dma_start(rb[:, 0:NG], rg_b.partition_broadcast(P).rearrange("p a n -> p (a n)")).then_inc(s_rw, 16)
            sp.dma_start(rb[:, NG:], re_b.partition_broadcast(P).rearrange("p a n -> p (a n)")).then_inc(s_rw, 16)
            sp.dma_start(g2[:], mod_b[0:1, 2 * D:3 * D].partition_broadcast(P).rearrange("p a n -> p (a n)"))\
                .then_inc(s_gb2, 16)
            sp.wait_ge(s_zero, 1)
            for r in range(NE, MAXT):
                sp.dma_start(y_d[r], g5[:]).then_inc(s_zero_d, 16)
            mod_next = 2 * MCH
            everywhere = lambda a: a.partition_broadcast(P).rearrange("p a n -> p (a n)")
            for n in range(3, len(COLT)):
                load_win(n)
                for _ in range(2):
                    if mod_next < NMC - 2:
                        load_mod(mod_next)
                        mod_next += 1
                if n == 5:
                    sp.wait_ge(s_zero_d, 16 * (MAXT - NE))
                    sp.dma_start(g5[:], everywhere(mod_b[0:1, 5 * D:6 * D])).then_inc(s_gb5, 16)
            sp.dma_start(shr[:], everywhere(mod_b[0:1, 3 * D:4 * D])).then_inc(s_gb3, 16)
            sp.dma_start(scr[:], everywhere(mod_b[0:1, 4 * D:5 * D])).then_inc(s_gb3, 16)
            load_mod(NMC - 2)
            load_mod(NMC - 1)
            sp.wait_ge(s_z, len(UNITS))
            for k in range(NT):
                if k >= 3:
                    sp.wait_ge(s_dftu, k - 2)
                sp.dma_start(dring[:, k % 3], dft[k * P:(k + 1) * P, :]).then_inc(s_dft[k % 3], 16)
                if k in (2, 3):
                    h = 3 - k
                    sp.dma_start(wout_sb[:, 4 * h:4 * h + 4],
                                 w_out[0].rearrange("(k p) n -> p k n", p=P)[:, 4 * h:4 * h + 4]).then_inc(s_wout[h], 16)
                if k == 2:
                    sp.wait_ge(s_modv, 4 * MCH)
                    sp.dma_start(gff[:], everywhere(norm_ffn_g[0:1])).then_inc(s_gff, 16)
            sp.wait_ge(s_y, NI)
            for t in range(NX):
                sp.dma_start(xr[t][:], xv[:, t]).then_inc(s_xr[t], 16)
            x1v = x1_d.rearrange("(t p) d -> p t d", p=P)
            xnv = xn_d.rearrange("(t p) d -> p t d", p=P)
            for t in range(NT):
                sp.wait_ge(s_x1, t + 1)
                sp.dma_start(x1v[:, t], xr[t % NX][:]).then_inc(s_x1d[t % NX], 16)
                sp.wait_ge(s_xn, t + 1)
                sp.dma_start(xnv[:, t], xs[t % 2][:]).then_inc(s_xnd[t % 2], 16)
                if t + NX < NT:
                    sp.wait_ge(s_x1d[t % NX], 16 * (t // NX + 1))
                    sp.dma_start(xr[t % NX][:], xv[:, t + NX]).then_inc(s_xr[t % NX], 16)

            def load_gate_up(e, j):
                for g, w in enumerate((wg, wu)):
                    a = w[0, e] if isinstance(e, int) else w[0, e].rearrange("a k n -> (a k) n")
                    sp.dma_start(raw[:, j, g * D:(g + 1) * D].rearrange("p (k n) -> p k n", n=HALF),
                                 a[2 * P * j:2 * P * (j + 1), :].rearrange("(k p) n -> p k n", p=P)).then_inc(s_rgu[j], 16)

            def load_down(e, j):
                a = wd[0, e] if isinstance(e, int) else wd[0, e].rearrange("a h n -> (a h) n")
                sp.dma_start(raw[:, j, 2 * D:], a[j * P:(j + 1) * P, :]).then_inc(s_rdn[j], 16)

            sp.wait_ge(s_lg, NT)
            for n in range(NX):
                sp.wait_ge(s_x1d[n], 16 * len(range(n, NT, NX)))
            for n in range(2):
                sp.wait_ge(s_xnd[n], 16 * (NT // 2))
            sp.wait_ge(s_mrow, 8)
            for j in range(KE):
                load_gate_up(0, j)
            for j in range(KE):
                load_down(0, j)
            with sp.Fori(1, NE) as e:
                for j in range(KE):
                    sp.wait_ge(s_logu[j], e)
                    load_gate_up(bass.ds(e, 1), j)
                for j in range(KE):
                    sp.wait_ge(s_lod[j], e)
                    load_down(bass.ds(e, 1), j)
            for j in range(KE):
                sp.wait_ge(s_logu[j], NE)
                sp.wait_ge(s_lod[j], NE)
            sp.dma_start(fx[:, 0:4], x1v[:, 0:4]).then_inc(s_fl[0], 16)
            sp.dma_start(gfin[:], final_g.partition_broadcast(P)).then_inc(s_gf, 16)
            sp.wait_ge(s_end, 1)
            sp.dma_start(fx[:, 4:8], x1v[:, 4:8]).then_inc(s_fl[1], 16)
            ov = out[0].rearrange("(t p) d -> p t d", p=P)
            for t in range(NT):
                sp.wait_ge(s_fo, t + 1)
                sp.dma_start(ov[:, t], fb[t][:]).then_inc(s_out, 16)
            sp.wait_ge(s_out, 16 * NT)

        @block.gpsimd
        def _(pool):
            pool.memset(g5[:], 0.0).then_inc(s_zero, 1)
            pool.memset(held[:], 0.0).then_inc(s_held, 1)
            pool.memset(zpad[:], 0.0).then_inc(s_zp, 1)
            pool.memset(bdg[:], 0.0).then_inc(s_bd0, 1)
            pool.memset(wfb[:], 0.0).then_inc(s_bd0, 1)
            pool.memset(wpb[:], 0.0).then_inc(s_bd0, 1)
            pool.wait_ge(s_prow, 16 * (len(PV) + 1))
            pool.tensor_copy(tri_b[:], K("tri")).then_inc(s_tri, 1)
            pool.tensor_copy(ones_b[:], ones).then_inc(s_tri, 1)

            chain = [0]

            def link(ins):
                chain[0] += 1
                ins.then_inc(s_pc, 1)
                pool.wait_ge(s_pc, chain[0])

            def add(o_, a_, b_):
                return pool.tensor_tensor(o_, a_, b_, ALU.add)

            for m in range(2):
                z = yT[:, 4 + m, :].rearrange("p (r c) -> p r c", c=COLS)
                pool.wait_ge(s_zu, UNIT[(("p", m), 1)] + 1)
                if m == 1:
                    pool.wait_ge(s_pd, 1)
                if m == 0:
                    pool.wait_ge(s_tpe, 3 * KD)
                link(pool.memset(P0[:, 0:GRID_PAD, :], 0.0))
                link(pool.memset(P0[:, GRID_PAD + ROWS:, :], 0.0))
                link(pool.tensor_copy(P0[:, GRID_PAD:GRID_PAD + ROWS, :], z))
                link(add(P1[:, 0:31, :], P0[:, 0:31, :], P0[:, 1:32, :]))
                if m == 1:
                    link(add(P0[:, 0:29, :], P1[:, 0:29, :], P1[:, 2:31, :]))
                    link(add(P1[:, 0:25, :], P0[:, 0:25, :], P0[:, 4:29, :]))
                a, b, c_ = ((7, 6, 8), (4, 0, 8))[m]
                link(pool.memset(C0[:, :, 0:8], 0.0))
                link(pool.memset(C0[:, :, 8 + COLS:], 0.0))
                link(pool.tensor_copy(C0[0:64, :, 8:8 + COLS], P1[0:64, a:a + ROWS, :]))
                link(add(C0[64:128, :, 8:8 + COLS], P1[64:128, b:b + ROWS, :], P1[64:128, c_:c_ + ROWS, :]))
                link(add(C1[:, :, 0:79], C0[:, :, 0:79], C0[:, :, 1:80]))
                if m == 1:
                    link(add(C0[:, :, 0:77], C1[:, :, 0:77], C1[:, :, 2:79]))
                    link(add(C1[:, :, 0:73], C0[:, :, 0:73], C0[:, :, 4:77]))
                icr = K("icr")[:, m * ROWS:(m + 1) * ROWS].unsqueeze(2)
                icc = K("icc")[:, m * COLS:(m + 1) * COLS].unsqueeze(1)
                link(add(C0[64:128, :, 0:COLS], C1[64:128, :, b:b + COLS], C1[64:128, :, c_:c_ + COLS]))
                link(pool.tensor_tensor(C0[64:128, :, 0:COLS], C0[64:128, :, 0:COLS],
                                        icr[64:128].to_broadcast([64, ROWS, COLS]), ALU.mult))
                link(pool.tensor_tensor(C0[0:64, :, 0:COLS], C1[0:64, :, a:a + COLS],
                                        icr[0:64].to_broadcast([64, ROWS, COLS]), ALU.mult))
                link(pool.tensor_tensor(C0[:, :, 0:COLS], C0[:, :, 0:COLS], icc.to_broadcast([P, ROWS, COLS]),
                                        ALU.mult))
                pool.tensor_tensor(z, C0[:, :, 0:COLS], z, ALU.subtract).then_inc(s_pd, 1)

            def hold(n):
                pool.wait_ge(s_held, n + 1)
                pool.tensor_tensor(held[:], held[:], held[:], ALU.mult).then_inc(s_held, 1)

            def split_down(e1, j):
                pool.wait_ge(s_hdn, 4 * e1 + j + 1)
                pool.tensor_tensor(WP[:, j, 1, 2 * D:], raw[:, j, 2 * D:], WP[:, j, 0, 2 * D:].bitcast(F32),
                                   ALU.subtract).then_inc(s_lod[j], 1)

            def gather(q):
                pool.wait_ge(s_ids, q + 1)
                if not isinstance(q, int):
                    hold(q - 2)
                pool.indirect_dma_start(out=xg[:], out_offset=None, in_=xn_d,
                                        in_offset=bass.IndirectOffsetOnAxis(ap=idg[:, 0:1], axis=0)).then_inc(s_xg, 16)

            for j in range(2):
                pool.wait_ge(s_hgu, j + 1)
                pool.tensor_tensor(WP[:, j, 1, 0:2 * D], raw[:, j, 0:2 * D], WP[:, j, 0, 0:2 * D].bitcast(F32),
                                   ALU.subtract).then_inc(s_logu[j], 1)
            for n in range(2):
                pool.wait_ge(s_xnd[n], 16 * (NT // 2))
            gather(0)
            pool.wait_ge(s_xgt, 2)
            gather(1)
            for j in range(KE):
                split_down(0, j)
            W = pool.value_load(tab[0:1, 3, 0:1], min_val=NE, max_val=MAXT)
            with pool.Fori(0, MAXT // 2) as it:
                for par in range(2):
                    with pool.If(2 * it + par < W):
                        s = 2 * it + par
                        L = pool.value_load(tab[0:1, 2, bass.ds(s, 1)], min_val=0, max_val=1)
                        E1 = pool.value_load(tab[0:1, 0, bass.ds(s + 1, 1)], min_val=0, max_val=NE - 1)
                        pool.wait_ge(s_xgt, 2 * s + 4)
                        gather(s + 2)
                        with pool.If(L > 0):
                            for j in range(KE):
                                split_down(E1, j)
            Wl = pool.value_load(tab[0:1, 3, 1:2], min_val=NE, max_val=MAXT)
            Wf = pool.value_load(tab[0:1, 3, 2:3], min_val=NE, max_val=MAXT)
            pool.wait_ge(s_ys[0], 8 * Wl + 16)
            pool.wait_ge(s_ys[1], 8 * Wf + 16)
            pool.wait_ge(s_xg, 16 * W + 32)
            hold(W)
            pool.memset(stat[:, 63:64], 0.0).then_inc(s_end, 1)
            y_rows = y_d.rearrange("s p d -> (s p) d")
            for t in range(NT):
                for a, buf in enumerate((fa, fb)):
                    pool.indirect_dma_start(out=buf[t][:], out_offset=None, in_=y_rows,
                                            in_offset=bass.IndirectOffsetOnAxis(ap=pos[:, a, t:t + 1], axis=0))\
                        .then_inc(s_fg[t], 16)
            for t in POOL_SUMS:
                pool.wait_ge(s_fg[t], 32)
                pool.tensor_tensor(fa[t][:], fa[t][:], fb[t][:], ALU.add).then_inc(s_fps, 1)

        @block.tensor
        def _(pe):
            pe.wait_ge(s_prow, 16 * (len(PV) + 1))
            pe.transpose(bank[7][:, 0:NPV], prow[0:NPV, :], ident[0:NPV, 0:NPV]).then_inc(s_pvp, 1)

            pe.wait_ge(s_silu, 1)
            for n in range(2 * MCH):
                pe.wait_ge(s_mod[mod_slot(n)], 16 * mod_fill(n))
                for k in range(KD):
                    mm = pe.matmul(bank[n // 2][0:2, n % 2 * 256:(n % 2 + 1) * 256], silu_c[:, :, k],
                                   mslot[mod_slot(n)][:, k, :], start=k == 0, stop=k == KD - 1)
                mm.then_inc(s_modu, 1)
            pe.wait_ge(s_mcol, 4)
            for j in range(2 * KD):
                mm = pe.transpose(bank[6][:, 2 * j:2 * j + 2], mrow[:, j * P:(j + 1) * P], ident[0:2, 0:2])
            mm.then_inc(s_mtr, 1)

            def z_unit(n, part):
                ct = COLT[n]
                pe.wait_ge(s_win[n % 3], 16 * (n // 3 + 1))
                u = UNIT[(ct, part)]
                if u >= 4:
                    pe.wait_ge(s_zu, u - 3)
                o_ = bank[u % 4][:, 0:CTX] if part == "c" else bank[u % 4][:]
                for k in range(KD):
                    src = hTc[:, k, :] if part == "c" else hT[:, k, part * HALF:(part + 1) * HALF]
                    mm = pe.matmul(o_, wring[:, n % 3, k, :], src, start=k == 0, stop=k == KD - 1)
                mm.then_inc(s_z, 1)

            def z_tile(n):
                for part in ((("c",) if COLT[n][0] == "x" else ()) + (0, 1)):
                    z_unit(n, part)

            pe.wait_ge(s_scsh, 1)
            n = 0
            for i, part in enumerate(("c", 0, 1)):
                cnt = NC_ if part == "c" else 4
                pe.wait_ge(s_xs, {"c": 2, 0: 6, 1: 10}[part])
                for k in range(KD):
                    if n >= 4:
                        m_ = n - 4
                        pe.wait_ge(s_tpa if m_ % 2 == 0 else s_tpv, m_ // 2 + 1)
                    for t in range(cnt):
                        src = ctxt[:, t] if part == "c" else xt[:, 4 * part + t]
                        mm = pe.transpose(bank[4 + n % 4][:, t * P:(t + 1) * P], src[:, k * P:(k + 1) * P], ident)
                    n += 1
                    mm.then_inc(s_tpe, 1)
                pe.wait_ge(s_tpa, 4 * i + 4)
                pe.wait_ge(s_tpv, 4 * i + 4)
                z_unit(0, part)

            pe.wait_ge(s_bd, 16 * 12)
            pe.wait_ge(s_pv, 1)
            for m in range(2):
                for q, name in enumerate(("cos64", "sin64")):
                    mm = pe.matmul(bank[7][:, (2 * m + q) * P:(2 * m + q + 1) * P], K(name), wfb[:, m, :],
                                   start=True, stop=True)
            mm.then_inc(s_csw, 1)

            def gates(i):
                pe.wait_ge(s_conv, i + 1)
                for d in range(2):
                    for g in range(2):
                        for q, (a, w) in enumerate(GPARTS):
                            n = GUNITS.index((i, d, g, q))
                            if n >= 3:
                                pe.wait_ge(s_gu, n - 2)
                            pe.matmul(bank[4 + n % 3][:, 0:w], bdg[:, 2 * d + g, i, :], U[i % 2][:, a:a + w],
                                      start=True, stop=True).then_inc(s_g, 1)

            def mod_product(m, h):
                i = MORD.index(m) - 2
                pe.wait_ge(s_macc, i + 1)
                if i + h:
                    pe.wait_ge(s_mrow, 2 * i + h)
                pe.matmul(bank[7][:], ones, macc[:, h * HALF:(h + 1) * HALF], start=True,
                          stop=True).then_inc(s_m25, 1)

            MOD_AFTER = {3: [(2, 0)], 4: [(2, 1)], 6: [(5, 0)], 7: [(5, 1)], 8: [(3, 0)], 9: [(3, 1)],
                         11: [(4, 0), (4, 1)]}
            pe.wait_ge(s_cswc, 1)
            for n, ct in enumerate(COLT):
                if n:
                    z_tile(n)
                for m, h in MOD_AFTER.get(n, []):
                    mod_product(m, h)
                if ct in GATES_AFTER:
                    gates(GATES_AFTER[ct])

            NU = len(UNITS)
            pe.wait_ge(s_zu, NU)
            pe.wait_ge(s_pd, 2)
            for i in range(NT):
                u = NU + i
                pe.wait_ge(s_zu, u - 3)
                for m, zf in enumerate((zf0, zf1)):
                    mm = pe.matmul(bank[u % 4][:, m * 256:(m + 1) * 256], zf[:, i * P:(i + 1) * P], csw[:, m, :],
                                   start=True, stop=True)
                mm.then_inc(s_z, 1)

            pe.wait_ge(s_mrow, 8)
            pe.wait_ge(s_gu, len(GUNITS))
            for m in range(2):
                for h in range(2):
                    q = 2 * m + h
                    if q >= 2:
                        pe.wait_ge(s_py, q - 1)
                    pe.matmul(bank[6 + q % 2][:], wpb[:, m, :], yT[:, 4 + m, h * HALF:(h + 1) * HALF], start=True,
                              stop=True).then_inc(s_pm, 1)

            pe.wait_ge(s_zu, NU + NT)
            for k in range(NT):
                pe.wait_ge(s_dft[k % 3], 16 * (k // 3 + 1))
                for m in range(2):
                    pe.matmul(bank[4 + m][:, 0:1], Vf[:, k, m, 0:P], K("alt"), start=k == 0, stop=k == NT - 1)
                    pe.matmul(bank[m][:], Vf[:, k, m, 0:P], dring[:, k % 3, 0:HALF], start=k == 0, stop=k == NT - 1)
                    mm = pe.matmul(bank[2 + m][:], Vf[:, k, m, P:2 * P], dring[:, k % 3, HALF:], start=k == 0,
                                   stop=k == NT - 1)
                mm.then_inc(s_dftu, 1)

            def out_proj(t):
                for h in range(2):
                    u = 2 * t + h
                    if u >= 4:
                        pe.wait_ge(s_mixu, u - 3)
                    if u == 0:
                        pe.wait_ge(s_fc, 1)
                    for i, k in enumerate(K_ORDER):
                        if u == 0:
                            pe.wait_ge(s_spl, 1 + max(SPLIT.index(("w", k)), SPLIT.index(("y", k))))
                        cols, toks = slice(h * HALF, (h + 1) * HALF), slice(t * P, (t + 1) * P)
                        pe.matmul(bank[u % 4][:], y_hi[:, k, toks], w_hi[:, k, cols], start=i == 0, stop=False)
                        pe.matmul(bank[u % 4][:], y_hi[:, k, toks], w_lo[:, k, cols], start=False, stop=False)
                        mm = pe.matmul(bank[u % 4][:], y_lo[:, k, toks], w_hi[:, k, cols], start=False,
                                       stop=i == KD - 1)
                    mm.then_inc(s_mix, 1)

            def turn(t):
                pe.wait_ge(s_xn, t + 1)
                if t >= 1:
                    pe.wait_ge(s_h2, t)
                for k in range(KD):
                    mm = pe.transpose(bank[4 + k // 4][:, (k % 4) * P:(k % 4 + 1) * P], xs[t % 2][:, k * P:(k + 1) * P],
                                      ident)
                mm.then_inc(s_t2, 1)

            def logits(t):
                pe.wait_ge(s_h2, t + 1)
                if t >= 1:
                    pe.wait_ge(s_lg, t)
                for k in range(KD):
                    mm = pe.matmul(bank[6][:, 0:NG + NE], h2[:, k, :], rw[:, k, :], start=k == 0, stop=k == KD - 1)
                mm.then_inc(s_lgp, 1)

            for t in range(NT + 2):
                if t < NT:
                    out_proj(t)
                if t >= 2:
                    logits(t - 2)
                if 1 <= t <= NT:
                    turn(t - 1)

            pe.wait_ge(s_tri, 2)
            pe.wait_ge(s_mk, 1)
            mb = oh[:, 0, :]
            for i in range(NT):
                for j in range(i + 1):
                    pe.matmul(bank[4][:, NE * i:NE * (i + 1)], (tri_b if j == i else ones_b)[:],
                              mb[:, NE * j:NE * (j + 1)], start=j == 0, stop=j == i)
            for j in range(NT):
                mm = pe.matmul(bank[5][:, 0:NE], ones_b[:], mb[:, NE * j:NE * (j + 1)], start=j == 0,
                               stop=j == NT - 1)
            mm.then_inc(s_rk, 1)

            def slot_numbers(q, E1, first=False):
                pe.wait_ge(s_oh, q + 1)
                if not first or q:
                    pe.wait_ge(s_idf, q)
                for i in range(NT):
                    mm = pe.matmul(bank[2][:, 0:NFLD], oh[:, i, :],
                                   RV[:, E1, i, :] if isinstance(E1, int) else
                                   RV[:, bass.ds(E1, 1), i, :].rearrange("p a n -> p (a n)"),
                                   start=i == 0, stop=i == NT - 1)
                mm.then_inc(s_idx, 1)

            def turn_rows(q, r):
                if r == 0:
                    pe.wait_ge(s_xg, 16 * q + 16)
                for k in range(4):
                    kk = 4 * r + k
                    mm = pe.transpose(bank[(3, 6)[r]][:, k * P:(k + 1) * P], xg[:, kk * P:(kk + 1) * P], ident)
                mm.then_inc(s_xgt, 1)

            def gate_up(E, par, j):
                pe.wait_ge(s_logu[j], E + 1)
                order = [(g, kk) for kk in range(2) for g in range(2)] if j < KE - 1 else \
                    [(g, kk) for g in range(2) for kk in range(2)]
                for g, kk in order:
                    k, a = 2 * j + kk, g * D + kk * HALF
                    w_hi, w_lo = WP[:, j, 0, a:a + HALF], WP[:, j, 1, a:a + HALF]
                    x_hi, x_lo = xp[:, par, 0, k, :], xp[:, par, 1, k, :]
                    pe.matmul(bank[g][:], x_hi, w_hi, start=k == 0, stop=False)
                    pe.matmul(bank[g][:], x_hi, w_lo, start=False, stop=False)
                    mm = pe.matmul(bank[g][:], x_lo, w_hi, start=False, stop=k == KD - 1)
                    if g == 0 and k == KD - 1:
                        mm.then_inc(s_gate, 1)
                mm.then_inc(s_gud, 1)

            def turn_hidden(s, h):
                pe.wait_ge(s_hid, 2 * s + h + 1)
                for j in range(2 * h, 2 * h + 2):
                    mm = pe.transpose(bank[(7, 0)[h]][:, j * P:(j + 1) * P], sg[:, j * P:(j + 1) * P], ident)
                mm.then_inc(s_hT, 1)

            def down(s, E, j):
                pe.wait_ge(s_lod[j], E + 1)
                if j % 2 == 0:
                    pe.wait_ge(s_hps, 2 * s + j // 2 + 1)
                if j == 0:
                    pe.wait_ge(s_ye, 2 * s + 2)
                for h in range(2):
                    w_hi = WP[:, j, 0, 2 * D + h * HALF:2 * D + (h + 1) * HALF]
                    w_lo = WP[:, j, 1, 2 * D + h * HALF:2 * D + (h + 1) * HALF]
                    pe.matmul(bank[4 + h][:], hp[:, 0, j, :], w_hi, start=j == 0, stop=False)
                    pe.matmul(bank[4 + h][:], hp[:, 0, j, :], w_lo, start=False, stop=False)
                    mm = pe.matmul(bank[4 + h][:], hp[:, 1, j, :], w_hi, start=False, stop=j == KE - 1)
                mm.then_inc(s_dd, 1)

            slot_numbers(0, 0, first=True)
            pe.wait_ge(s_tab, 1)
            W = pe.value_load(tab[0:1, 3, 0:1], min_val=NE, max_val=MAXT)
            slot_numbers(1, pe.value_load(tab[0:1, 0, 1:2], min_val=0, max_val=NE - 1))
            for r in range(2):
                turn_rows(0, r)
            with pe.Fori(0, MAXT // 2) as it:
                for par in range(2):
                    with pe.If(2 * it + par < W):
                        s = 2 * it + par
                        E = pe.value_load(tab[0:1, 0, bass.ds(s, 1)], min_val=0, max_val=NE - 1)
                        E2 = pe.value_load(tab[0:1, 0, bass.ds(s + 2, 1)], min_val=0, max_val=NE - 1)
                        pe.wait_ge(s_xgr, 2 * s + 2)
                        gate_up(E, par, 0)
                        gate_up(E, par, 1)
                        gate_up(E, par, 2)
                        gate_up(E, par, 3)
                        turn_rows(s + 1, 0)
                        turn_rows(s + 1, 1)
                        turn_hidden(s, 0)
                        turn_hidden(s, 1)
                        slot_numbers(s + 2, E2)
                        for j in range(KE):
                            down(s, E, j)

        @block.scalar
        def _(act):
            A_ = act.activation
            xv = x[0].rearrange("(t p) d -> p t d", p=P)
            act.wait_ge(s_prow, 16 * (len(PV) + 1))
            act.dma_start(ctxt[:], ctx[0].rearrange("(t p) d -> p t d", p=P)).then_inc(s_x[0], 16)
            act.wait_ge(s_pv, 1)
            A_(silu_c[:].rearrange("p a k -> p (a k)"), pv[:, 0:2 * KD], ACT.Tanh, scale=0.5).then_inc(s_sil, 1)
            act.wait_ge(s_lam, 1)
            A_(lamw[:, 1], lamw[:, 0], ACT.Exp, scale=-1.0).then_inc(s_lame, 1)
            def squares(b):
                act.wait_ge(s_x[b], 16)
                for t in XPARTS[b]:
                    src = ctxt[:, t] if t < NC_ else xt[:, t - NC_]
                    if t >= 2:
                        act.wait_ge(s_ss, t - 1)
                    A_(AA[t % 2][:, 0:D], src, ACT.Square, accum_out=stat[:, t:t + 1]).then_inc(s_ss, 1)
                act.wait_ge(s_ms, b + 1)
                cols = stat[:, XPARTS[b][0]:XPARTS[b][-1] + 1]
                A_(cols, cols, ACT.Sqrt).then_inc(s_sq, 1)

            def h_units(part):
                for n in range(part * KD, (part + 1) * KD, 2):
                    k, g = n % KD, 1 if part == 0 else 0
                    dst = hTc[:, k, :] if part == 0 else hT[:, k, (part - 1) * HALF:part * HALF]
                    act.wait_ge(s_tpe, n + 1)
                    A_(dst, bank[4 + n % 4][:, 0:CTX if part == 0 else HALF], ACT.Identity, scale=sc_mix[:, k, g:g + 1],
                       bias=sh_mix[:, k, g:g + 1]).then_inc(s_tpa, 1)

            for b in range(2):
                act.wait_ge(s_modu, 2 * b + 2)
                act.dma_start(xt[:, 4 * b:4 * b + 4], xv[:, 4 * b:4 * b + 4]).then_inc(s_x[b + 1], 16)
                squares(b)
            for q in range(4):
                act.wait_ge(s_modu, 2 * q + 2)
                A_(mrow[:, q * HALF:(q + 1) * HALF], bank[q][0:2, :], ACT.Copy).then_inc(s_mcol, 1)
            act.wait_ge(s_scsh, 1)
            h_units(0)
            squares(2)
            h_units(1)
            h_units(2)
            act.wait_ge(s_csw, 1)
            A_(csw[:].rearrange("p m n -> p (m n)"), bank[7][:], ACT.Copy).then_inc(s_cswc, 1)

            def take_x(i):
                if i == 0:
                    act.wait_ge(s_zp, 1)
                else:
                    act.wait_ge(s_conv, i)
                if i >= 2:
                    act.wait_ge(s_y, i - 1)
                for part in ("c", 0, 1):
                    u = UNIT[(("x", i), part)]
                    act.wait_ge(s_z, u + 1)
                    w = CTX if part == "c" else HALF
                    zo = 2 if part == "c" else CTX + 5 + part * HALF
                    uo = 0 if part == "c" else CTX + part * HALF
                    A_(zpad[:, zo:zo + w], bank[u % 4][:, 0:w], ACT.Copy)
                    A_(U[i % 2][:, uo:uo + w], bank[u % 4][:, 0:w], ACT.Identity, scale=V("convw", 2 * NI + i),
                       bias=V("convb", i)).then_inc(s_zu, 1)

            def take_g(i):
                if i >= 2:
                    act.wait_ge(s_y, i - 1)
                if i >= 1:
                    act.wait_ge(s_gel, i)
                for part in (0, 1):
                    u = UNIT[(("g", i), part)]
                    act.wait_ge(s_z, u + 1)
                    A_(gz[i % 2][:, part * HALF:(part + 1) * HALF], bank[u % 4][:], ACT.Copy)
                    A_(gt[:, part * HALF:(part + 1) * HALF], bank[u % 4][:], ACT.Square).then_inc(s_zu, 1)

            def gelu_tanh(i):
                act.wait_ge(s_gp, i + 1)
                A_(gt[:], gt[:], ACT.Tanh, scale=GELU_C).then_inc(s_gth, 1)

            def take_p(m):
                for part in (0, 1):
                    u = UNIT[(("p", m), part)]
                    act.wait_ge(s_z, u + 1)
                    A_(yT[:, 4 + m, part * HALF:(part + 1) * HALF], bank[u % 4][:], ACT.Copy).then_inc(s_zu, 1)

            def take_f(m):
                if m == 0:
                    act.wait_ge(s_m25, 8)
                else:
                    act.wait_ge(s_conv, NI)
                for part in (0, 1):
                    u = UNIT[(("f", m), part)]
                    act.wait_ge(s_z, u + 1)
                    A_((zf0, zf1)[m][:, part * HALF:(part + 1) * HALF], bank[u % 4][:], ACT.Copy).then_inc(s_zu, 1)

            def rec_gates(i):
                if i >= 1:
                    act.wait_ge(s_y, i)
                else:
                    act.wait_ge(s_lamc, 1)
                for d in range(2):
                    for g in range(2):
                        for q, (a, w) in enumerate(GPARTS):
                            n = GUNITS.index((i, d, g, q))
                            act.wait_ge(s_g, n + 1)
                            A_((RH, IH)[g][d][:, a:a + w], bank[4 + n % 3][:, 0:w], ACT.Tanh, scale=0.5,
                               bias=hb_[:, 2 * d + g, i:i + 1]).then_inc(s_gu, 1)
                    act.wait_ge(s_gu, GUNITS.index((i, d, 1, 2)) + 1)
                    A_(AA[d][:], RH[d][:], ACT.Exp, scale=lamw[:, 5, d * NI + i:d * NI + i + 1],
                       bias=lamw[:, 5, d * NI + i:d * NI + i + 1])
                    A_(RH[d][:], RH[d][:], ACT.Tanh, scale=lamw[:, 4, d * NI + i:d * NI + i + 1],
                       bias=lamw[:, 4, d * NI + i:d * NI + i + 1]).then_inc(s_ra, 1)

            def rec_root(i):
                for d in range(2):
                    act.wait_ge(s_rm, 2 * i + d + 1)
                    A_(RH[d][:], RH[d][:], ACT.Sqrt, scale=0.25).then_inc(s_rr, 1)

            take_x(0)
            take_g(0)
            gelu_tanh(0)
            take_p(0)
            rec_gates(0)
            take_x(1)
            rec_root(0)
            take_g(1)
            gelu_tanh(1)
            take_p(1)
            rec_gates(1)
            take_x(2)
            rec_root(1)
            take_g(2)
            gelu_tanh(2)
            rec_gates(2)
            take_x(3)
            rec_root(2)
            take_g(3)
            gelu_tanh(3)
            rec_gates(3)
            rec_root(3)
            take_f(0)
            take_f(1)
            NU = len(UNITS)
            for i in range(NT):
                act.wait_ge(s_z, NU + i + 1)
                A_(Vf[:, i].rearrange("p m n -> p (m n)"), bank[(NU + i) % 4][:], ACT.Copy).then_inc(s_zu, 1)
            for q in range(4):
                m, h = q // 2, q % 2
                act.wait_ge(s_pm, q + 1)
                A_(yT[:, 4 + m, h * HALF:(h + 1) * HALF], bank[6 + q % 2][:], ACT.Copy, scale=V("psc", m)).then_inc(s_py, 1)

            def split_hi(i):
                what, k = SPLIT[i]
                if what == "w":
                    act.wait_ge(s_wout[k // 4], 16)
                    if k >= 3:
                        act.wait_ge(s_scr, 1)
                    A_(w_hi[:, k, :], wout_sb[:, k, :], ACT.Copy).then_inc(s_sph, 1)
                else:
                    if 4 <= k < 6:
                        act.wait_ge(s_py, 2 * (k - 4) + 2)
                    if k >= 5:
                        act.wait_ge(s_fy, 2)
                    A_(y_hi[:, k, :], yT[:, k, :], ACT.Copy).then_inc(s_sph, 1)

            act.wait_ge(s_y, NI)
            act.wait_ge(s_z, NU + NT)
            for i in range(EARLY):
                split_hi(i)
            act.wait_ge(s_dftu, NT)
            for m in range(2):
                A_((gt, Q)[m][:, 0:HALF], bank[m][:], ACT.Copy).then_inc(s_fc, 1)
            for i in range(EARLY, 2 * KD):
                split_hi(i)

            for t in range(NT):
                act.wait_ge(s_x1, t + 1)
                A_(xm[t % 2][:], xr[t % NX][:], ACT.Square, accum_out=stat[:, 10 + t:11 + t]).then_inc(s_ss2, 1)
                act.wait_ge(s_ms2, t + 1)
                A_(stat[:, 18 + t:19 + t], stat[:, 10 + t:11 + t], ACT.Sqrt).then_inc(s_rt2, 1)
                act.wait_ge(s_t2, t + 1)
                if t >= 1:
                    act.wait_ge(s_lgp, t)
                for h in range(2):
                    ins = A_(h2[:, 4 * h:4 * h + 4, :], bank[4 + h][:].rearrange("p (k n) -> p k n", n=P), ACT.Copy)
                ins.then_inc(s_h2, 1)

            act.wait_ge(s_e1, 1)
            A_(R_["d"], R_["d"], ACT.Exp).then_inc(s_e2, 1)
            act.wait_ge(s_e1, 2)
            A_(R_["ex"], R_["ex"], ACT.Exp).then_inc(s_e2, 1)

            def hi_gate_up(e1, j):
                act.wait_ge(s_rgu[j], 32 * e1 + 32)
                A_(WP[:, j, 0, 0:2 * D], raw[:, j, 0:2 * D], ACT.Copy).then_inc(s_hgu, 1)

            def hi_down(e1, j):
                act.wait_ge(s_rdn[j], 16 * e1 + 16)
                A_(WP[:, j, 0, 2 * D:], raw[:, j, 2 * D:], ACT.Copy).then_inc(s_hdn, 1)

            def hi_rows(q, p2, r):
                act.wait_ge(s_xgt, 2 * q + r + 1)
                A_(xp[:, p2, 0, 4 * r:4 * r + 4, :], bank[(3, 6)[r]][:].rearrange("p (k n) -> p k n", n=P),
                   ACT.Copy).then_inc(s_xgh, 1)

            for n in range(2):
                act.sem_inc(s_ys[n], 16)
            for j in range(KE):
                hi_gate_up(0, j)
            for r in range(2):
                hi_rows(0, 0, r)
            for j in range(KE):
                hi_down(0, j)
            act.wait_ge(s_tab, 1)
            W = act.value_load(tab[0:1, 3, 0:1], min_val=NE, max_val=MAXT)
            with act.Fori(0, MAXT // 2) as it:
                for par in range(2):
                    with act.If(2 * it + par < W):
                        s = 2 * it + par
                        L = act.value_load(tab[0:1, 2, bass.ds(s, 1)], min_val=0, max_val=1)
                        E1 = act.value_load(tab[0:1, 0, bass.ds(s + 1, 1)], min_val=0, max_val=NE - 1)
                        with act.If(L > 0):
                            for j in range(2):
                                act.wait_ge(s_gud, 4 * s + j + 1)
                                hi_gate_up(E1, j)
                        act.wait_ge(s_gate, s + 1)
                        A_(sg[:], bank[0][:], ACT.Tanh, scale=0.5).then_inc(s_sg, 1)
                        for h in range(2):
                            act.wait_ge(s_hT, 2 * s + h + 1)
                            A_(hp[:, 0, 2 * h:2 * h + 2, :],
                               bank[(7, 0)[h]][:, h * 2 * P:(h + 1) * 2 * P].rearrange("p (k n) -> p k n", n=P),
                               ACT.Copy).then_inc(s_hfr, 1)
                        for r in range(2):
                            hi_rows(s + 1, 1 - par, r)
                        with act.If(L > 0):
                            act.wait_ge(s_gud, 4 * s + 4)
                            for j in range(2, KE):
                                hi_gate_up(E1, j)
                            for j in range(KE):
                                act.wait_ge(s_dd, 4 * s + j + 1)
                                hi_down(E1, j)
                        act.wait_ge(s_ye, 2 * s + 4)
                        act.dma_start(y_d[bass.ds(s, 1)].rearrange("a p d -> (a p) d"),
                                      ysc[:, par, :]).then_inc(s_ys[par], 16)

            for t in range(NT):
                act.wait_ge(s_fx1, t + 1)
                if t >= 2:
                    act.wait_ge(s_fs, t - 1)
                A_(fj[t % 2][:], fx[:, t], ACT.Square, accum_out=stat[:, 28 + t:29 + t]).then_inc(s_fs, 1)
                act.wait_ge(s_fm, t + 1)
                A_(stat[:, 36 + t:37 + t], stat[:, 28 + t:29 + t], ACT.Sqrt).then_inc(s_fr, 1)

        @block.vector
        def _(dve):
            chain = [0]

            def link(ins):
                chain[0] += 1
                ins.then_inc(s_dv, 1)
                dve.wait_ge(s_dv, chain[0])

            tt, ts, stt = dve.tensor_tensor, dve.tensor_scalar, dve.scalar_tensor_tensor
            dve.wait_ge(s_pvp, 1)
            link(dve.tensor_copy(pv[:], bank[7][:, 0:NPV]))
            lamv = V("lam")
            link(ts(lamw[:, 2], lamv, -1.0, None, ALU.mult))
            link(tt(lamw[:, 0], lamw[:, 2], lamv, ALU.max))
            ts(lamw[:, 2], lamw[:, 2], 0.0, None, ALU.max).then_inc(s_lam, 1)
            for d in range(2):
                ts(hb_[:, 2 * d], V("ba")[:, d * NI:(d + 1) * NI], 0.5, None, ALU.mult)
                ts(hb_[:, 2 * d + 1], V("bx")[:, d * NI:(d + 1) * NI], 0.5, None, ALU.mult)
            link(dve.memset(stat[:], 0.0))
            dve.memset(stat[:, 62:63], 0.0).then_inc(s_pv, 1)
            dve.wait_ge(s_sil, 1)
            sc_ = silu_c[:].rearrange("p a k -> p (a k)")
            link(stt(out=sc_, in0=sc_, scalar=1.0, in1=pv[:, 0:2 * KD], op0=ALU.add, op1=ALU.mult))
            ts(sc_, sc_, 0.5, None, ALU.mult).then_inc(s_silu, 1)
            dve.wait_ge(s_lame, 1)
            e_, s2_, p_, s_ = lamw[:, 1], lamw[:, 3], lamw[:, 4], lamw[:, 5]
            link(ts(s_, e_, 2.0, None, ALU.add))
            link(dve.reciprocal(s_, s_))
            link(tt(s_, s_, e_, ALU.mult))
            link(tt(s2_, s_, s_, ALU.mult))
            link(dve.memset(p_, 0.0))
            for n in range(19, 1, -2):
                link(stt(out=p_, in0=p_, scalar=1.0 / n, in1=s2_, op0=ALU.add, op1=ALU.mult))
            link(stt(out=p_, in0=p_, scalar=1.0, in1=s_, op0=ALU.add, op1=ALU.mult))
            link(stt(out=p_, in0=p_, scalar=2.0, in1=lamw[:, 2], op0=ALU.mult, op1=ALU.add))
            link(ts(p_, p_, 1e-25, None, ALU.max))
            ts(s_, p_, -4.0, None, ALU.mult)
            ts(p_, p_, 4.0, None, ALU.mult).then_inc(s_lamc, 1)

            def scale_rows(b):
                tiles = XPARTS[b]
                cols = stat[:, tiles[0]:tiles[-1] + 1]
                dve.wait_ge(s_ss, tiles[-1] + 1)
                ts(cols, cols, 1.0 / D, EPS, ALU.mult, ALU.add).then_inc(s_ms, 1)
                dve.wait_ge(s_sq, b + 1)
                link(dve.reciprocal(cols, cols))
                for t in tiles:
                    src = ctxt[:, t] if t < NC_ else xt[:, t - NC_]
                    ts(src, src, stat[:, t:t + 1], None, ALU.mult).then_inc(s_xs, 1)

            def h_units(part):
                for n in range(part * KD + 1, (part + 1) * KD, 2):
                    k, g = n % KD, 1 if part == 0 else 0
                    dst = hTc[:, k, :] if part == 0 else hT[:, k, (part - 1) * HALF:part * HALF]
                    dve.wait_ge(s_tpe, n + 1)
                    ts(dst, bank[4 + n % 4][:, 0:CTX if part == 0 else HALF], sc_mix[:, k, g:g + 1],
                       sh_mix[:, k, g:g + 1], ALU.mult, ALU.add).then_inc(s_tpv, 1)

            scale_rows(0)
            scale_rows(1)
            dve.wait_ge(s_mtr, 1)
            m01 = bank[6][:, 0:4 * KD].rearrange("p (j g) -> p j g", g=2)
            mb_ = V("modb").unsqueeze(2)
            tt(sh_mix[:], m01[:, 0:KD], mb_[:, 0:KD].to_broadcast([P, KD, 2]), ALU.add)
            link(tt(sc_mix[:], m01[:, KD:2 * KD], mb_[:, KD:2 * KD].to_broadcast([P, KD, 2]), ALU.add))
            stt(out=sc_mix[:], in0=sc_mix[:], scalar=1.0, in1=V("gmix").unsqueeze(2).to_broadcast([P, KD, 2]),
                op0=ALU.add, op1=ALU.mult).then_inc(s_scsh, 1)
            dve.wait_ge(s_scsh, 1)
            h_units(0)
            scale_rows(2)
            h_units(1)
            h_units(2)

            def conv(i):
                dve.wait_ge(s_zu, UNIT[(("x", i), 1)] + 1)
                for a, b, w in ((0, 0, CTX), (CTX, CTX + 3, SEQ)):
                    u = U[i % 2][:, a:a + w]
                    for tap in (0, 1, 3):
                        ins = stt(out=u, in0=zpad[:, b + tap:b + tap + w], scalar=V("convw", tap * NI + i), in1=u,
                                  op0=ALU.mult, op1=ALU.add)
                        if tap != 3:
                            link(ins)
                ins.then_inc(s_conv, 1)

            def gelu_poly(i):
                dve.wait_ge(s_zu, UNIT[(("g", i), 1)] + 1)
                link(ts(gt[:], gt[:], 0.044715, 1.0, ALU.mult, ALU.add))
                tt(gt[:], gt[:], gz[i % 2][:], ALU.mult).then_inc(s_gp, 1)

            def gelu_end(i):
                dve.wait_ge(s_gth, i + 1)
                stt(out=gz[i % 2][:], in0=gt[:], scalar=1.0, in1=gz[i % 2][:], op0=ALU.add,
                    op1=ALU.mult).then_inc(s_gel, 1)

            def rec_input(i):
                for d in range(2):
                    dve.wait_ge(s_ra, 2 * i + d + 1)
                    stt(out=IH[d][:], in0=IH[d][:], scalar=1.0, in1=U[i % 2][:], op0=ALU.add, op1=ALU.mult)
                    if d:
                        dve.wait_ge(s_rm, 2 * i + 1)
                    link(tt(Q[:], AA[d][:], AA[d][:], ALU.mult))
                    stt(out=RH[d][:], in0=Q[:], scalar=1.0, in1=RH[d][:], op0=ALU.add, op1=ALU.mult).then_inc(s_rm, 1)

            def rec_scan(i):
                for d in range(2):
                    dve.wait_ge(s_rr, 2 * i + d + 1)
                    link(tt(IH[d][:], IH[d][:], RH[d][:], ALU.mult))
                    if d == 0:
                        link(dve.tensor_tensor_scan(RH[0][:], AA[0][:], IH[0][:], 0.0, ALU.mult, ALU.add))
                    else:
                        r = lambda b_, lo, hi: b_[:, lo:hi][:, ::-1]
                        link(dve.tensor_tensor_scan(r(RH[1], 0, CTX), r(AA[1], 0, CTX), r(IH[1], 0, CTX), 0.0,
                                                    ALU.mult, ALU.add))
                        link(dve.tensor_tensor_scan(r(RH[1], CTX, TOT), r(AA[1], CTX, TOT), r(IH[1], CTX, TOT),
                                                    RH[1][:, 0:1], ALU.mult, ALU.add))
                link(tt(RH[0][:, CTX:], RH[0][:, CTX:], RH[1][:, CTX:], ALU.add))
                stt(out=yT[:, i, :], in0=gz[i % 2][:], scalar=0.5, in1=RH[0][:, CTX:], op0=ALU.mult,
                    op1=ALU.mult).then_inc(s_y, 1)

            def mod_sums(m):
                for q in range(MCH):
                    n = MORD.index(m) * MCH + q
                    dve.wait_ge(s_mod[mod_slot(n)], 16 * mod_fill(n))
                    dst = macc[:, q * 256:(q + 1) * 256]
                    for k in range(KD):
                        ck = silu_c[:, 0, k:k + 1]
                        if k == 0:
                            link(ts(dst, mring[:, n % 2, k, :], ck, None, ALU.mult))
                        else:
                            ins = stt(out=dst, in0=mring[:, n % 2, k, :], scalar=ck, in1=dst, op0=ALU.mult,
                                      op1=ALU.add)
                            if k < KD - 1:
                                link(ins)
                    ins.then_inc(s_modv, 1)
                    dve.wait_ge(s_modv, n + 1 - 2 * MCH)
                dve.memset(stat[:, 62:63], 0.0).then_inc(s_macc, 1)

            def mod_end(m, h):
                i = MORD.index(m) - 2
                g = {2: g2, 5: g5, 3: shr, 4: scr}[m]
                dve.wait_ge({2: s_gb2, 5: s_gb5, 3: s_gb3, 4: s_gb3}[m], 16 if m in (2, 5) else 32)
                dve.wait_ge(s_m25, 2 * i + h + 1)
                tt(g[:, h * HALF:(h + 1) * HALF], g[:, h * HALF:(h + 1) * HALF], bank[7][:], ALU.add).then_inc(s_mrow, 1)
                if (m, h) == (4, 1):
                    dve.wait_ge(s_mrow, 8)
                    dve.wait_ge(s_gff, 16)
                    stt(out=scr[:], in0=scr[:], scalar=1.0, in1=gff[:], op0=ALU.add, op1=ALU.mult).then_inc(s_scr, 1)

            conv(0)
            gelu_poly(0)
            mod_sums(2)
            gelu_end(0)
            rec_input(0)
            for i, (m, m_next) in enumerate(((2, 5), (5, 3), (3, 4))):
                conv(i + 1)
                mod_end(m, 0)
                rec_scan(i)
                gelu_poly(i + 1)
                mod_end(m, 1)
                mod_sums(m_next)
                gelu_end(i + 1)
                rec_input(i + 1)
            rec_scan(3)
            mod_end(4, 0)
            mod_end(4, 1)

            def split_lo(i):
                what, k = SPLIT[i]
                src, hi, lo = (wout_sb, w_hi, w_lo) if what == "w" else (yT, y_hi, y_lo)
                dve.wait_ge(s_sph, i + 1)
                tt(lo[:, k, :], src[:, k, :], hi[:, k, :].bitcast(F32), ALU.subtract).then_inc(s_spl, 1)

            for i in range(EARLY):
                split_lo(i)
            for m in range(2):
                dve.wait_ge(s_fc, m + 1)
                cs = (gt, Q)[m]
                tt(yT[:, 6 + m, 0:HALF], cs[:, 0:HALF], bank[2 + m][:], ALU.add)
                tt(yT[:, 6 + m, HALF + 1:SEQ][:, ::-1], cs[:, 1:HALF], bank[2 + m][:, 1:HALF], ALU.subtract)
                dve.tensor_copy(yT[:, 6 + m, HALF:HALF + 1], bank[4 + m][:, 0:1]).then_inc(s_fy, 1)

            for i in range(EARLY, 2 * KD):
                split_lo(i)

            for t in range(NT + 1):
                if t < NT:
                    xb, tmp = xr[t % NX], xm[t % 2]
                    dve.wait_ge(s_xr[t % NX], 16 * (t // NX + 1))
                    for h in range(2):
                        dve.wait_ge(s_mix, 2 * t + h + 1)
                        tt(tmp[:, h * HALF:(h + 1) * HALF], bank[(2 * t + h) % 4][:], g2[:, h * HALF:(h + 1) * HALF],
                           ALU.mult).then_inc(s_mixu, 1)
                    dve.wait_ge(s_mixu, 2 * t + 2)
                    tt(xb[:], xb[:], tmp[:], ALU.add).then_inc(s_x1, 1)
                    dve.wait_ge(s_ss2, t + 1)
                    ts(stat[:, 10 + t:11 + t], stat[:, 10 + t:11 + t], 1.0 / D, EPS, ALU.mult,
                       ALU.add).then_inc(s_ms2, 1)
                    dve.wait_ge(s_rt2, t + 1)
                    link(dve.reciprocal(stat[:, 18 + t:19 + t], stat[:, 18 + t:19 + t]))
                    if t >= 2:
                        dve.wait_ge(s_xnd[t % 2], 16 * (t // 2))
                        dve.wait_ge(s_t2, t - 1)
                    link(stt(out=xs[t % 2][:], in0=xb[:], scalar=stat[:, 18 + t:19 + t], in1=scr[:], op0=ALU.mult,
                             op1=ALU.mult))
                    tt(xs[t % 2][:], xs[t % 2][:], shr[:], ALU.add).then_inc(s_xn, 1)
                if t >= 1:
                    if t == 1:
                        dve.wait_ge(s_rw, 64)
                    dve.wait_ge(s_lgp, t)
                    tt(LG[:, t - 1, :], bank[6][:, 0:NG + NE], rb[:], ALU.add).then_inc(s_lg, 1)

            dve.wait_ge(s_lg, NT)
            lg, le = LG[:, :, 0:NG], LG[:, :, NG:].rearrange("p t (g j) -> p t g j", g=NG)
            f4 = K("first4").unsqueeze(1).to_broadcast([P, NT, 4])

            def b4(a):
                return a.unsqueeze(2).to_broadcast([P, NT, 4])

            def first_max(src, mx, hot, key, km):
                link(dve.tensor_reduce(mx, src, AX.X, ALU.max))
                link(tt(key, src, b4(mx), ALU.is_equal))
                link(tt(key, key, f4, ALU.mult))
                link(dve.tensor_reduce(km, key, AX.X, ALU.max))
                link(tt(hot, key, b4(km), ALU.is_equal))

            first_max(lg, R_["m"], R_["goh"], R_["key"], R_["km"])
            tt(R_["d"], lg, b4(R_["m"]), ALU.subtract).then_inc(s_e1, 1)
            link(tt(R_["big"], le, R_["goh"].unsqueeze(3).to_broadcast([P, NT, NG, EPG]), ALU.mult))
            link(dve.tensor_reduce(R_["les"], R_["big"].rearrange("p t g j -> p t j g"), AX.X, ALU.add))
            first_max(R_["les"], R_["m1"], R_["oh1"], R_["key"], R_["km"])
            link(stt(out=R_["les"], in0=R_["oh1"], scalar=-3e38, in1=R_["les"], op0=ALU.mult, op1=ALU.add))
            first_max(R_["les"], R_["m2"], R_["oh2"], R_["key"], R_["km"])
            tt(R_["ex"], R_["m2"], R_["m1"], ALU.subtract).then_inc(s_e1, 1)
            dve.wait_ge(s_e2, 1)
            link(dve.tensor_reduce(R_["pg"], R_["d"], AX.X, ALU.add))
            dve.wait_ge(s_e2, 2)
            link(ts(R_["w1"], R_["ex"], 1.0, None, ALU.add))
            link(tt(R_["w1"], R_["w1"], R_["pg"], ALU.mult))
            link(ts(R_["w1"], R_["w1"], 2.0, None, ALU.mult))
            link(dve.reciprocal(R_["w1"], R_["w1"]))
            link(tt(R_["w2"], R_["w1"], R_["ex"], ALU.mult))
            M1, M2, G = R_["M1"], R_["M2"], R_["G"]
            g_b = R_["goh"].unsqueeze(3).to_broadcast([P, NT, NG, EPG])
            for M_, o_, w_ in ((M1, "oh1", "w1"), (M2, "oh2", "w2")):
                link(dve.tensor_copy(R_["big"], R_[o_].unsqueeze(2).to_broadcast([P, NT, NG, EPG])))
                link(tt(M_, R_["big"], g_b, ALU.mult))
            m16 = lambda a: a.rearrange("p t g j -> p t (g j)")
            w16 = lambda a: a.unsqueeze(2).to_broadcast([P, NT, NE])
            link(tt(m16(G), m16(M1), w16(R_["w1"]), ALU.mult))
            link(tt(m16(R_["big"]), m16(M2), w16(R_["w2"]), ALU.mult))
            link(tt(G, G, R_["big"], ALU.add))
            link(tt(M1, M1, M2, ALU.add))
            dve.tensor_copy(oh[:, 0, :].rearrange("p (t e) -> p t e", e=NE), m16(M1)).then_inc(s_mk, 1)
            ge = G.rearrange("p t g j -> p (g j) t")
            rem = R_["rem"]
            dve.tensor_copy(RV[:, :, :, 0], K("pidx").unsqueeze(2).to_broadcast([P, NE, NT]))
            dve.tensor_copy(RV[:, :, :, 1], K("tok0").unsqueeze(1).to_broadcast([P, NE, NT]))
            link(dve.tensor_copy(RV[:, :, :, 2], ge))
            link(tt(rem, ge, RV[:, :, :, 2], ALU.subtract))
            link(dve.tensor_copy(RV[:, :, :, 3], rem))
            link(tt(rem, rem, RV[:, :, :, 3], ALU.subtract))
            link(dve.tensor_copy(RV[:, :, :, 4], rem))
            dve.wait_ge(s_rk, 1)
            rk = bank[4][:, 0:P].rearrange("p (t e) -> p e t", e=NE)
            me = M1.rearrange("p t g j -> p (g j) t")
            link(stt(out=RK[:], in0=rk, scalar=1.0, in1=me, op0=ALU.add, op1=ALU.mult))
            link(ts(RK[:], RK[:], -1.0, None, ALU.add))

            row = lambda a, n: rs[0:1, a:a + n]
            every = lambda a, n: rs[:, a:a + n]
            cnt, nt_, inc, sq_ = every(1200, NE), every(1216, NE), every(1232, NE), every(1248, NE)
            t7 = every(0, NE * 7).rearrange("p (e k) -> p e k", k=7)
            link(dve.tensor_copy(cnt, bank[5][:, 0:NE]))
            link(tt(t7, cnt.unsqueeze(2).to_broadcast([P, NE, 7]), K("tcount").unsqueeze(1).to_broadcast([P, NE, 7]),
                    ALU.is_gt))
            link(dve.tensor_reduce(nt_, t7, AX.X, ALU.add))
            link(ts(nt_, nt_, 1.0, None, ALU.add))
            link(dve.tensor_tensor_scan(inc, K("ones")[:, 0:NE], nt_, 0.0, ALU.mult, ALU.add))
            link(tt(sq_, inc, nt_, ALU.subtract))
            sq_all = sq_
            inc, sq_ = inc[0:1], sq_[0:1]
            big = row(1800, TAB * NE).rearrange("p (s e) -> p s e", e=NE)
            eT, mT, lT = row(1264, TAB), row(1300, TAB), row(1340, TAB)
            sq_b = sq_.unsqueeze(1).to_broadcast([1, TAB, NE])
            link(tt(big, sq_b, K("sidx")[0:1].unsqueeze(2).to_broadcast([1, TAB, NE]), ALU.is_le))
            link(dve.tensor_reduce(eT, big, AX.X, ALU.add))
            link(ts(eT, eT, -1.0, None, ALU.add))
            link(tt(big, big, sq_b, ALU.mult))
            link(dve.tensor_reduce(mT, big, AX.X, ALU.max))
            link(tt(mT, K("sidx")[0:1], mT, ALU.subtract))
            link(dve.memset(lT, 0.0))
            link(tt(lT[:, 0:TAB - 1], eT[:, 1:TAB], eT[:, 0:TAB - 1], ALU.subtract))
            pr = row(1400, MAXT // 2)
            link(ts(pr, K("slot0")[0:1, 0:MAXT // 2], 2.0 / P, None, ALU.mult))
            link(tt(pr, pr, inc[:, NE - 1:NE].to_broadcast([1, MAXT // 2]), ALU.is_lt))
            link(dve.tensor_reduce(row(1440, 1), pr, AX.X, ALU.add))
            link(ts(row(1440, 1), row(1440, 1), 2.0, None, ALU.mult))
            link(dve.tensor_copy(tab[0:1, 0, :], eT))
            link(dve.tensor_copy(tab[0:1, 1, :], mT))
            link(dve.tensor_copy(tab[0:1, 2, :], lT))
            link(dve.tensor_copy(tab[0:1, 3, 0:1], inc[:, NE - 1:NE]))
            link(stt(out=row(1450, 1), in0=inc[:, NE - 1:NE], scalar=2.0, in1=row(1440, 1), op0=ALU.mult,
                     op1=ALU.subtract))
            link(dve.tensor_copy(tab[0:1, 3, 2:3], row(1450, 1)))
            dve.tensor_copy(tab[0:1, 3, 1:2], row(1440, 1)).then_inc(s_tab, 1)
            dve.wait_ge(s_tab, 1)

            def lo_gate_up(e1, j):
                dve.wait_ge(s_hgu, 4 * e1 + j + 1)
                tt(WP[:, j, 1, 0:2 * D], raw[:, j, 0:2 * D], WP[:, j, 0, 0:2 * D].bitcast(F32),
                   ALU.subtract).then_inc(s_logu[j], 1)

            NLINK = 2

            def plink(q, ins, k):
                ins.then_inc(s_pch, 1)
                dve.wait_ge(s_pch, NLINK * q + k)

            def prepare_slots(q, E1, T1):
                rk1 = RK[:, E1, :] if isinstance(E1, int) else RK[:, bass.ds(E1, 1), :].rearrange("p a n -> p (a n)")
                s0 = K("slot0")[:, 0:1] if isinstance(T1, int) else K("slot0")[:, bass.ds(T1, 1)]
                plink(q, ts(rkt[:], rk1, s0, None, ALU.subtract), 1)
                if not isinstance(q, int) or q:
                    dve.wait_ge(s_idx, q)
                tt(oh[:], K("iota").unsqueeze(1).to_broadcast([P, NT, P]),
                   rkt[:].unsqueeze(2).to_broadcast([P, NT, P]), ALU.is_equal).then_inc(s_oh, 1)

            def slot_ids(q):
                dve.wait_ge(s_idx, q + 1)
                if not isinstance(q, int) or q:
                    dve.wait_ge(s_pch, NLINK * q)
                dve.tensor_copy(idf[:, 0:NFLD], bank[2][:, 0:NFLD]).then_inc(s_idf, 1)
                dve.wait_ge(s_idf, q + 1)
                if not isinstance(q, int) or q:
                    dve.wait_ge(s_xg, 16 * q)
                tt(idg[:], idf[:, 0:1], idf[:, 1:2], ALU.add).then_inc(s_ids, 1)

            def slot_gates(q, p2):
                dve.tensor_reduce(gcol[:, p2], idf[:, 2:5], AX.X, ALU.add).then_inc(s_pch, 1)

            def lo_rows(q, p2, r):
                dve.wait_ge(s_xgh, 2 * q + r + 1)
                tt(xp[:, p2, 1, 4 * r:4 * r + 4, :], bank[(3, 6)[r]][:].rearrange("p (k n) -> p k n", n=P),
                   xp[:, p2, 0, 4 * r:4 * r + 4, :].bitcast(F32), ALU.subtract).then_inc(s_xgr, 1)

            dve.sem_inc(s_ye, 2)
            prepare_slots(0, 0, 0)
            slot_ids(0)
            slot_gates(0, 0)
            E1, E2 = (dve.value_load(tab[0:1, 0, q:q + 1], min_val=0, max_val=NE - 1) for q in (1, 2))
            T1, T2 = (dve.value_load(tab[0:1, 1, q:q + 1], min_val=0, max_val=TAB - 1) for q in (1, 2))
            prepare_slots(1, E1, T1)
            lo_gate_up(0, 2)
            slot_ids(1)
            slot_gates(1, 1)
            for r in range(2):
                lo_rows(0, 0, r)
            lo_gate_up(0, 3)
            prepare_slots(2, E2, T2)
            Gp, sq128, p2, p1 = m16(G), every(1500, NE), every(1520, NT), every(1530, NT)
            link(ts(sq128, sq_all, float(P), None, ALU.mult))
            link(tt(Gp, RK[:].rearrange("p e t -> p t e"), sq128.unsqueeze(1).to_broadcast([P, NT, NE]), ALU.add))
            link(tt(m16(R_["big"]), m16(M2), Gp, ALU.mult))
            link(dve.tensor_reduce(p2, m16(R_["big"]), AX.X, ALU.add))
            link(tt(Gp, m16(M1), Gp, ALU.mult))
            link(dve.tensor_reduce(p1, Gp, AX.X, ALU.add))
            link(tt(p1, p1, p2, ALU.subtract))
            link(dve.tensor_copy(pos[:, 0, :], p1))
            link(dve.tensor_copy(pos[:, 1, :], p2))
            W = dve.value_load(tab[0:1, 3, 0:1], min_val=NE, max_val=MAXT)
            with dve.Fori(0, MAXT // 2) as it:
                for par in range(2):
                    with dve.If(2 * it + par < W):
                        s = 2 * it + par
                        L = dve.value_load(tab[0:1, 2, bass.ds(s, 1)], min_val=0, max_val=1)
                        E1 = dve.value_load(tab[0:1, 0, bass.ds(s + 1, 1)], min_val=0, max_val=NE - 1)
                        with dve.If(L > 0):
                            lo_gate_up(E1, 0)
                        dve.wait_ge(s_sg, s + 1)
                        stt(out=sg[:], in0=sg[:], scalar=1.0, in1=bank[0][:], op0=ALU.add,
                            op1=ALU.mult).then_inc(s_sil2, 1)
                        dve.wait_ge(s_sil2, s + 1)
                        dve.wait_ge(s_gud, 4 * s + 4)
                        for h in range(2):
                            hs = slice(h * 2 * P, (h + 1) * 2 * P)
                            tt(sg[:, hs], bank[1][:, hs], sg[:, hs], ALU.mult).then_inc(s_hid, 1)
                        for h in range(2):
                            dve.wait_ge(s_hfr, 2 * s + h + 1)
                            tt(hp[:, 1, 2 * h:2 * h + 2, :],
                               bank[(7, 0)[h]][:, h * 2 * P:(h + 1) * 2 * P].rearrange("p (k n) -> p k n", n=P),
                               hp[:, 0, 2 * h:2 * h + 2, :].bitcast(F32), ALU.subtract).then_inc(s_hps, 1)
                        for r in range(2):
                            lo_rows(s + 1, 1 - par, r)
                        slot_ids(s + 2)
                        with dve.If(L > 0):
                            for j in range(1, KE):
                                lo_gate_up(E1, j)
                        dve.wait_ge(s_dd, 4 * s + 4)
                        dve.wait_ge(s_ys[par], 16 * it + 16)
                        for h in range(2):
                            hs = slice(h * HALF, (h + 1) * HALF)
                            stt(out=ysc[:, par, hs], in0=bank[4 + h][:], scalar=gcol[:, par, 0:1], in1=g5[:, hs],
                                op0=ALU.mult, op1=ALU.mult).then_inc(s_ye, 1)
                        dve.wait_ge(s_ye, 2 * s + 4)
                        slot_gates(s + 2, par)
                        E3 = dve.value_load(tab[0:1, 0, bass.ds(s + 3, 1)], min_val=0, max_val=NE - 1)
                        T3 = dve.value_load(tab[0:1, 1, bass.ds(s + 3, 1)], min_val=0, max_val=TAB - 1)
                        prepare_slots(s + 3, E3, T3)

            dve.wait_ge(s_gf, 16)

            def final_sum(t):
                if t in POOL_SUMS:
                    dve.wait_ge(s_fps, POOL_SUMS.index(t) + 1)
                else:
                    dve.wait_ge(s_fg[t], 32)
                    link(tt(fa[t][:], fa[t][:], fb[t][:], ALU.add))
                if t % 4 == 0:
                    dve.wait_ge(s_fl[t // 4], 16)
                tt(fx[:, t], fx[:, t], fa[t][:], ALU.add).then_inc(s_fx1, 1)

            def final_row(t):
                dve.wait_ge(s_fs, t + 1)
                ts(stat[:, 28 + t:29 + t], stat[:, 28 + t:29 + t], 1.0 / D, EPS, ALU.mult, ALU.add).then_inc(s_fm, 1)
                dve.wait_ge(s_fr, t + 1)
                link(dve.reciprocal(stat[:, 36 + t:37 + t], stat[:, 36 + t:37 + t]))
                stt(out=fb[t][:], in0=fx[:, t], scalar=stat[:, 36 + t:37 + t], in1=gfin[:], op0=ALU.mult,
                    op1=ALU.mult).then_inc(s_fo, 1)

            for t in range(NT):
                final_sum(t)
                if t >= 1:
                    final_row(t - 1)
            final_row(NT - 1)


_INS = ["x", "c", "ctx", "c_ctx", "mod_w", "mod_b", "norm_mix_g", "norm_ffn_g", "w_in", "conv_w", "conv_b",
        "rec_gate_a_w", "rec_gate_a_b", "rec_gate_x_w", "rec_gate_x_b", "rec_lambda", "pool_w", "pool_scale",
        "fourier_w", "w_out", "router_group_w", "router_group_b", "router_expert_w", "router_expert_b",
        "expert_w_gate", "expert_w_up", "expert_w_down", "final_norm_g"]


def kernel(**inputs):
    import concourse.bacc as bacc
    from concourse.bass_utils import run_bass_kernel_spmd

    nc = bacc.Bacc("TRN2", target_bir_lowering=False, num_devices=1)
    arrays, args = {}, []
    packed, dft = constants()
    for name in _INS + ["consts", "dft"]:
        a = {"consts": packed, "dft": dft}[name] if name in ("consts", "dft") else np.ascontiguousarray(inputs[name])
        arrays[f"in_{name}"] = a
        args.append(nc.dram_tensor(f"in_{name}", a.shape, mybir.dt.from_np(a.dtype), kind="ExternalInput").ap())
    args.append(nc.dram_tensor("result", (1, SEQ, D), F32, kind="ExternalOutput").ap())
    build(nc, *args)
    r = run_bass_kernel_spmd(nc, [arrays], core_ids=[0])
    return r.results[0]["result"]
```
